# Optimizing a Trainium2 kernel written in Bass

```python
import jax, jax.numpy as jnp
from jax import lax
import numpy as np
import math

D_MODEL = 1024
BATCH = 1
SEQ = 512
DEPTH = 1

CHUNK = 64
D_MIX = D_MODEL
HEAD_DIM = 64
N_HEADS_A = 8
N_HEADS_B = 8
D_A = N_HEADS_A * HEAD_DIM
D_B = N_HEADS_B * HEAD_DIM
SG_BLOCK = 128
Q_BLOCK = 128
D_FF = 2816
CONV_W = 3
EPS = 1e-6
D_IN = 2 * D_A + 3 * D_B + N_HEADS_B


def rms_norm(x, g):
    xf = x.astype(jnp.float32)
    y = xf * lax.rsqrt(jnp.mean(xf * xf, axis=-1, keepdims=True) + EPS)
    return (y * g.astype(jnp.float32)).astype(x.dtype)

def spatial_gating(u, v, ln_g, w_s, b_s):
    B, S, _ = u.shape
    n = S // SG_BLOCK
    v = v.reshape(B, n, SG_BLOCK, N_HEADS_A, HEAD_DIM)
    vf = v.astype(jnp.float32)
    mu = jnp.mean(vf, axis=-1, keepdims=True)
    var = jnp.mean(jnp.square(vf - mu), axis=-1, keepdims=True)
    vn = ((vf - mu) * lax.rsqrt(var + EPS) * ln_g.astype(jnp.float32)).astype(u.dtype)
    pos_chunk = jnp.arange(SG_BLOCK) // CHUNK
    mask = pos_chunk[:, None] >= pos_chunk[None, :]
    w = jnp.where(mask[None], w_s, 0).astype(u.dtype)
    mixed = jnp.einsum('hts,bnshd->bnthd', w, vn) + b_s.T.astype(u.dtype)[None, None, :, :, None]
    out = u.reshape(B, n, SG_BLOCK, N_HEADS_A, HEAD_DIM) * mixed
    return out.reshape(B, S, D_A)

def forgetting_attention(q, k, v, f_logit):
    B, S, H, Dh = q.shape
    n = S // Q_BLOCK
    scale = Dh ** -0.5
    c = jnp.cumsum(jax.nn.log_sigmoid(f_logit.astype(jnp.float32)), axis=1)
    c = c.transpose(0, 2, 1)
    qb = q.reshape(B, n, Q_BLOCK, H, Dh).transpose(1, 0, 3, 2, 4)
    cb = c.reshape(B, H, n, Q_BLOCK).transpose(2, 0, 1, 3)
    kpos = jnp.arange(S)

    def block(args):
        i, qi, ci = args
        s = jnp.einsum('bhtd,bshd->bhts', qi, k, preferred_element_type=jnp.float32) * scale
        s = s + ci[..., :, None] - c[:, :, None, :]
        qpos = i * Q_BLOCK + jnp.arange(Q_BLOCK)
        s = jnp.where(kpos[None, :] <= qpos[:, None], s, -jnp.inf)
        p = jax.nn.softmax(s, axis=-1)
        return jnp.einsum('bhts,bshd->bthd', p.astype(v.dtype), v)

    out = lax.map(block, (jnp.arange(n), qb, cb))
    return out.transpose(1, 0, 2, 3, 4).reshape(B, S, H * Dh)

def conv_ffn(h, w_up, w_conv, b_conv, w_down):
    a = h @ w_up
    C = a.shape[-1]
    a = lax.conv_general_dilated(
        a, w_conv[:, None, :].astype(a.dtype), window_strides=(1,),
        padding=[(CONV_W - 1, 0)], dimension_numbers=('NWC', 'WIO', 'NWC'),
        feature_group_count=C) + b_conv.astype(a.dtype)
    g, val = jnp.split(a, 2, axis=-1)
    return (jax.nn.silu(g) * val) @ w_down

def first_inputs(seed: int = 0) -> dict:
    key = jax.random.key(seed)
    ks = jax.random.split(key, 14)
    L = DEPTH
    nrm = jax.random.normal
    return {
        "x": nrm(ks[0], (BATCH, SEQ, D_MODEL), jnp.float32),
        "norm_mix_g": 1.0 + 0.02 * nrm(ks[1], (L, D_MODEL), jnp.float32),
        "w_in": nrm(ks[2], (L, D_MODEL, D_IN), jnp.float32) * D_MODEL ** -0.5,
        "f_bias": 3.0 + 0.5 * nrm(ks[3], (L, N_HEADS_B), jnp.float32),
        "sg_ln_g": 1.0 + 0.02 * nrm(ks[4], (L, N_HEADS_A, HEAD_DIM), jnp.float32),
        "sg_w": nrm(ks[5], (L, N_HEADS_A, SG_BLOCK, SG_BLOCK), jnp.float32) * SG_BLOCK ** -0.5,
        "sg_b": 1.0 + 0.1 * nrm(ks[6], (L, N_HEADS_A, SG_BLOCK), jnp.float32),
        "w_out": nrm(ks[7], (L, D_MIX, D_MODEL), jnp.float32) * D_MIX ** -0.5,
        "norm_ffn_g": 1.0 + 0.02 * nrm(ks[8], (L, D_MODEL), jnp.float32),
        "w_up": nrm(ks[9], (L, D_MODEL, 2 * D_FF), jnp.float32) * D_MODEL ** -0.5,
        "w_conv": nrm(ks[10], (L, CONV_W, 2 * D_FF), jnp.float32) * CONV_W ** -0.5,
        "b_conv": 0.02 * nrm(ks[11], (L, 2 * D_FF), jnp.float32),
        "w_down": nrm(ks[12], (L, D_FF, D_MODEL), jnp.float32) * D_FF ** -0.5,
        "norm_final_g": 1.0 + 0.02 * nrm(ks[13], (D_MODEL,), jnp.float32),
    }

def first_block(x, norm_mix_g, w_in, f_bias, sg_ln_g, sg_w, sg_b, w_out,
              norm_ffn_g, w_up, w_conv, b_conv, w_down, norm_final_g):
    B, S, _ = x.shape
    for l in range(DEPTH):
        h = rms_norm(x, norm_mix_g[l])
        z = h @ w_in[l]
        o = 0
        u_a = jax.nn.gelu(z[..., o:o + D_A], approximate=False); o += D_A
        v_a = jax.nn.gelu(z[..., o:o + D_A], approximate=False); o += D_A
        q_b = z[..., o:o + D_B].reshape(B, S, N_HEADS_B, HEAD_DIM); o += D_B
        k_b = z[..., o:o + D_B].reshape(B, S, N_HEADS_B, HEAD_DIM); o += D_B
        v_b = z[..., o:o + D_B].reshape(B, S, N_HEADS_B, HEAD_DIM); o += D_B
        f_logit = z[..., o:o + N_HEADS_B] + f_bias[l].astype(z.dtype)
        out_a = spatial_gating(u_a, v_a, sg_ln_g[l], sg_w[l], sg_b[l])
        out_b = forgetting_attention(q_b, k_b, v_b, f_logit)
        x = x + jnp.concatenate([out_a, out_b], axis=-1) @ w_out[l]
        x = x + conv_ffn(rms_norm(x, norm_ffn_g[l]), w_up[l], w_conv[l], b_conv[l], w_down[l])
    return rms_norm(x, norm_final_g)


D_MIX_2 = D_MODEL
DN_WIDTH = D_MIX_2 // 2
DN_HEAD_K = 128
DN_HEAD_V = 128
DN_HEADS = DN_WIDTH // DN_HEAD_V
CONV_WIDTH = 4
DF_WIDTH = D_MIX_2 - DN_WIDTH
DF_HEAD_QK = 64
DF_HEAD_V = 2 * DF_HEAD_QK
DF_HEADS = DF_WIDTH // DF_HEAD_V

DN_QK = DN_HEADS * DN_HEAD_K
DN_V = DN_HEADS * DN_HEAD_V
DF_QK = DF_HEADS * 2 * DF_HEAD_QK
DF_V = DF_HEADS * DF_HEAD_V
COL_SIZES = (DN_QK, DN_QK, DN_V, DN_V, DN_HEADS, DN_HEADS, DF_QK, DF_QK, DF_V, DF_V)
IN_COLS = sum(COL_SIZES)
COL_OFFSETS = tuple(int(o) for o in np.cumsum(COL_SIZES)[:-1])


def rmsnorm(x, gain):
    xf = x.astype(jnp.float32)
    y = xf * lax.rsqrt(jnp.mean(xf * xf, axis=-1, keepdims=True) + EPS)
    return (y * gain.astype(jnp.float32)).astype(x.dtype)

def l2norm(x):
    return x * lax.rsqrt(jnp.sum(x * x, axis=-1, keepdims=True) + EPS)

def causal_depthwise_conv(x, w):
    c = x.shape[-1]
    return lax.conv_general_dilated(
        x, w[:, None, :].astype(x.dtype), window_strides=(1,),
        padding=[(CONV_WIDTH - 1, 0)], dimension_numbers=("NWC", "WIO", "NWC"),
        feature_group_count=c)

def gated_delta_rule(q, k, v, g, beta):
    b, t, h, dk = q.shape
    dv = v.shape[-1]
    n = t // CHUNK

    def chunks(a):
        a = jnp.moveaxis(a, 2, 1)
        return a.reshape((b, h, n, CHUNK) + a.shape[3:])

    qc, kc, vc = chunks(q), chunks(k), chunks(v)
    gc = jnp.cumsum(chunks(g), axis=-1)
    bc = chunks(beta)
    k_beta = kc * bc[..., None]
    v_beta = vc * bc[..., None]

    tril = jnp.tril(jnp.ones((CHUNK, CHUNK), bool))
    strict = jnp.tril(jnp.ones((CHUNK, CHUNK), bool), -1)
    diff = gc[..., :, None] - gc[..., None, :]
    decay = jnp.exp(jnp.where(tril, diff, -jnp.inf))

    m = jnp.where(strict, jnp.einsum('bhncd,bhnsd->bhncs', k_beta, kc) * decay, 0.0)
    lmat = m + jnp.eye(CHUNK, dtype=m.dtype)
    rhs = jnp.concatenate([v_beta, k_beta * jnp.exp(gc)[..., None]], axis=-1)
    sol = lax.linalg.triangular_solve(lmat, rhs, left_side=True, lower=True,
                                      unit_diagonal=True)
    u, w = sol[..., :dv], sol[..., dv:]
    a_qk = jnp.einsum('bhncd,bhnsd->bhncs', qc, kc) * decay

    def step(state, inp):
        q_i, k_i, u_i, w_i, g_i, a_i = inp
        v_new = u_i - jnp.einsum('bhcd,bhdv->bhcv', w_i, state)
        o_i = (jnp.einsum('bhcd,bhdv->bhcv', q_i * jnp.exp(g_i)[..., None], state)
               + jnp.einsum('bhcs,bhsv->bhcv', a_i, v_new))
        g_last = g_i[..., -1]
        k_dec = k_i * jnp.exp(g_last[..., None] - g_i)[..., None]
        state = (state * jnp.exp(g_last)[..., None, None]
                 + jnp.einsum('bhcd,bhcv->bhdv', k_dec, v_new))
        return state, o_i

    xs = tuple(jnp.moveaxis(a, 2, 0) for a in (qc, kc, u, w, gc, a_qk))
    s0 = jnp.zeros((b, h, dk, dv), jnp.float32)
    _, o = lax.scan(step, s0, xs)
    o = jnp.transpose(o, (1, 0, 3, 2, 4))
    return o.reshape(b, t, h, dv)

def gated_deltanet_group(q, k, v, z, bb, aa, conv_w, a_log, dt_bias, out_gain):
    b, t, _ = q.shape
    qkv = jax.nn.silu(causal_depthwise_conv(jnp.concatenate([q, k, v], -1), conv_w))
    q, k, v = jnp.split(qkv, [DN_QK, 2 * DN_QK], axis=-1)
    q = l2norm(q.reshape(b, t, DN_HEADS, DN_HEAD_K).astype(jnp.float32)) * (DN_HEAD_K ** -0.5)
    k = l2norm(k.reshape(b, t, DN_HEADS, DN_HEAD_K).astype(jnp.float32))
    v = v.reshape(b, t, DN_HEADS, DN_HEAD_V).astype(jnp.float32)
    beta = jax.nn.sigmoid(bb.astype(jnp.float32))
    g = -jnp.exp(a_log.astype(jnp.float32)) * jax.nn.softplus(
        aa.astype(jnp.float32) + dt_bias.astype(jnp.float32))
    o = gated_delta_rule(q, k, v, g, beta)
    zf = z.reshape(b, t, DN_HEADS, DN_HEAD_V).astype(jnp.float32)
    o = rmsnorm(o, out_gain) * jax.nn.silu(zf)
    return o.reshape(b, t, DN_V).astype(z.dtype)

def diff_attention_group(q, k, v, z, q_gain, k_gain, lq1, lk1, lq2, lk2, out_gain, lambda_init):
    b, t, _ = q.shape
    q = rmsnorm(q.reshape(b, t, DF_HEADS, 2, DF_HEAD_QK), q_gain) * (DF_HEAD_QK ** -0.5)
    k = rmsnorm(k.reshape(b, t, DF_HEADS, 2, DF_HEAD_QK), k_gain)
    v = v.reshape(b, t, DF_HEADS, DF_HEAD_V)
    lam = (jnp.exp(jnp.sum(lq1.astype(jnp.float32) * lk1.astype(jnp.float32)))
           - jnp.exp(jnp.sum(lq2.astype(jnp.float32) * lk2.astype(jnp.float32)))
           + lambda_init)
    nb = t // Q_BLOCK
    qb = jnp.moveaxis(q.reshape(b, nb, Q_BLOCK, DF_HEADS, 2, DF_HEAD_QK), 1, 0)
    starts = jnp.arange(nb, dtype=jnp.int32) * Q_BLOCK
    key_pos = jnp.arange(t, dtype=jnp.int32)
    neg = jnp.finfo(jnp.float32).min

    def block(args):
        q_blk, start = args
        s = jnp.einsum('bqhcd,bkhcd->bhcqk', q_blk, k).astype(jnp.float32)
        q_pos = start + jnp.arange(Q_BLOCK, dtype=jnp.int32)
        mask = key_pos[None, :] <= q_pos[:, None]
        p = jax.nn.softmax(jnp.where(mask, s, neg), axis=-1)
        wts = p[:, :, 0] - lam * p[:, :, 1]
        return jnp.einsum('bhqk,bkhv->bqhv', wts.astype(v.dtype), v)

    o = lax.map(block, (qb, starts))
    o = jnp.moveaxis(o, 0, 1).reshape(b, t, DF_HEADS, DF_HEAD_V)
    o = rmsnorm(o, out_gain).astype(jnp.float32) * (1.0 - lambda_init)
    zf = z.reshape(b, t, DF_HEADS, DF_HEAD_V).astype(jnp.float32)
    o = o * jax.nn.silu(zf)
    return o.reshape(b, t, DF_V).astype(z.dtype)

def second_inputs(seed: int = 0) -> dict:
    key = jax.random.key(seed)
    ks = jax.random.split(key, 16)
    f32 = jnp.float32
    x = jax.random.normal(ks[0], (BATCH, SEQ, D_MODEL), f32)
    norm_gain = 1.0 + 0.05 * jax.random.normal(ks[1], (DEPTH, D_MODEL), f32)
    w_in = jax.random.normal(ks[2], (DEPTH, D_MODEL, IN_COLS), f32) * D_MODEL ** -0.5
    conv_w = jax.random.normal(ks[3], (DEPTH, CONV_WIDTH, DN_QK * 2 + DN_V), f32) * CONV_WIDTH ** -0.5
    a_log = jnp.log(jax.random.uniform(ks[4], (DEPTH, DN_HEADS), f32, 1.0, 16.0))
    dt = jnp.exp(jax.random.uniform(ks[5], (DEPTH, DN_HEADS), f32,
                                    math.log(1e-3), math.log(1e-1)))
    dt_bias = dt + jnp.log(-jnp.expm1(-dt))
    dn_out_gain = 1.0 + 0.05 * jax.random.normal(ks[6], (DEPTH, DN_HEAD_V), f32)
    q_gain = 1.0 + 0.05 * jax.random.normal(ks[7], (DEPTH, DF_HEAD_QK), f32)
    k_gain = 1.0 + 0.05 * jax.random.normal(ks[8], (DEPTH, DF_HEAD_QK), f32)
    lambda_q1 = 0.1 * jax.random.normal(ks[9], (DEPTH, DF_HEAD_QK), f32)
    lambda_k1 = 0.1 * jax.random.normal(ks[10], (DEPTH, DF_HEAD_QK), f32)
    lambda_q2 = 0.1 * jax.random.normal(ks[11], (DEPTH, DF_HEAD_QK), f32)
    lambda_k2 = 0.1 * jax.random.normal(ks[12], (DEPTH, DF_HEAD_QK), f32)
    df_out_gain = 1.0 + 0.05 * jax.random.normal(ks[13], (DEPTH, DF_HEAD_V), f32)
    w_out = jax.random.normal(ks[14], (DEPTH, D_MIX_2, D_MODEL), f32) * D_MIX_2 ** -0.5
    return {"x": x, "norm_gain": norm_gain, "w_in": w_in, "conv_w": conv_w,
            "a_log": a_log, "dt_bias": dt_bias, "dn_out_gain": dn_out_gain,
            "q_gain": q_gain, "k_gain": k_gain, "lambda_q1": lambda_q1,
            "lambda_k1": lambda_k1, "lambda_q2": lambda_q2, "lambda_k2": lambda_k2,
            "df_out_gain": df_out_gain, "w_out": w_out}

def second_block(x, norm_gain, w_in, conv_w, a_log, dt_bias, dn_out_gain, q_gain, k_gain,
              lambda_q1, lambda_k1, lambda_q2, lambda_k2, df_out_gain, w_out):
    for l in range(DEPTH):
        lambda_init = 0.8 - 0.6 * math.exp(-0.3 * l)
        h = rmsnorm(x, norm_gain[l])
        proj = jnp.einsum('btd,dc->btc', h, w_in[l])
        (dn_q, dn_k, dn_v, dn_z, dn_b, dn_a,
         df_q, df_k, df_v, df_z) = jnp.split(proj, COL_OFFSETS, axis=-1)
        o_dn = gated_deltanet_group(dn_q, dn_k, dn_v, dn_z, dn_b, dn_a, conv_w[l],
                                    a_log[l], dt_bias[l], dn_out_gain[l])
        o_df = diff_attention_group(df_q, df_k, df_v, df_z, q_gain[l], k_gain[l],
                                    lambda_q1[l], lambda_k1[l], lambda_q2[l], lambda_k2[l],
                                    df_out_gain[l], lambda_init)
        mixed = jnp.concatenate([o_dn, o_df], axis=-1)
        x = x + jnp.einsum('btc,cd->btd', mixed, w_out[l])
    return x


def setup_inputs(seed=0):
    out = dict(first_inputs(seed))
    for name, value in second_inputs(seed + 1).items():
        if name != "x":
            out[name + "_2"] = value
    return out


def reference(
    x, norm_mix_g, w_in, f_bias, sg_ln_g, sg_w, sg_b, w_out, norm_ffn_g, w_up, w_conv, b_conv,
    w_down, norm_final_g, norm_gain_2, w_in_2, conv_w_2, a_log_2, dt_bias_2, dn_out_gain_2,
    q_gain_2, k_gain_2, lambda_q1_2, lambda_k1_2, lambda_q2_2, lambda_k2_2, df_out_gain_2,
    w_out_2,
):
    x = first_block(
        x, norm_mix_g, w_in, f_bias, sg_ln_g, sg_w, sg_b, w_out, norm_ffn_g, w_up, w_conv,
        b_conv, w_down, norm_final_g,
    )
    return second_block(
        x, norm_gain_2, w_in_2, conv_w_2, a_log_2, dt_bias_2, dn_out_gain_2, q_gain_2, k_gain_2,
        lambda_q1_2, lambda_k1_2, lambda_q2_2, lambda_k2_2, df_out_gain_2, w_out_2,
    )


_drawn_inputs = setup_inputs


def setup_inputs(seed=0):
    import zlib

    import numpy as np

    out = dict(_drawn_inputs(seed))
    spreads = {}
    factors = {'norm_mix_g': 2.924,
     'sg_ln_g': 7.09,
     'norm_ffn_g': 4.031,
     'b_conv': 3.631,
     'dn_out_gain_2': 2.917,
     'q_gain_2': 7.882,
     'k_gain_2': 7.853,
     'lambda_q1_2': 6.177,
     'lambda_k1_2': 8.0,
     'df_out_gain_2': 3.71}
    for name, (base, spread) in spreads.items():
        noise = np.random.default_rng([zlib.crc32(name.encode()), seed]).standard_normal(out[name].shape)
        drawn = base * np.exp(spread * noise) if base else spread * noise
        out[name] = __import__('jax').numpy.asarray(drawn.astype(out[name].dtype))
    for name, factor in factors.items():
        out[name] = (out[name] * factor).astype(out[name].dtype)
    return out
```

```python
from contextlib import ExitStack

import numpy as np

import concourse.bass as bass
from concourse import mybir

F32 = mybir.dt.float32
F32R = mybir.dt.float32r
ALU = mybir.AluOpType
ACT = mybir.ActivationFunctionType
AX_X = mybir.AxisListType.X

P = 128
T = 512
D = 1024
KC = D // P
NB = T // P
HD = 64
CH = 64
FF = 2816
NFF = FF // P
EPS = 1e-6
NEG = -1e30
LEVELS = 6
LAMBDA_INIT = 0.2

U_VB = 0
U_VA = 4
U_F = 8
U_QK = 9
U_UA = 17
U_WO = 21
U_UP = 29
U_DN = U_UP + 2 * NFF
U_BA = U_DN + NFF
U_KQV = U_BA + 1
U_DFV = U_KQV + 12
U_DFQK = U_DFV + 4
U_Z = U_DFQK + 8
U_WO2 = U_Z + 8
UNITS = U_WO2 + 8
RING = 4

G_F = 0
G_QK = 1
G_UA = 9
G_WO = 13
G_UP = 21
G_DN = G_UP + 2 * NFF
G_BA = G_DN + KC
G_KQV = G_BA + 1
G_DFQK = G_KQV + 12
G_Z = G_DFQK + 8
G_WO2 = G_Z + 8

_at = 0


def _cols(n):
    global _at
    _at += n
    return _at - n


C_GMIX, C_GFFN, C_GFIN, C_GN2 = (_cols(KC) for _ in range(4))
C_SGG = _cols(4)
C_FCW = _cols(2 * NFF * 3)
C_FCB = _cols(2 * NFF)
C_DCW = _cols(12 * 4)
C_FB, C_ALOG, C_DTB, C_DNG, C_QG, C_KG, C_DFG = (_cols(1) for _ in range(7))
C_LAM = _cols(4)
NPAR = _at

K_ID, K_ONE, K_HALF, K_CAUSAL, K_GNEG, K_LV = 0, 128, 256, 384, 896, 1024
NCON = K_LV + 128 * LEVELS

MIX1_ORDER = [
    ("qk", 0), ("qk", 1), ("A", 0), ("qk", 2), ("qk", 3),
    ("A", 1), ("qk", 4), ("B", 0), ("qk", 5), ("C", 0),
    ("A", 2), ("qk", 6), ("B", 1), ("qk", 7), ("C", 1),
    ("A", 3), ("u", 0), ("B", 2), ("u", 1), ("C", 2),
    ("A", 4), ("u", 2), ("B", 3), ("u", 3), ("C", 3), ("gelu", 0),
    ("A", 5), ("gate", 0), ("B", 4), ("gate", 1), ("C", 4),
    ("A", 6), ("gate", 2), ("B", 5), ("gate", 3), ("C", 5),
    ("A", 7), ("B", 6), ("C", 6), ("B", 7), ("C", 7),
]


def _level(b, l):
    return [(what, (x, l)) for what in ("Y", "Z", "X") if l or what != "Z" for x in (b, b + 1)]


def _prepare(b):
    unit = [("dfqk", 2 * b + n) for n in range(4)]
    return ([("T", b), ("T", b + 1), unit[0]] + _level(b, 0) + _level(b, 1) + [unit[1]] + _level(b, 2)
            + [unit[2]] + _level(b, 3) + [unit[3]] + _level(b, 4) + _level(b, 5) + [("W", b), ("W", b + 1)])


def step(b, l):
    return (b // 2) * 2 * LEVELS + 2 * l + b % 2


MIX2_ORDER = (
    [("lam", 0), ("ba", 0)] + [("kqv", t) for t in range(12)] + [("cols", 0), ("dfv", 0)]
    + [("l2", t) for t in range(8)] + _prepare(0) + _prepare(2)
    + [("A", 0), ("scan", 0), ("scan", 1), ("A", 1), ("scan", 2), ("B", 0), ("scan", 3), ("C", 0),
       ("A", 2), ("scan", 4), ("B", 1), ("scan", 5), ("C", 1), ("scan", 6),
       ("A", 3), ("scan", 7), ("B", 2), ("z", 0), ("C", 2), ("z", 1), ("B", 3), ("z", 2), ("C", 3),
       ("z", 3), ("z", 4), ("z", 5), ("z", 6), ("z", 7), ("silu", 0)]
    + [("out", t) for t in range(8)]
)
PCOL = [P * i * (i + 1) // 2 for i in range(NB)]
PALL = P * NB * (NB + 1) // 2


def build(nc, x_t, wstream, params, consts, sgw_t, sgb, out_t):
    with ExitStack() as ctx:
        here = [16512]

        def place(name, shape, dt, at=None):
            size = 4 * int(np.prod(shape[1:]))
            if at is None:
                at = here[0]
                here[0] += (size + 31) // 32 * 32
            return nc.alloc_sbuf_tensor_at(name, shape, dt, offset=at)

        def sem(name):
            return ctx.enter_context(nc.semaphore(name))

        X = place("X", [P, KC, T], F32)
        GH = place("GH", [P, KC, T], F32R)
        GL = place("GL", [P, KC, T], F32R)
        RAW = place("RAW", [P, RING, 1024], F32)
        HI = place("HI", [P, RING, 1024], F32R)
        LO = place("LO", [P, RING, 1024], F32R)
        CON = place("CON", [P, NCON], F32)
        PAR = place("PAR", [P, NPAR], F32)
        RB = place("RB", [P, T], F32)
        SM = place("SM", [P, 320], F32)
        arena = here[0]
        KB = 1024

        MT = place("MT", [P, 8, T], F32, arena)
        KT1 = place("KT1", [P, 4, T], F32, arena + 16 * KB)
        VA = place("VA", [P, NB, 512], F32, arena + 24 * KB)
        VB = place("VB", [P, NB, 512], F32, arena + 32 * KB)
        P1 = place("P1", [P, 2, PALL], F32, arena + 40 * KB)
        PT1 = place("PT1", [P, NB, T], F32, arena + 50 * KB)
        NCB = place("NCB", [P, 2, T], F32, arena + 58 * KB)
        NCD = place("NCD", [P, 2, T], F32, arena + 62 * KB)
        SGW = place("SGW", [P, 8, P], F32, arena + 66 * KB)
        SGB = place("SGB", [P, 4, P], F32, arena + 70 * KB)
        FR = place("FR", [P, 3, T], F32, arena + 72 * KB)
        SQV = place("SQV", [P, NB, 512], F32, arena + 78 * KB)
        AH = place("AH", [P, NFF, T], F32R, arena)
        AL = place("AL", [P, NFF, T], F32R, arena + 44 * KB)
        AB = place("AB", [P, 2, T + 2], F32, arena + 88 * KB)
        YC = place("YC", [P, 2, T], F32, arena + 88 * KB + 4128)
        SQ = place("SQ", [P, 2, T], F32, arena + 96 * KB + 96)
        ACC = SQ[:, 1, :]
        assert arena + 100 * KB + 96 <= 229368, arena
        KT = place("KT", [P, 4, T], F32, arena)
        QT = place("QT", [P, 4, T], F32, arena + 8 * KB)
        VT = place("VT", [P, 4, T], F32, arena + 16 * KB)
        EG = place("EG", [P, 4, T], F32, arena + 24 * KB)
        AQK = place("AQK", [P, NB, 4, P], F32, arena + 32 * KB)
        KDEC = place("KDEC", [P, NB, 4, P], F32, arena + 40 * KB)
        TR = arena + 48 * KB
        NT = place("NT", [P, 2, 4, P], F32, TR)
        XI = place("XI", [P, 2, 4, P], F32, TR + 4 * KB)
        XT = place("XT", [P, 2, 4, P], F32, TR + 8 * KB)
        YM = place("YM", [P, 2, 4, P], F32, TR + 12 * KB)
        KBE = place("KBE", [P, 2, 4, P], F32, TR + 16 * KB)
        VBT = place("VBT", [P, 2, 4, P], F32, TR + 20 * KB)
        CB = place("CB", [P, 2, T + 4], F32, TR)
        R1 = place("R1", [P, T], F32, TR + 5 * KB)
        R2 = place("R2", [P, T], F32, TR + 7 * KB)
        R3 = place("R3", [P, T], F32, TR + 9 * KB)
        BR = place("BR", [P, T], F32, TR + 11 * KB)
        SQ2 = place("SQ2", [P, 2, T], F32, TR + 13 * KB)
        NR2 = place("NR2", [P, 2, T], F32, TR + 17 * KB)
        P0 = place("P0", [P, 2, PALL], F32, TR)
        PB = place("PB", [P, PALL], F32, TR + 10 * KB)
        PT2 = place("PT2", [P, NB, T], F32, TR + 15 * KB)
        DQ = place("DQ", [P, 4, T], F32, arena + 72 * KB)
        DK = place("DK", [P, 4, T], F32, arena + 80 * KB)
        DV = place("DV", [P, NB, 512], F32, arena + 88 * KB)
        RS = place("RS", [P, T], F32, arena + 96 * KB)
        SQD = place("SQD", [P, T], F32, arena + 96 * KB)
        NRD = place("NRD", [P, T], F32, arena + 98 * KB)
        ZT = place("ZT", [P, 8, T], F32, arena + 32 * KB)
        ST = place("ST", [P, 4, P], F32, arena + 96 * KB)
        SQO = place("SQO", [P, 8, T], F32, TR)
        NRO = place("NRO", [P, 8, T], F32, arena + 80 * KB)

        PS = [ctx.enter_context(nc.psum_tensor(f"bank{b}", [P, 512], F32)) for b in range(8)]

        EPSC = SM[:, 0:4]
        RCOL = SM[:, 4:8]
        MX = SM[:, 8:24].rearrange("p (a b) -> p a b", a=2)
        SU = SM[:, 24:40].rearrange("p (a b) -> p a b", a=2)
        RC = SM[:, 40:56].rearrange("p (a b) -> p a b", a=2)
        LP, LE, NEGLAM = SM[:, 56:58], SM[:, 58:60], SM[:, 60:61]
        EA = SM[:, 61:62]
        S1 = SM[:, 62:64]
        LNS, LNV = SM[:, 64:96], SM[:, 96:128]
        COLS = SM[:, 128:192].rearrange("p (b q h) -> p b q h", b=NB, q=4)
        MXA = SM[:, 192:200]

        IDENT, ONES, HALF = (CON[:, c:c + P] for c in (K_ID, K_ONE, K_HALF))
        CAUSAL = CON[:, K_CAUSAL:K_CAUSAL + 512]
        GNEG = CON[:, K_GNEG:K_GNEG + P]

        def level_mask(l):
            return CON[:, K_LV + P * l:K_LV + P * (l + 1)]

        def par(c, n=1, p0=0, p1=P):
            return PAR[p0:p1, c:c + n]

        def heads(ap):
            return ap.rearrange("p (h c) -> p h c", h=4)

        x_landed = [sem(f"x_landed{k}") for k in range(KC)]
        par_landed, con_landed = sem("par_landed"), sem("con_landed")
        sg_landed = sem("sg_landed")
        w_landed = [sem("w_landed0"), sem("w_landed1")]
        hi_made, unit_split, unit_done = sem("hi_made"), sem("unit_split"), sem("unit_done")
        stored = sem("stored")
        sq_made, sq_added, ss_made = sem("sq_made"), sem("sq_added"), sem("ss_made")
        rms_made, rb_ready = sem("rms_made"), sem("rb_ready")
        gh_made, gl_made, x_updated = sem("gh_made"), sem("gl_made"), sem("x_updated")
        gemm_freed = sem("gemm_freed")
        rcol_mm, rcol_made = sem("rcol_mm"), sem("rcol_made")
        v_chain, a_chain = sem("v_chain"), sem("a_chain")
        eps_made = sem("eps_made")
        vb_freed, va_freed = sem("vb_freed"), sem("va_freed")
        ln_centered, ln_squared, ln_summed, ln_root, vn_ready = (
            sem(n) for n in ("ln_centered", "ln_squared", "ln_summed", "ln_root", "vn_ready"))
        sgw_masked = sem("sgw_masked")
        f_made, f_log, negc_ready = sem("f_made"), sem("f_log"), sem("negc_ready")
        gelu_made = sem("gelu_made")
        ncb_mm, ncb_made = sem("ncb_mm"), sem("ncb_made")
        s_made, max_made, exp_made, p_ready = (sem(n) for n in ("s_made", "max_made", "exp_made", "p_ready"))
        pt_mm, pt_freed, pv_made, attended = (sem(n) for n in ("pt_mm", "pt_freed", "pv_made", "attended"))
        gate_mm, gated = sem("gate_mm"), sem("gated")
        conv_started, conv_made = sem("conv_started"), sem("conv_made")
        silu_ff, ff_made, ah_made, al_made = (sem(n) for n in ("silu_ff", "ff_made", "ah_made", "al_made"))
        down_done = sem("down_done")
        lam_prod, lam_mm, lam_exp, lam_made = (sem(n) for n in ("lam_prod", "lam_mm", "lam_exp", "lam_made"))
        ba_v, ba_a, rows_ready = sem("ba_v"), sem("ba_a"), sem("rows_ready")
        cb_zero = sem("cb_zero")
        cv_a, cv_v, cv_s = sem("cv_a"), sem("cv_v"), sem("cv_s")
        cols_mm, cols_made, gcb_mm, gcb_made = (sem(n) for n in ("cols_mm", "cols_made", "gcb_mm", "gcb_made"))
        dfv_freed = sem("dfv_freed")
        l2_sq, l2_mm, l2_rt, l2_made = (sem(n) for n in ("l2_sq", "l2_mm", "l2_rt", "l2_made"))
        qn_sq, qn_mm, qn_rt, qn_made = (sem(n) for n in ("qn_sq", "qn_mm", "qn_rt", "qn_made"))
        tk_mm, tv_mm, g_mm, aq_mm = (sem(n) for n in ("tk_mm", "tv_mm", "g_mm", "aq_mm"))
        d_made, d_exp, eg_made, kd_made, vbt_made, nt_made, qe_made = (
            sem(n) for n in ("d_made", "d_exp", "eg_made", "kd_made", "vbt_made", "nt_made", "qe_made"))
        y_mm, ym_made, z_mm, xi_made, xt_mm, xt_made = (
            sem(n) for n in ("y_mm", "ym_made", "z_mm", "xi_made", "xt_mm", "xt_made"))
        u_mm, w_mm, uw_made = sem("u_mm"), sem("w_mm"), sem("uw_made")
        st_made, ws_mm, vn_made, ot_mm, kv_mm, od_made = (
            sem(n) for n in ("st_made", "ws_mm", "vn_made", "ot_mm", "kv_mm", "od_made"))
        ds_mm, dmax, dexp, dw_made = (sem(n) for n in ("ds_mm", "dmax", "dexp", "dw_made"))
        dpt_mm, dpt_freed, dpv_mm, dpv_freed = (sem(n) for n in ("dpt_mm", "dpt_freed", "dpv_mm", "dpv_freed"))
        silu_z = sem("silu_z")
        o_sq, o_mm, o_rt, o_made = (sem(n) for n in ("o_sq", "o_mm", "o_rt", "o_made"))

        def bank_of(g):
            return PS[g % 2]

        block = ctx.enter_context(nc.Block())

        @block.sync
        def _(sp):
            for k in range(KC):
                sp.dma_start(X[:, k, :], x_t[P * k:P * (k + 1), :]).then_inc(x_landed[k], 16)

            def load(pair, slot):
                sp.dma_start(RAW[:, 2 * slot:2 * slot + 2, :],
                             wstream[pair].rearrange("p (a n) -> p a n", a=2)).then_inc(w_landed[slot], 16)

            load(0, 0)
            load(1, 1)
            with sp.Fori(1, UNITS // 4) as i:
                for s in range(2):
                    sp.wait_ge(unit_split, 4 * i + (2 * s - 2))
                    sp.dma_start(RAW[:, 2 * s:2 * s + 2, :],
                                 wstream[bass.ds(2 * i + s, 1)].rearrange("o p (a n) -> p (o a) n", a=2))\
                      .then_inc(w_landed[s], 16)
            for m in range(KC):
                sp.wait_ge(gemm_freed, G_WO2 + m + 1)
                sp.dma_start(out_t[P * m:P * (m + 1), :], X[:, m, :]).then_inc(stored, 16)
            sp.wait_ge(stored, 16 * KC)

        @block.gpsimd
        def _(pool):
            def split(slot, done, unit):
                pool.wait_ge(w_landed[slot // 2], done)
                pool.tensor_tensor(HI[:, slot, :].rearrange("p (a n) -> p a n", n=P),
                                   RAW[:, slot, :].rearrange("p (a n) -> p a n", n=P),
                                   ONES.unsqueeze(1).to_broadcast([P, KC, P]), ALU.mult).then_inc(hi_made, 1)
                pool.wait_ge(hi_made, unit + 1)
                pool.tensor_tensor(LO[:, slot, :], RAW[:, slot, :], HI[:, slot, :].bitcast(F32),
                                   ALU.subtract).then_inc(unit_split, 1)

            pool.wait_ge(con_landed, 16)
            for s in range(RING):
                split(s, 16, s)
            with pool.Fori(1, UNITS // 4) as i:
                for s in range(RING):
                    pool.wait_ge(unit_done, 4 * i + (s - RING + 1))
                    split(s, 16 * i + 16, 4 * i + s)

        @block.tensor
        def _(pe):
            def three(out, w, x, k, first, last, flip=False):
                (wh, wl), (xh, xl) = w, x
                for n, (a, b) in enumerate(((wh, xh), (wh, xl), (wl, xh))):
                    if flip:
                        a, b = b, a
                    mm = pe.matmul(out, a, b, start=(first and n == 0), stop=(last and n == 2))
                return mm

            def ring(u, blk, n=P):
                s = u % RING
                return HI[:, s, n * blk:n * (blk + 1)], LO[:, s, n * blk:n * (blk + 1)]

            def product(u, g, split0):
                pe.wait_ge(unit_split, u + 1)
                if g >= 2:
                    pe.wait_ge(gemm_freed, g - 1)
                for k in range(KC):
                    pe.wait_ge(gl_made, split0 + k + 1)
                    mm = three(bank_of(g)[:, :], ring(u, k), (GH[:, k, :], GL[:, k, :]), k, k == 0, k == KC - 1)
                mm.then_inc(unit_done, 1)

            def product_tokens(u0, banks, split0):
                for u in range(u0, u0 + 4):
                    pe.wait_ge(unit_split, u + 1)
                    for kk in range(2):
                        k = 2 * (u - u0) + kk
                        pe.wait_ge(gl_made, split0 + k + 1)
                        for b in range(NB):
                            mm = three(PS[banks[b]][:, :], ring(u, kk, 512),
                                       (GH[:, k, P * b:P * (b + 1)], GL[:, k, P * b:P * (b + 1)]),
                                       k, k == 0, k == KC - 1, flip=True)
                    mm.then_inc(unit_done, 1)

            def sum_squares(n):
                pe.wait_ge(sq_added, KC * (n + 1))
                pe.matmul(PS[7][:, :], ONES, ACC, start=True, stop=True).then_inc(ss_made, 1)

            def token_columns(n, bank):
                pe.wait_ge(rb_ready, n)
                for b in range(NB):
                    mm = pe.matmul(PS[bank][:, b:b + 1], RB[0:1, P * b:P * (b + 1)], ONES[0:1, 0:1],
                                   start=True, stop=True)
                mm.then_inc(rcol_mm, 1)

            pe.wait_ge(con_landed, 16)

            sum_squares(0)
            product_tokens(U_VB, (2, 3, 4, 5), 0)
            token_columns(1, 7)
            pe.wait_ge(rcol_made, 1)
            product_tokens(U_VA, (6, 7, 0, 1), 0)
            pe.wait_ge(va_freed, 4)
            product(U_F, G_F, 0)

            def scores(h):
                pe.wait_ge(negc_ready, 1)
                if h >= 1:
                    pe.wait_ge(ncb_made, h)
                pe.matmul(PS[7][:, :], IDENT[0:8, h:h + 1].to_broadcast([8, P]), FR[0:8, 2, :],
                          start=True, stop=True).then_inc(ncb_mm, 1)
                pe.wait_ge(gemm_freed, G_QK + 2 * (h // 2) + 2)
                pe.wait_ge(vb_freed, 4)
                r = 64 * (h % 2)
                for i in range(NB):
                    s = NB * h + i
                    if s >= 2:
                        pe.wait_ge(exp_made, s - 1)
                    pe.matmul(PS[2 + s % 2][:, 0:P * (i + 1)], MT[r:r + 64, 4 + h // 2, P * i:P * (i + 1)],
                              KT1[r:r + 64, h // 2, 0:P * (i + 1)], start=True, stop=True).then_inc(s_made, 1)

            def turn(h):
                for i in range(NB):
                    n = NB * h + i
                    pe.wait_ge(p_ready, n + 1)
                    if n >= 2:
                        pe.wait_ge(pt_freed, n - 1)
                    for j in range(i + 1):
                        mm = pe.transpose(PS[4 + n % 2][:, P * j:P * (j + 1)],
                                          P1[:, h % 2, PCOL[i] + P * j:PCOL[i] + P * (j + 1)], IDENT)
                    mm.then_inc(pt_mm, 1)

            def attend(h):
                pe.wait_ge(pt_freed, NB * (h + 1))
                if h % 2 == 0 and h >= 2:
                    pe.wait_ge(attended, h // 2)
                r = 64 * (h % 2)
                for j in range(NB):
                    mm = pe.matmul(PS[6][r:r + 64, P * j:T], VB[:, j, 64 * h:64 * (h + 1)], PT1[:, j, P * j:T],
                                   start=(j == 0), stop=(j == NB - 1))
                mm.then_inc(pv_made, 1)

            def gate(p):
                pe.wait_ge(vn_ready, 1)
                pe.wait_ge(sgw_masked, 1)
                pe.wait_ge(gemm_freed, G_WO)
                if p >= 2:
                    pe.wait_ge(gated, p - 1)
                for b in range(NB):
                    for e in range(2):
                        hh = 2 * p + e
                        mm = pe.matmul(PS[p % 2][64 * e:64 * e + 64, P * b:P * (b + 1)],
                                       VA[:, b, 64 * hh:64 * (hh + 1)], SGW[:, hh, :], start=True, stop=True)
                mm.then_inc(gate_mm, 1)

            for what, n in MIX1_ORDER:
                if what == "qk":
                    product(U_QK + n, G_QK + n, 0)
                elif what == "u":
                    product(U_UA + n, G_UA + n, 0)
                elif what == "A":
                    scores(n)
                elif what == "B":
                    turn(n)
                elif what == "C":
                    attend(n)
                elif what == "gate":
                    gate(n)
            pe.wait_ge(gated, 4)
            for m in range(KC):
                product(U_WO + m, G_WO + m, KC)

            sum_squares(1)
            with pe.Fori(0, NFF // 2) as i:
                for q in range(4):
                    u, g = U_UP + q, G_UP + q
                    pe.wait_ge(unit_split, 4 * i + (u + 1))
                    pe.wait_ge(gemm_freed, 4 * i + (g - 1))
                    for k in range(KC):
                        if q == 0:
                            pe.wait_ge(gl_made, 2 * KC + k + 1)
                        mm = three(bank_of(g)[:, :], ring(u, k), (GH[:, k, :], GL[:, k, :]), k, k == 0, k == KC - 1)
                    mm.then_inc(unit_done, 1)
            for m in range(KC):
                pe.wait_ge(gemm_freed, G_DN + m - 1)
                for c in range(NFF):
                    n = NFF * m + c
                    u = U_DN + n // 8
                    if n % 8 == 0:
                        pe.wait_ge(unit_split, u + 1)
                    if m == 0:
                        pe.wait_ge(al_made, c + 1)
                    mm = three(bank_of(G_DN + m)[:, :], ring(u, n % 8), (AH[:, c, :], AL[:, c, :]), c, c == 0, c == NFF - 1)
                    if n % 8 == 7:
                        mm.then_inc(unit_done, 1)
                    elif c == NFF - 1:
                        mm.then_inc(down_done, 1)
            sum_squares(2)

            sum_squares(3)

            def lam():
                pe.wait_ge(lam_prod, 1)
                pe.matmul(PS[2][:, 0:2], ONES[0:64, :], LP[0:64, :], start=True, stop=True).then_inc(lam_mm, 1)
                token_columns(4, 3)

            def rows_to_columns():
                pe.wait_ge(rows_ready, 1)
                for b in range(NB):
                    mm = pe.transpose(PS[4][:, P * b:P * (b + 1)], RS[:, P * b:P * (b + 1)], IDENT)
                mm.then_inc(cols_mm, 1)
                for h in range(4):
                    if h >= 2:
                        pe.wait_ge(gcb_made, h - 1)
                    pe.matmul(PS[2 + h % 2][:, :], IDENT[0:4, h:h + 1].to_broadcast([4, P]), RS[0:4, :],
                              start=True, stop=True).then_inc(gcb_mm, 1)

            def head_sums(t):
                pe.wait_ge(l2_sq, t + 1)
                if t >= 2:
                    pe.wait_ge(l2_rt, t - 1)
                else:
                    pe.wait_ge(gcb_made, 4)
                pe.matmul(PS[2 + t % 2][:, :], ONES, SQ2[:, t % 2, :], start=True, stop=True).then_inc(l2_mm, 1)

            def qk_sums(n):
                pe.wait_ge(qn_sq, n + 1)
                pe.matmul(bank_of(G_DFQK + n)[:, :], HALF, SQD[:, :], start=True, stop=True).then_inc(qn_mm, 1)

            def blk(b):
                return slice(P * b, P * (b + 1))

            def banks_for(b):
                return (PS[2 + 3 * (b % 2)], PS[3 + 3 * (b % 2)], PS[4 + 3 * (b % 2)])

            def token_major(b):
                A, B, C = banks_for(b)
                if b < 2:
                    pe.wait_ge(l2_made, 8)
                    pe.wait_ge(cv_s, 12)
                    pe.wait_ge(cols_made, 1)
                    pe.wait_ge(dfv_freed, 2)
                else:
                    pe.wait_ge(uw_made, 2 * (b - 1))
                for h in range(4):
                    mm = pe.transpose(A[:, blk(h)], KT[:, h, blk(b)], IDENT)
                mm.then_inc(tk_mm, 1)
                for h in range(4):
                    mm = pe.transpose(B[:, blk(h)], VT[:, h, blk(b)], IDENT)
                mm.then_inc(tv_mm, 1)
                for h in range(4):
                    mm = pe.matmul(C[:, blk(h)], KT[:, h, blk(b)], KT[:, h, blk(b)], start=True, stop=True)
                mm.then_inc(g_mm, 1)
                pe.wait_ge(kd_made, b + 1)
                for h in range(4):
                    mm = pe.matmul(A[:, blk(h)], KT[:, h, blk(b)], QT[:, h, blk(b)], start=True, stop=True)
                mm.then_inc(aq_mm, 1)

            def inverse_y(b, l):
                A = banks_for(b)[0]
                s = b % 2
                if l == 0:
                    pe.wait_ge(nt_made, b + 1)
                else:
                    pe.wait_ge(xi_made, step(b, l - 1) + 1)
                for h in range(4):
                    rhs = IDENT if l == 0 else XI[:, s, h, :]
                    mm = pe.matmul(A[:, blk(h)], NT[:, s, h, :], rhs, start=True, stop=True)
                mm.then_inc(y_mm, 1)

            def inverse_z(b, l):
                s = b % 2
                pe.wait_ge(ym_made, step(b, l) + 1)
                pe.wait_ge(xt_made, step(b, l - 1) + 1)
                for h in range(4):
                    mm = pe.matmul(banks_for(b)[1][:, blk(h)], XT[:, s, h, :], YM[:, s, h, :], start=True, stop=True)
                mm.then_inc(z_mm, 1)

            def inverse_x(b, l):
                pe.wait_ge(xi_made, step(b, l) + 1)
                if l >= 1:
                    pe.wait_ge(xt_made, step(b, l - 1) + 1)
                for h in range(4):
                    mm = pe.transpose(banks_for(b)[2][:, blk(h)], XI[:, b % 2, h, :], IDENT)
                mm.then_inc(xt_mm, 1)

            def solve(b):
                A, B, C = banks_for(b)
                s = b % 2
                pe.wait_ge(xt_made, step(b, LEVELS - 1) + 1)
                pe.wait_ge(vbt_made, b + 1)
                for h in range(4):
                    mm = pe.matmul(A[:, blk(h)], XT[:, s, h, :], VBT[:, s, h, :], start=True, stop=True)
                mm.then_inc(u_mm, 1)
                for h in range(4):
                    mm = pe.matmul(B[:, blk(h)], KBE[:, s, h, :], XT[:, s, h, :], start=True, stop=True)
                mm.then_inc(w_mm, 1)

            def scan(i):
                b, r = i // 2, 64 * (i % 2)
                pe.wait_ge(st_made, i + 1)
                pe.wait_ge(uw_made, 8)
                pe.wait_ge(qe_made, 4)
                if i >= 1:
                    pe.wait_ge(od_made, i)
                for h in range(4):
                    mm = pe.matmul(PS[6][r:r + 64, blk(h)], KT[:, h, P * b + r:P * b + r + 64], ST[:, h, :],
                                   start=True, stop=True)
                mm.then_inc(ws_mm, 1)
                pe.wait_ge(vn_made, i + 1)
                for h in range(4):
                    o = PS[6][:, 64 * h:64 * h + 64]
                    pe.matmul(o, ST[:, h, :], QT[:, h, CH * i:CH * (i + 1)], start=True, stop=False)
                    mm = pe.matmul(o, VT[:, h, blk(b)], AQK[:, b, h, r:r + 64], start=False, stop=True)
                mm.then_inc(ot_mm, 1)
                for h in range(4):
                    mm = pe.matmul(PS[7][:, blk(h)], KDEC[r:r + 64, b, h, :], VT[r:r + 64, h, blk(b)],
                                   start=True, stop=True)
                mm.then_inc(kv_mm, 1)

            def df_scores(h):
                pe.wait_ge(qn_made, 8)
                pe.wait_ge(uw_made, 8)
                for i in range(NB):
                    for c in range(2):
                        e = 2 * (NB * h + i) + c
                        if e >= 2:
                            pe.wait_ge(dexp, e - 1)
                        pe.matmul(PS[2 + c][:, 0:P * (i + 1)], DQ[64 * c:64 * c + 64, h, blk(i)],
                                  DK[64 * c:64 * c + 64, h, 0:P * (i + 1)], start=True, stop=True)\
                          .then_inc(ds_mm, 1)

            def df_turn(h):
                for i in range(NB):
                    n = NB * h + i
                    pe.wait_ge(dw_made, n + 1)
                    if n >= 1:
                        pe.wait_ge(dpt_freed, n)
                    for j in range(i + 1):
                        mm = pe.transpose(PS[4][:, blk(j)], P0[:, h % 2, PCOL[i] + P * j:PCOL[i] + P * (j + 1)], IDENT)
                    mm.then_inc(dpt_mm, 1)

            def df_attend(h):
                pe.wait_ge(dpt_freed, NB * (h + 1))
                if h >= 1:
                    pe.wait_ge(dpv_freed, h)
                for j in range(NB):
                    mm = pe.matmul(PS[5][:, P * j:T], DV[:, j, blk(h)], PT2[:, j, P * j:T],
                                   start=(j == 0), stop=(j == NB - 1))
                mm.then_inc(dpv_mm, 1)

            def out_sums(t):
                pe.wait_ge(o_sq, t + 1)
                if t >= 2:
                    pe.wait_ge(o_rt, t - 1)
                pe.matmul(PS[2 + t % 2][:, :], ONES, SQO[:, t, :], start=True, stop=True).then_inc(o_mm, 1)

            for what, n in MIX2_ORDER:
                if what == "lam":
                    lam()
                elif what == "ba":
                    product(U_BA, G_BA, 3 * KC)
                elif what == "kqv":
                    product(U_KQV + n, G_KQV + n, 3 * KC)
                elif what == "cols":
                    rows_to_columns()
                elif what == "dfv":
                    pe.wait_ge(gemm_freed, G_DFQK)
                    product_tokens(U_DFV, (6, 7, 0, 1), 3 * KC)
                    pe.wait_ge(dfv_freed, 4)
                elif what == "l2":
                    head_sums(n)
                elif what == "dfqk":
                    if n >= 2:
                        pe.wait_ge(qn_rt, n - 1)
                    product(U_DFQK + n, G_DFQK + n, 3 * KC)
                    if n >= 1:
                        qk_sums(n - 1)
                elif what == "T":
                    token_major(n)
                elif what == "Y":
                    inverse_y(*n)
                elif what == "Z":
                    inverse_z(*n)
                elif what == "X":
                    inverse_x(*n)
                elif what == "W":
                    solve(n)
                elif what == "scan":
                    scan(n)
                elif what == "A":
                    if n == 0:
                        qk_sums(7)
                    df_scores(n)
                elif what == "B":
                    df_turn(n)
                elif what == "C":
                    df_attend(n)
                elif what == "z":
                    if n == 0:
                        pe.wait_ge(qn_rt, 8)
                    product(U_Z + n, G_Z + n, 3 * KC)
                elif what == "out":
                    out_sums(n)
            for m in range(KC):
                product(U_WO2 + m, G_WO2 + m, 4 * KC)

        @block.scalar
        def _(act):
            act.dma_start(PAR[:, :], params).then_inc(par_landed, 16)
            act.dma_start(CON[:, :], consts).then_inc(con_landed, 16)
            act.dma_start(SGW[:, :, :], sgw_t).then_inc(sg_landed, 16)
            for e in range(2):
                act.dma_start(SGB[64 * e:64 * e + 64, :, :],
                              sgb[:, e, :].unsqueeze(0).to_broadcast([64, 4, P])).then_inc(sg_landed, 16)
            act.wait_ge(par_landed, 16)
            act.wait_ge(eps_made, 4)

            def square_tile(n, k):
                if KC * n + k >= 1:
                    act.wait_ge(sq_added, KC * n + k)
                act.activation(SQ[:, 0, :], X[:, k, :], ACT.Square).then_inc(sq_made, 1)

            def root(n):
                act.wait_ge(ss_made, n + 1)
                act.activation(RB[:, :], PS[7][:, :], ACT.Sqrt, scale=1.0 / D, bias=EPSC[:, 0:1])\
                   .then_inc(rms_made, 1)

            def high(src, k, gain=None):
                act.activation(GH[:, k, :], src, ACT.Copy, scale=1.0 if gain is None else par(gain + k))\
                   .then_inc(gh_made, 1)

            for k in range(KC):
                act.wait_ge(x_landed[k], 16)
                high(X[:, k, :], k, C_GMIX)
                square_tile(0, k)
            root(0)
            act.wait_ge(rcol_made, 1)
            act.wait_ge(unit_done, U_VB + 4)
            for b in range(NB):
                act.activation(VB[:, b, :], PS[2 + b][:, :], ACT.Copy, scale=RCOL[:, b:b + 1]).then_inc(vb_freed, 1)
            act.wait_ge(unit_done, U_VA + 4)
            for b, bank in enumerate((6, 7, 0, 1)):
                act.activation(VA[:, b, :], PS[bank][:, :], ACT.Gelu, scale=RCOL[:, b:b + 1]).then_inc(va_freed, 1)
            act.wait_ge(ln_centered, 1)
            act.activation(SQV[:, :, :], VA[:, :, :], ACT.Square).then_inc(ln_squared, 1)
            act.wait_ge(ln_summed, 1)
            act.activation(LNV, LNV, ACT.Sqrt, scale=1.0 / HD, bias=EPSC[:, 0:1]).then_inc(ln_root, 1)
            act.wait_ge(f_made, 1)
            act.activation(FR[0:8, 1, :], FR[0:8, 0, :], ACT.Abs).then_inc(f_log, 1)
            act.wait_ge(f_log, 1)
            act.activation(FR[0:8, 1, :], FR[0:8, 1, :], ACT.Exp, scale=-1.0).then_inc(f_log, 1)
            act.wait_ge(f_log, 2)
            act.activation(FR[0:8, 1, :], FR[0:8, 1, :], ACT.Ln, bias=EPSC[0:8, 3:4]).then_inc(f_log, 1)

            for what, h in MIX1_ORDER:
                if what == "A":
                    act.wait_ge(ncb_mm, h + 1)
                    if h >= 2:
                        act.wait_ge(max_made, NB * (h - 1))
                    act.activation(NCB[:, h % 2, :], PS[7][:, :], ACT.Copy).then_inc(ncb_made, 1)
                    for i in range(NB):
                        s = NB * h + i
                        w = P * (i + 1)
                        act.wait_ge(max_made, s + 1)
                        if h >= 2:
                            act.wait_ge(pt_mm, NB * (h - 2) + i + 1)
                        act.activation(P1[:, h % 2, PCOL[i]:PCOL[i] + w], PS[2 + s % 2][:, 0:w], ACT.Exp,
                                       scale=-1.0, bias=MX[:, h % 2, i:i + 1], accum_out=SU[:, h % 2, i:i + 1])\
                           .then_inc(exp_made, 1)
                elif what == "B":
                    if h >= 1:
                        act.wait_ge(pv_made, h)
                    for i in range(NB):
                        n = NB * h + i
                        act.wait_ge(pt_mm, n + 1)
                        act.activation(PT1[:, 0:i + 1, P * i:P * (i + 1)],
                                       PS[4 + n % 2][:, 0:P * (i + 1)].rearrange("p (j c) -> p j c", c=P),
                                       ACT.Copy).then_inc(pt_freed, 1)
                elif what == "gelu":
                    for p in range(4):
                        act.wait_ge(gemm_freed, G_UA + p + 1)
                        act.activation(MT[:, p, :], MT[:, p, :], ACT.Gelu).then_inc(gelu_made, 1)
            act.wait_ge(unit_done, U_WO)
            for k in range(KC):
                if k < 4:
                    act.wait_ge(gated, k + 1)
                else:
                    act.wait_ge(attended, k - 3)
                high(MT[:, k, :], k)
            for m in range(KC):
                act.wait_ge(gemm_freed, G_WO + m + 1)
                square_tile(1, m)

            act.wait_ge(unit_done, U_UP)
            for k in range(KC):
                high(X[:, k, :], k, C_GFFN)
            root(1)

            def feed_forward(t):
                for gv in range(2):
                    act.wait_ge(gemm_freed, 2 * t + (G_UP + gv + 1))
                    act.activation(YC[:, gv, :], AB[:, gv, 2:T + 2], ACT.Identity,
                                   scale=PAR[:, bass.ds(6 * t + (C_FCW + 3 * gv + 2), 1)],
                                   bias=PAR[:, bass.ds(2 * t + (C_FCB + gv), 1)]).then_inc(conv_started, 1)
                act.wait_ge(conv_made, 2 * t + 1)
                act.activation(YC[:, 0, :], YC[:, 0, :], ACT.Silu).then_inc(silu_ff, 1)
                act.wait_ge(ff_made, t + 1)
                act.activation(AH[:, bass.ds(t, 1), :], YC[:, 0:1, :], ACT.Copy).then_inc(ah_made, 1)

            feed_forward(0)
            with act.Fori(1, NFF) as t:
                act.wait_ge(al_made, t)
                feed_forward(t)
            for m in range(KC):
                act.wait_ge(gemm_freed, G_DN + m + 1)
                square_tile(2, m)
            root(2)
            for k in range(KC):
                act.wait_ge(x_updated, k + 1)
                high(X[:, k, :], k, C_GN2)
                square_tile(3, k)
            root(3)

            def rows():
                act.activation(EA[0:4, :], par(C_ALOG, 1, 0, 4), ACT.Exp).then_inc(ba_a, 1)
                act.wait_ge(ba_v, 1)
                act.activation(R2[0:4, :], R1[0:4, :], ACT.Abs).then_inc(ba_a, 1)
                act.wait_ge(ba_a, 2)
                act.activation(R2[0:4, :], R2[0:4, :], ACT.Exp, scale=-1.0).then_inc(ba_a, 1)
                act.wait_ge(ba_a, 3)
                act.activation(R2[0:4, :], R2[0:4, :], ACT.Ln, bias=EPSC[0:4, 3:4]).then_inc(ba_a, 1)
                act.activation(R3[32:36, :], BR[32:36, :], ACT.Exp, scale=-1.0).then_inc(ba_a, 1)
                act.wait_ge(ba_v, 3)
                act.activation(R3[32:36, :], RS[0:4, :], ACT.Exp).then_inc(ba_a, 1)
                act.activation(RS[96:100, :], R1[0:4, :], ACT.Exp).then_inc(ba_a, 1)

            def tile_of(t):
                return (KT, QT, VT)[t // 4][:, t % 4, :]

            for what, n in MIX2_ORDER:
                if what == "lam":
                    act.wait_ge(lam_mm, 1)
                    act.activation(LE, PS[2][:, 0:2], ACT.Exp).then_inc(lam_exp, 1)
                elif what == "ba":
                    rows()
                elif what == "kqv":
                    act.wait_ge(gemm_freed, G_KQV + n + 1)
                    act.activation(tile_of(n), CB[:, n % 2, 3:T + 3], ACT.Copy,
                                   scale=par(C_DCW + 4 * n + 3)).then_inc(cv_a, 1)
                    act.wait_ge(cv_v, n + 1)
                    act.activation(tile_of(n), tile_of(n), ACT.Silu).then_inc(cv_s, 1)
                elif what == "cols":
                    for h in range(4):
                        act.wait_ge(gcb_mm, h + 1)
                        act.activation(EG[:, h, :], PS[2 + h % 2][:, :], ACT.Copy).then_inc(gcb_made, 1)
                elif what == "dfv":
                    act.wait_ge(rcol_made, 2)
                    act.wait_ge(unit_done, U_DFV + 4)
                    for b, bank in enumerate((6, 7, 0, 1)):
                        act.activation(DV[:, b, :], PS[bank][:, :], ACT.Copy, scale=RCOL[:, b:b + 1])\
                           .then_inc(dfv_freed, 1)
                elif what == "l2":
                    act.wait_ge(cv_s, n + 1)
                    if n >= 2:
                        act.wait_ge(l2_mm, n - 1)
                    act.activation(SQ2[:, n % 2, :], tile_of(n), ACT.Square).then_inc(l2_sq, 1)
                    act.wait_ge(l2_mm, n + 1)
                    if n >= 2:
                        act.wait_ge(l2_made, n - 1)
                    act.activation(NR2[:, n % 2, :], PS[2 + n % 2][:, :], ACT.Sqrt, scale=1.0 if n < 4 else 128.0,
                                   bias=EPSC[:, 0:1] if n < 4 else EPSC[:, 1:2]).then_inc(l2_rt, 1)
                elif what == "dfqk" or (what == "A" and n == 0):
                    if what == "dfqk":
                        m = n - 1
                    else:
                        m = 7
                    if m >= 0:
                        tile = (DQ if m % 2 == 0 else DK)[:, m // 2, :]
                        act.wait_ge(gemm_freed, G_DFQK + m + 1)
                        if m >= 1:
                            act.wait_ge(qn_mm, m)
                        act.activation(SQD[:, :], tile, ACT.Square).then_inc(qn_sq, 1)
                        act.wait_ge(qn_mm, m + 1)
                        if m >= 1:
                            act.wait_ge(qn_made, m)
                        act.activation(NRD[:, :], bank_of(G_DFQK + m)[:, :], ACT.Sqrt,
                                       scale=1.0 if m % 2 == 0 else 1.0 / HD,
                                       bias=EPSC[:, 2:3] if m % 2 == 0 else EPSC[:, 0:1]).then_inc(qn_rt, 1)
                elif what == "T":
                    act.wait_ge(d_made, n + 1)
                    act.activation(NT[:, n % 2, :, :], NT[:, n % 2, :, :], ACT.Exp).then_inc(d_exp, 1)
                    act.activation(EG[:, :, P * n:P * (n + 1)], EG[:, :, P * n:P * (n + 1)], ACT.Exp)\
                       .then_inc(eg_made, 1)
                elif what == "X":
                    b, l = n
                    act.wait_ge(xt_mm, step(b, l) + 1)
                    act.activation(XT[:, b % 2, :, :], heads(PS[4 + 3 * (b % 2)][:, :]), ACT.Copy)\
                       .then_inc(xt_made, 1)
                elif what == "W":
                    act.wait_ge(u_mm, n + 1)
                    act.activation(VT[:, :, P * n:P * (n + 1)], heads(PS[2 + 3 * (n % 2)][:, :]), ACT.Copy)\
                       .then_inc(uw_made, 1)
                    act.wait_ge(w_mm, n + 1)
                    act.activation(KT[:, :, P * n:P * (n + 1)], heads(PS[3 + 3 * (n % 2)][:, :]), ACT.Copy)\
                       .then_inc(uw_made, 1)
                elif what == "scan":
                    act.wait_ge(ot_mm, n + 1)
                    act.activation(QT[:, :, CH * n:CH * (n + 1)],
                                   PS[6][:, 0:4 * CH].rearrange("p (h c) -> p h c", h=4), ACT.Copy)\
                       .then_inc(od_made, 1)
                elif what == "B":
                    if n >= 1:
                        act.wait_ge(dpv_mm, n)
                    for i in range(NB):
                        m = NB * n + i
                        act.wait_ge(dpt_mm, m + 1)
                        act.activation(PT2[:, 0:i + 1, P * i:P * (i + 1)],
                                       PS[4][:, 0:P * (i + 1)].rearrange("p (j c) -> p j c", c=P),
                                       ACT.Copy).then_inc(dpt_freed, 1)
                elif what == "C":
                    act.wait_ge(dpv_mm, n + 1)
                    act.activation(DQ[:, n, :], PS[5][:, :], ACT.Copy).then_inc(dpv_freed, 1)
                elif what == "silu":
                    for t in range(8):
                        act.wait_ge(gemm_freed, G_Z + t + 1)
                        act.activation(ZT[:, t, :], ZT[:, t, :], ACT.Silu).then_inc(silu_z, 1)
                    act.wait_ge(od_made, 8)
                    act.wait_ge(dpv_freed, 4)
                    for t in range(8):
                        act.activation(SQO[:, t, :], (QT, DQ)[t // 4][:, t % 4, :], ACT.Square).then_inc(o_sq, 1)
                    act.wait_ge(unit_done, U_WO2)
                    for t in range(8):
                        act.wait_ge(o_mm, t + 1)
                        act.activation(NRO[:, t, :], PS[2 + t % 2][:, :], ACT.Sqrt, scale=1.0 / P,
                                       bias=EPSC[:, 0:1]).then_inc(o_rt, 1)
                    for t in range(8):
                        act.wait_ge(o_made, t + 1)
                        high((QT, DQ)[t // 4][:, t % 4, :], t)
                if what == "A":
                    for i in range(NB):
                        w = P * (i + 1)
                        if n >= 2:
                            act.wait_ge(dpt_mm, NB * (n - 2) + i + 1)
                        if n >= 1:
                            act.wait_ge(dw_made, NB * (n - 1) + i + 1)
                        else:
                            act.wait_ge(uw_made, 8)
                        for c in range(2):
                            e = 2 * (NB * n + i) + c
                            dst = P0[:, n % 2, PCOL[i]:PCOL[i] + w] if c == 0 else PB[:, PCOL[i]:PCOL[i] + w]
                            act.wait_ge(dmax, e + 1)
                            act.activation(dst, PS[2 + c][:, 0:w], ACT.Exp, scale=-1.0,
                                           bias=MX[:, n % 2, 2 * i + c:2 * i + c + 1],
                                           accum_out=SU[:, n % 2, 2 * i + c:2 * i + c + 1]).then_inc(dexp, 1)

        @block.vector
        def _(dve):
            chain = [0]

            def then(ins):
                chain[0] += 1
                ins.then_inc(v_chain, 1)
                dve.wait_ge(v_chain, chain[0])

            for c, v in enumerate((EPS, 128 * EPS, 64 * EPS, 1.0)):
                dve.memset(EPSC[:, c:c + 1], v).then_inc(eps_made, 1)
            dve.wait_ge(par_landed, 16)
            dve.wait_ge(con_landed, 16)

            def low(src, k, n, gain=None):
                dve.wait_ge(gh_made, KC * n + k + 1)
                if gain is None:
                    dve.tensor_tensor(GL[:, k, :], src, GH[:, k, :].bitcast(F32), ALU.subtract).then_inc(gl_made, 1)
                else:
                    dve.scalar_tensor_tensor(GL[:, k, :], src, par(gain + k), GH[:, k, :].bitcast(F32),
                                             ALU.mult, ALU.subtract).then_inc(gl_made, 1)

            def add_square(n, k):
                dve.wait_ge(sq_made, KC * n + k + 1)
                if k == 0:
                    if n:
                        dve.wait_ge(ss_made, n)
                    dve.tensor_copy(ACC, SQ[:, 0, :]).then_inc(sq_added, 1)
                else:
                    dve.wait_ge(sq_added, KC * n + k)
                    dve.tensor_tensor(ACC, ACC, SQ[:, 0, :], ALU.add).then_inc(sq_added, 1)

            def invert_rms(n):
                dve.wait_ge(rms_made, n + 1)
                dve.reciprocal(RB[:, :], RB[:, :]).then_inc(rb_ready, 1)
                dve.wait_ge(rb_ready, n + 1)

            def evacuate(g, unit, out, rows=P):
                dve.wait_ge(unit_done, unit + 1)
                dve.tensor_tensor(out, bank_of(g)[0:rows, :], RB[0:rows, :], ALU.mult).then_inc(gemm_freed, 1)
                dve.wait_ge(gemm_freed, g + 1)

            for k in range(KC):
                low(X[:, k, :], k, 0, C_GMIX)
                add_square(0, k)
            dve.wait_ge(sg_landed, 48)
            dve.memset(SGW[64:128, :, 0:64], 0.0).then_inc(sgw_masked, 1)
            invert_rms(0)
            dve.wait_ge(rcol_mm, 1)
            dve.tensor_copy(RCOL, PS[7][:, 0:NB]).then_inc(rcol_made, 1)

            groups = VA[:, :, :].rearrange("p b (h d) -> p (b h) d", d=HD)

            def over_group(col):
                return col.unsqueeze(2).to_broadcast([P, 32, HD])

            dve.wait_ge(va_freed, 4)
            then(dve.tensor_reduce(LNS, groups, AX_X, ALU.add))
            then(dve.tensor_scalar(LNS, LNS, 1.0 / HD, None, ALU.mult))
            dve.tensor_tensor(groups, groups, over_group(LNS), ALU.subtract).then_inc(ln_centered, 1)
            evacuate(G_F, U_F, FR[0:8, 0, :], 8)
            dve.tensor_scalar(FR[0:8, 0, :], FR[0:8, 0, :], par(C_FB, 1, 0, 8), None, ALU.add).then_inc(f_made, 1)
            dve.wait_ge(ln_squared, 1)
            dve.tensor_reduce(LNV, SQV[:, :, :].rearrange("p b (h d) -> p (b h) d", d=HD), AX_X, ALU.add)\
               .then_inc(ln_summed, 1)
            dve.wait_ge(f_log, 3)
            then(dve.tensor_scalar(FR[0:8, 0, :], FR[0:8, 0, :], -1.0, 0.0, ALU.mult, ALU.max))
            dve.tensor_tensor_scan(FR[0:8, 2, :], FR[0:8, 0, :], FR[0:8, 1, :], 0.0, ALU.add, ALU.add)\
               .then_inc(negc_ready, 1)
            dve.wait_ge(ln_root, 1)
            then(dve.reciprocal(LNV, LNV))
            dve.wait_ge(ln_centered, 1)
            dve.tensor_tensor(groups, groups, over_group(LNV), ALU.mult).then_inc(vn_ready, 1)

            def biased_max(h, i):
                s = NB * h + i
                S = PS[2 + s % 2]
                e = h % 2
                dve.wait_ge(s_made, s + 1)
                first = 3e38
                if i:
                    then(dve.tensor_tensor_reduce(S[:, 0:P * i], S[:, 0:P * i], NCB[:, e, 0:P * i], -1.0, 3e38,
                                                  ALU.add, ALU.min, MXA[:, 4 * e + i:4 * e + i + 1]))
                    first = MXA[:, 4 * e + i:4 * e + i + 1]
                dve.tensor_tensor_reduce(S[:, P * i:P * (i + 1)], S[:, P * i:P * (i + 1)],
                                         NCD[:, e, P * i:P * (i + 1)], -1.0, first,
                                         ALU.add, ALU.min, MX[:, e, i:i + 1]).then_inc(max_made, 1)

            def normalise(h, i):
                e = h % 2
                p = P1[:, e, PCOL[i]:PCOL[i] + P * (i + 1)]
                dve.wait_ge(exp_made, NB * h + i + 1)
                then(dve.reciprocal(RC[:, e, i:i + 1], SU[:, e, i:i + 1]))
                dve.tensor_scalar(p, p, RC[:, e, i:i + 1], None, ALU.mult).then_inc(p_ready, 1)

            for what, n in MIX1_ORDER:
                if what == "qk":
                    g = G_QK + n
                    p = n // 2
                    if n % 2 == 0:
                        dve.wait_ge(unit_done, U_QK + n + 1)
                        dve.scalar_tensor_tensor(MT[:, 4 + p, :], bank_of(g)[:, :], HD ** -0.5, RB[:, :],
                                                 ALU.mult, ALU.mult).then_inc(gemm_freed, 1)
                    else:
                        dve.wait_ge(unit_done, U_QK + n + 1)
                        dve.tensor_tensor(KT1[:, p, :], bank_of(g)[:, :], RB[:, :], ALU.mult)\
                           .then_inc(gemm_freed, 1)
                    dve.wait_ge(gemm_freed, g + 1)
                elif what == "u":
                    evacuate(G_UA + n, U_UA + n, MT[:, n, :])
                elif what == "A":
                    dve.wait_ge(ncb_made, n + 1)
                    then(dve.tensor_tensor(heads(NCD[:, n % 2, :]), heads(NCB[:, n % 2, :]),
                                           CAUSAL[:, 384:512].unsqueeze(1).to_broadcast([P, 4, P]), ALU.add))
                    biased_max(n, 0)
                    for i in range(1, NB):
                        biased_max(n, i)
                        normalise(n, i - 1)
                    normalise(n, NB - 1)
                elif what == "C" and n % 2 == 1:
                    dve.wait_ge(pv_made, n + 1)
                    dve.tensor_copy(MT[:, 4 + n // 2, :], PS[6][:, :]).then_inc(attended, 1)
                elif what == "gate":
                    dve.wait_ge(gate_mm, n + 1)
                    dve.wait_ge(gelu_made, n + 1)
                    then(dve.scalar_tensor_tensor(heads(SQV[:, n, :]), heads(PS[n % 2][:, :]), par(C_SGG + n),
                                                  SGB[:, n, :].unsqueeze(1).to_broadcast([P, 4, P]),
                                                  ALU.mult, ALU.add))
                    dve.tensor_tensor(MT[:, n, :], MT[:, n, :], SQV[:, n, :], ALU.mult).then_inc(gated, 1)
            for k in range(KC):
                low(MT[:, k, :], k, 1)
            for m in range(KC):
                dve.wait_ge(unit_done, U_WO + m + 1)
                dve.tensor_tensor(X[:, m, :], X[:, m, :], bank_of(G_WO + m)[:, :], ALU.add).then_inc(gemm_freed, 1)
                dve.wait_ge(gemm_freed, G_WO + m + 1)
                add_square(1, m)
            for k in range(KC):
                low(X[:, k, :], k, 2, C_GFFN)
            invert_rms(1)
            then(dve.memset(AB[:, :, 0:2], 0.0))
            c0 = chain[0]
            with dve.Fori(0, NFF) as t:
                for gv in range(2):
                    dve.wait_ge(unit_done, 2 * t + (U_UP + gv + 1))
                    dve.tensor_tensor(AB[:, gv, 2:T + 2], bank_of(G_UP + gv)[:, :], RB[:, :], ALU.mult)\
                       .then_inc(gemm_freed, 1)
                for gv in range(2):
                    dve.wait_ge(gemm_freed, 2 * t + (G_UP + gv + 1))
                    dve.wait_ge(conv_started, 2 * t + (gv + 1))
                    dve.scalar_tensor_tensor(YC[:, gv, :], AB[:, gv, 1:T + 1],
                                             PAR[:, bass.ds(6 * t + (C_FCW + 3 * gv + 1), 1)], YC[:, gv, :],
                                             ALU.mult, ALU.add).then_inc(v_chain, 1)
                    dve.wait_ge(v_chain, 2 * t + (c0 + gv + 1))
                    dve.scalar_tensor_tensor(YC[:, gv, :], AB[:, gv, 0:T],
                                             PAR[:, bass.ds(6 * t + (C_FCW + 3 * gv), 1)], YC[:, gv, :],
                                             ALU.mult, ALU.add).then_inc(conv_made, 1)
                dve.wait_ge(silu_ff, t + 1)
                dve.wait_ge(conv_made, 2 * t + 2)
                dve.tensor_tensor(YC[:, 0, :], YC[:, 0, :], YC[:, 1, :], ALU.mult).then_inc(ff_made, 1)
                dve.wait_ge(ff_made, t + 1)
                dve.wait_ge(ah_made, t + 1)
                dve.tensor_tensor(AL[:, bass.ds(t, 1), :], YC[:, 0:1, :], AH[:, bass.ds(t, 1), :].bitcast(F32),
                                  ALU.subtract).then_inc(al_made, 1)
            chain[0] += 2 * NFF

            for m in range(KC):
                if m in (3, 7):
                    dve.wait_ge(unit_done, U_DN + 11 * (m + 1) // 4)
                else:
                    dve.wait_ge(down_done, m + 1 - m // 4)
                dve.tensor_tensor(X[:, m, :], X[:, m, :], bank_of(G_DN + m)[:, :], ALU.add).then_inc(gemm_freed, 1)
                dve.wait_ge(gemm_freed, G_DN + m + 1)
                add_square(2, m)
            invert_rms(2)
            for k in range(KC):
                dve.scalar_tensor_tensor(X[:, k, :], X[:, k, :], par(C_GFIN + k), RB[:, :],
                                         ALU.mult, ALU.mult).then_inc(x_updated, 1)
            for k in range(KC):
                low(X[:, k, :], k, 3, C_GN2)
                add_square(3, k)
            invert_rms(3)

            def rows():
                dve.tensor_scalar(R1[0:4, :], BR[0:4, :], par(C_DTB, 1, 0, 4), None, ALU.add).then_inc(ba_v, 1)
                then(dve.memset(RS[:, :], 0.0))
                dve.wait_ge(ba_a, 4)
                dve.wait_ge(ba_v, 1)
                then(dve.tensor_scalar(R1[0:4, :], R1[0:4, :], 0.0, None, ALU.max))
                then(dve.tensor_tensor(R1[0:4, :], R1[0:4, :], R2[0:4, :], ALU.add))
                then(dve.tensor_scalar(R1[0:4, :], R1[0:4, :], EA[0:4, :], -1.0, ALU.mult, ALU.mult))
                for c in range(T // CH):
                    last = dve.tensor_tensor_scan(RS[0:4, CH * c:CH * (c + 1)], ONES[0:4, 0:CH],
                                                  R1[0:4, CH * c:CH * (c + 1)], 0.0, ALU.mult, ALU.add)
                then(last)
                dve.wait_ge(ba_a, 5)
                then(dve.tensor_scalar(R3[32:36, :], R3[32:36, :], 1.0, None, ALU.add))
                dve.reciprocal(RS[32:36, :], R3[32:36, :]).then_inc(ba_v, 1)
                rows_by_chunk = RS[0:4, :].rearrange("p (c n) -> p c n", n=CH)
                dve.tensor_tensor(R1[0:4, :].rearrange("p (c n) -> p c n", n=CH),
                                  rows_by_chunk[:, :, CH - 1:CH].to_broadcast([4, T // CH, CH]),
                                  rows_by_chunk, ALU.subtract).then_inc(ba_v, 1)
                dve.wait_ge(ba_a, 7)
                dve.wait_ge(ba_v, 3)
                dve.tensor_tensor(RS[64:68, :], R3[32:36, :], RS[32:36, :], ALU.mult).then_inc(rows_ready, 1)

            def tile_of(t):
                return (KT, QT, VT)[t // 4][:, t % 4, :]

            def over_head(col):
                return col.unsqueeze(2).to_broadcast([P, 4, P])

            def block_inputs(b):
                s = b % 2
                A, B, C = (heads(PS[n + 3 * s][:, :]) for n in (2, 3, 4))
                cols = slice(P * b, P * (b + 1))
                dve.wait_ge(gcb_made, 4)
                dve.wait_ge(cols_made, 1)
                then(dve.tensor_tensor(NT[:, s, :, :], EG[:, :, cols], over_head(COLS[:, b, 0, :]), ALU.subtract))
                dve.tensor_tensor(NT[:, s, :, :], NT[:, s, :, :], GNEG.unsqueeze(1).to_broadcast([P, 4, P]),
                                  ALU.add).then_inc(d_made, 1)
                dve.wait_ge(tk_mm, b + 1)
                dve.tensor_tensor(KBE[:, s, :, :], A, over_head(COLS[:, b, 2, :]), ALU.mult)
                dve.tensor_tensor(KDEC[:, b, :, :], A, over_head(COLS[:, b, 3, :]), ALU.mult).then_inc(kd_made, 1)
                dve.wait_ge(tv_mm, b + 1)
                dve.tensor_tensor(VBT[:, s, :, :], B, over_head(COLS[:, b, 1, :]), ALU.mult).then_inc(vbt_made, 1)
                dve.wait_ge(d_exp, b + 1)
                dve.wait_ge(g_mm, b + 1)
                dve.wait_ge(aq_mm, b + 1)
                dve.tensor_tensor(AQK[:, b, :, :], A, NT[:, s, :, :], ALU.mult)
                dve.tensor_tensor(NT[:, s, :, :], C, NT[:, s, :, :], ALU.mult).then_inc(nt_made, 1)
                dve.wait_ge(eg_made, b + 1)
                dve.tensor_tensor(QT[:, :, cols], QT[:, :, cols], EG[:, :, cols], ALU.mult).then_inc(qe_made, 1)

            def masked_y(b, l):
                A = PS[2 + 3 * (b % 2)]
                dve.wait_ge(y_mm, step(b, l) + 1)
                for h in range(4):
                    last = dve.scalar_tensor_tensor(YM[:, b % 2, h, :], A[:, P * h:P * (h + 1)],
                                                    COLS[:, b, 1, h:h + 1], level_mask(l), ALU.mult, ALU.mult)
                last.then_inc(ym_made, 1)
                if l == 0:
                    dve.wait_ge(ym_made, step(b, l) + 1)
                    dve.tensor_tensor(XI[:, b % 2, :, :], IDENT.unsqueeze(1).to_broadcast([P, 4, P]),
                                      YM[:, b % 2, :, :], ALU.subtract).then_inc(xi_made, 1)

            def next_inverse(b, l):
                dve.wait_ge(z_mm, (b // 2) * 2 * (LEVELS - 1) + 2 * (l - 1) + b % 2 + 1)
                dve.wait_ge(xi_made, step(b, l - 1) + 1)
                dve.tensor_tensor(XI[:, b % 2, :, :], XI[:, b % 2, :, :], heads(PS[3 + 3 * (b % 2)][:, :]),
                                  ALU.subtract).then_inc(xi_made, 1)

            def normalise_qk(m):
                tile = (DQ if m % 2 == 0 else DK)[:, m // 2, :]
                dve.wait_ge(qn_rt, m + 1)
                then(dve.reciprocal(NRD[:, :], NRD[:, :]))
                dve.scalar_tensor_tensor(tile, tile, par(C_QG if m % 2 == 0 else C_KG), NRD[:, :],
                                         ALU.mult, ALU.mult).then_inc(qn_made, 1)

            def masked_max(h, i, c):
                e = 2 * (NB * h + i) + c
                w = P * (i + 1)
                dve.wait_ge(ds_mm, e + 1)
                dve.tensor_tensor_reduce(PS[2 + c][:, 0:w], PS[2 + c][:, 0:w], CAUSAL[:, 512 - w:512], -1.0, 3e38,
                                         ALU.add, ALU.min, MX[:, h % 2, 2 * i + c:2 * i + c + 1]).then_inc(dmax, 1)

            def difference(h, i):
                cols = slice(PCOL[i], PCOL[i] + P * (i + 1))
                rc = RC[:, h % 2, 2 * i:2 * i + 2]
                dve.wait_ge(dexp, 2 * (NB * h + i) + 2)
                then(dve.reciprocal(rc, SU[:, h % 2, 2 * i:2 * i + 2]))
                dve.tensor_scalar(P0[:, h % 2, cols], P0[:, h % 2, cols], rc[:, 0:1], None, ALU.mult)
                then(dve.tensor_scalar(S1[:, 0:1], rc[:, 1:2], NEGLAM, None, ALU.mult))
                dve.scalar_tensor_tensor(P0[:, h % 2, cols], PB[:, cols], S1[:, 0:1], P0[:, h % 2, cols],
                                         ALU.mult, ALU.add).then_inc(dw_made, 1)

            for what, n in MIX2_ORDER:
                if what == "lam":
                    dve.tensor_tensor(LP[0:64, :], par(C_LAM, 2, 0, 64), par(C_LAM + 2, 2, 0, 64), ALU.mult)\
                       .then_inc(lam_prod, 1)
                    dve.wait_ge(lam_exp, 1)
                    dve.scalar_tensor_tensor(NEGLAM, LE[:, 1:2], -LAMBDA_INIT, LE[:, 0:1],
                                             ALU.add, ALU.subtract).then_inc(lam_made, 1)
                    dve.tensor_scalar(par(C_DFG), par(C_DFG), 1.0 - LAMBDA_INIT, None, ALU.mult)\
                       .then_inc(lam_made, 1)
                    dve.wait_ge(rcol_mm, 2)
                    dve.tensor_copy(RCOL, PS[3][:, 0:NB]).then_inc(rcol_made, 1)
                    dve.wait_ge(lam_made, 2)
                elif what == "ba":
                    evacuate(G_BA, U_BA, BR[0:36, :], 36)
                    rows()
                    then(dve.memset(CB[:, :, 0:3], 0.0))
                elif what == "kqv":
                    evacuate(G_KQV + n, U_KQV + n, CB[:, n % 2, 3:T + 3])
                    dve.wait_ge(cv_a, n + 1)
                    for j in (2, 1, 0):
                        tap = dve.scalar_tensor_tensor(tile_of(n), CB[:, n % 2, j:T + j], par(C_DCW + 4 * n + j),
                                                       tile_of(n), ALU.mult, ALU.add)
                        if j:
                            then(tap)
                    tap.then_inc(cv_v, 1)
                elif what == "cols":
                    dve.wait_ge(cols_mm, 1)
                    dve.tensor_copy(COLS, PS[4][:, :].rearrange("p (b q r) -> p b q r", b=NB, q=4)[:, :, :, 0:4])\
                       .then_inc(cols_made, 1)
                elif what == "l2":
                    dve.wait_ge(l2_rt, n + 1)
                    then(dve.reciprocal(NR2[:, n % 2, :], NR2[:, n % 2, :]))
                    dve.tensor_tensor(tile_of(n), tile_of(n), NR2[:, n % 2, :], ALU.mult).then_inc(l2_made, 1)
                elif what == "dfqk":
                    evacuate(G_DFQK + n, U_DFQK + n, (DQ if n % 2 == 0 else DK)[:, n // 2, :])
                    if n >= 1:
                        normalise_qk(n - 1)
                elif what == "T":
                    block_inputs(n)
                elif what == "Y":
                    masked_y(*n)
                elif what == "Z":
                    next_inverse(*n)
                elif what == "A":
                    if n == 0:
                        normalise_qk(7)
                        dve.memset(ST[:, :, :], 0.0).then_inc(st_made, 1)
                    for i in range(NB):
                        masked_max(n, i, 0)
                        masked_max(n, i, 1)
                        if i:
                            difference(n, i - 1)
                    difference(n, NB - 1)
                elif what == "scan":
                    b, r = n // 2, 64 * (n % 2)
                    dve.wait_ge(uw_made, 8)
                    dve.wait_ge(ws_mm, n + 1)
                    new = VT[r:r + 64, :, P * b:P * (b + 1)]
                    dve.tensor_tensor(new, new, heads(PS[6][r:r + 64, :]), ALU.subtract).then_inc(vn_made, 1)
                    dve.wait_ge(kv_mm, n + 1)
                    dve.wait_ge(st_made, n + 1)
                    for h in range(4):
                        last = dve.scalar_tensor_tensor(ST[:, h, :], ST[:, h, :],
                                                        EG[:, h, CH * (n + 1) - 1:CH * (n + 1)],
                                                        PS[7][:, P * h:P * (h + 1)], ALU.mult, ALU.add)
                    last.then_inc(st_made, 1)
                elif what == "z":
                    evacuate(G_Z + n, U_Z + n, ZT[:, n, :])
                elif what == "out":
                    o = (QT, DQ)[n // 4][:, n % 4, :]
                    dve.wait_ge(o_rt, n + 1)
                    then(dve.reciprocal(NRO[:, n, :], NRO[:, n, :]))
                    then(dve.scalar_tensor_tensor(o, o, par(C_DNG if n < 4 else C_DFG), NRO[:, n, :],
                                                  ALU.mult, ALU.mult))
                    dve.wait_ge(silu_z, n + 1)
                    dve.tensor_tensor(o, o, ZT[:, n, :], ALU.mult).then_inc(o_made, 1)
                    if n:
                        low((QT, DQ)[(n - 1) // 4][:, (n - 1) % 4, :], n - 1, 4)
                    if n == 7:
                        dve.wait_ge(o_made, 8)
                        low(o, 7, 4)
            for m in range(KC):
                dve.wait_ge(unit_done, U_WO2 + m + 1)
                dve.tensor_tensor(X[:, m, :], X[:, m, :], bank_of(G_WO2 + m)[:, :], ALU.add).then_inc(gemm_freed, 1)


def _constants():
    con = np.zeros((P, NCON), np.float32)
    i = np.arange(P)
    con[:, K_ID:K_ID + P] = i[:, None] == i[None, :]
    con[:, K_ONE:K_ONE + P] = 1.0
    con[:, K_HALF:K_HALF + P] = i[:, None] // HD == i[None, :] // HD
    con[:, K_CAUSAL + 384:K_CAUSAL + 512] = np.where(i[None, :] <= i[:, None], 0.0, NEG)
    same = i[:, None] // CH == i[None, :] // CH
    con[:, K_GNEG:K_GNEG + P] = np.where(same & (i[:, None] <= i[None, :]), 0.0, NEG)
    for l in range(LEVELS):
        pair = i[:, None] >> (l + 1) == i[None, :] >> (l + 1)
        con[:, K_LV + P * l:K_LV + P * (l + 1)] = pair & ((i[:, None] >> l & 1) == 1) & ((i[None, :] >> l & 1) == 0)
    return con


def _tiles(w):
    k, n = w.shape
    return w.reshape(k // P, P, n // P, P).transpose(2, 1, 0, 3).reshape(n // P, P, 1024)


def _moving(w):
    return w.reshape(4, 2, P, 512).transpose(0, 2, 1, 3).reshape(4, P, 1024)


def _padded(parts):
    out = np.zeros((D, P), np.float32)
    for at, w in parts:
        out[:, at:at + w.shape[1]] = w
    return _tiles(out)


def _stream(i):
    w_in, w_in2 = i["w_in"][0], i["w_in_2"][0]
    u, va, q, k, vb = (w_in[:, 512 * n:512 * (n + 1)] for n in range(5))
    dq, dk, dv, dz = (w_in2[:, 512 * n:512 * (n + 1)] for n in range(4))
    fq, fk, fv, fz = (w_in2[:, 2056 + 512 * n:2056 + 512 * (n + 1)] for n in range(4))
    qk = np.stack([_tiles(q), _tiles(k)], 1).reshape(8, P, 1024)
    fqk = np.stack([_tiles(fq), _tiles(fk)], 1).reshape(8, P, 1024)
    up = i["w_up"][0]
    up = np.stack([_tiles(up[:, :FF]), _tiles(up[:, FF:])], 1).reshape(2 * NFF, P, 1024)
    down = i["w_down"][0].reshape(NFF, P, KC, P).transpose(2, 0, 1, 3)
    down = down.reshape(NFF, 8, P, P).transpose(0, 2, 1, 3).reshape(NFF, P, 1024)
    units = [_moving(vb), _moving(va), _padded([(0, w_in[:, 2560:2568])]), qk, _tiles(u), _tiles(i["w_out"][0]),
             up, down, _padded([(0, w_in2[:, 2052:2056]), (32, w_in2[:, 2048:2052])]),
             _tiles(dk), _tiles(dq), _tiles(dv), _moving(fv), fqk, _tiles(dz), _tiles(fz), _tiles(i["w_out_2"][0])]
    s = np.concatenate(units)
    assert s.shape[0] == UNITS
    return np.ascontiguousarray(s.reshape(UNITS // 2, 2, P, 1024).transpose(0, 2, 1, 3).reshape(UNITS // 2, P, 2048))


def _parameters(i):
    p = np.zeros((P, NPAR), np.float32)

    def columns(at, v):
        v = v.reshape(-1, P).T
        p[:, at:at + v.shape[1]] = v

    columns(C_GMIX, i["norm_mix_g"])
    columns(C_GFFN, i["norm_ffn_g"])
    columns(C_GFIN, i["norm_final_g"])
    columns(C_GN2, i["norm_gain_2"])
    columns(C_SGG, i["sg_ln_g"])
    taps = i["w_conv"][0].reshape(3, 2, NFF, P).transpose(3, 2, 1, 0)
    p[:, C_FCW:C_FCW + 6 * NFF] = taps.reshape(P, -1)
    p[:, C_FCB:C_FCB + 2 * NFF] = i["b_conv"][0].reshape(2, NFF, P).transpose(2, 1, 0).reshape(P, -1)
    taps = i["conv_w_2"][0].reshape(4, 3, 4, P)[:, [1, 0, 2]]
    p[:, C_DCW:C_DCW + 48] = taps.transpose(3, 1, 2, 0).reshape(P, -1)
    p[0:8, C_FB] = i["f_bias"][0]
    p[0:4, C_ALOG] = i["a_log_2"][0]
    p[0:4, C_DTB] = i["dt_bias_2"][0]
    p[:, C_DNG] = i["dn_out_gain_2"][0]
    for c, name in ((C_QG, "q_gain_2"), (C_KG, "k_gain_2")):
        p[0:64, c] = p[64:128, c] = i[name][0]
    p[:, C_DFG] = i["df_out_gain_2"][0]
    for n, name in enumerate(("lambda_q1_2", "lambda_q2_2", "lambda_k1_2", "lambda_k2_2")):
        p[0:64, C_LAM + n] = i[name][0]
    return p


def kernel(**inputs):
    import concourse.bacc as bacc
    from concourse.bass_utils import run_bass_kernel_spmd

    i = {name: np.asarray(v) for name, v in inputs.items()}
    arrays = {
        "x_t": np.ascontiguousarray(i["x"][0].T),
        "wstream": _stream(i),
        "params": _parameters(i),
        "consts": _constants(),
        "sgw_t": np.ascontiguousarray(i["sg_w"][0].transpose(2, 0, 1)),
        "sgb": np.ascontiguousarray(i["sg_b"][0].reshape(4, 2, P)),
    }
    nc = bacc.Bacc("TRN2", target_bir_lowering=False, num_devices=1)
    args = [nc.dram_tensor(name, a.shape, F32, kind="ExternalInput").ap() for name, a in arrays.items()]
    args.append(nc.dram_tensor("out_t", (D, T), F32, kind="ExternalOutput").ap())
    build(nc, *args)
    r = run_bass_kernel_spmd(nc, [arrays], core_ids=[0])
    return np.ascontiguousarray(r.results[0]["out_t"].T)[None]
```

```python
from contextlib import ExitStack

import numpy as np

import concourse.bass as bass
from concourse import mybir

F32 = mybir.dt.float32
F32R = mybir.dt.float32r
ALU = mybir.AluOpType
ACT = mybir.ActivationFunctionType
AX_X = mybir.AxisListType.X

P = 128
T = 512
D = 1024
KC = D // P
NB = T // P
HD = 64
CH = 64
FF = 2816
NFF = FF // P
EPS = 1e-6
NEG = -1e30
LEVELS = 6
LAMBDA_INIT = 0.2

U_VB = 0
U_VA = 4
U_F = 8
U_QK = 9
U_UA = 17
U_WO = 21
U_UP = 29
U_DN = U_UP + 2 * NFF
U_BA = U_DN + NFF
U_KQV = U_BA + 1
U_DFV = U_KQV + 12
U_DFQK = U_DFV + 4
U_Z = U_DFQK + 8
U_WO2 = U_Z + 8
UNITS = U_WO2 + 8
RING = 4

G_F = 0
G_QK = 1
G_UA = 9
G_WO = 13
G_UP = 21
G_DN = G_UP + 2 * NFF
G_BA = G_DN + KC
G_KQV = G_BA + 1
G_DFQK = G_KQV + 12
G_Z = G_DFQK + 8
G_WO2 = G_Z + 8

_at = 0


def _cols(n):
    global _at
    _at += n
    return _at - n


C_GMIX, C_GFFN, C_GFIN, C_GN2 = (_cols(KC) for _ in range(4))
C_SGG = _cols(4)
C_FCW = _cols(2 * NFF * 3)
C_FCB = _cols(2 * NFF)
C_DCW = _cols(12 * 4)
C_FB, C_ALOG, C_DTB, C_DNG, C_QG, C_KG, C_DFG = (_cols(1) for _ in range(7))
C_LAM = _cols(4)
NPAR = _at

K_ID, K_ONE, K_HALF, K_CAUSAL, K_GNEG, K_LV = 0, 128, 256, 384, 896, 1024
NCON = K_LV + 128 * LEVELS

MIX1_ORDER = [
    ("qk", 0), ("qk", 1), ("A", 0), ("qk", 2), ("qk", 3),
    ("A", 1), ("qk", 4), ("B", 0), ("qk", 5), ("C", 0),
    ("A", 2), ("qk", 6), ("B", 1), ("qk", 7), ("C", 1),
    ("A", 3), ("u", 0), ("B", 2), ("u", 1), ("C", 2),
    ("A", 4), ("u", 2), ("B", 3), ("u", 3), ("C", 3), ("gelu", 0),
    ("A", 5), ("gate", 0), ("B", 4), ("gate", 1), ("C", 4),
    ("A", 6), ("gate", 2), ("B", 5), ("gate", 3), ("C", 5),
    ("split", 0), ("split", 1), ("split", 2), ("split", 3),
    ("A", 7), ("split", 4), ("B", 6), ("split", 5), ("split", 6), ("C", 6), ("wo", 0), ("B", 7), ("wo", 1), ("C", 7),
    ("split", 7),
]


def _prepare(b, fills):
    groups = [[(what, b), (what, b + 1)] for what in ("T1", "T2")]
    groups += [[(what, (b, l)), (what, (b + 1, l))] for l in range(LEVELS) for what in ("Y", "Z", "X") if l or what != "Z"]
    return _spread(groups + [[("W", b), ("W", b + 1)]], fills)


def _quarters(what, units):
    return [(what, (n, part)) for n in units for part in range(4)]


def _merge(a, b):
    return _spread([[x] for x in a], b) if len(a) >= len(b) else _spread([[x] for x in b], a)


def _scans(steps):
    return [(what, i) for i in steps for what in ("sa", "sb")]


def _attention(fills):
    groups = []
    for n in range(19):
        if n >= 6 and (n - 6) % 4 == 0:
            groups.append([("C", (n - 6) // 4)])
        if n < 16:
            groups.append([("A", n)])
        if 1 <= n < 17:
            groups.append([("D", n - 1)])
        if 2 <= n < 18:
            groups.append([("B", n - 2)])
    return _spread(groups, fills)


def _gating():
    order = [("os", t) for t in range(4)] + [("or", 0), ("os", 4), ("or", 1)]
    for t in range(4):
        order += [("og", t), ("ol", t)]
    order += [("os", 5), ("og", 4), ("ol", 4), ("or", 2), ("og", 5), ("ol", 5)]
    return order


def step(b, l):
    return (b // 2) * 2 * LEVELS + 2 * l + b % 2


def _spread(groups, fills):
    order, used = [], 0
    for n, group in enumerate(groups):
        order += group
        upto = len(fills) * (n + 1) // len(groups)
        order += fills[used:upto]
        used = upto
    return order


def _projections():
    order = [("ba", 0)]
    for t in range(12):
        if t in (6, 10):
            order.append(("l2r", t // 4 - 1))
        order.append(("kqv", t))
        if t == 0:
            order.append(("lam", 0))
        if 1 <= t <= 3:
            order.append(("rows", t - 1))
        if 1 <= t <= 4:
            order.append(("x2", t - 1))
        if t == 5:
            order.append(("cols", 0))
        if 2 <= t <= 9:
            order.append(("l2s", t - 2))
        if t >= 7:
            order.append(("l2b", t - 7))
    return order + _spread([[("l2b", 5)], [("l2b", 6)], [("l2b", 7)]], [("dfv", n) for n in range(4)])


MIX2_ORDER = (
    _projections()
    + _prepare(0, [("dfv", n) for n in range(4, 8)] + _quarters("dfqk", range(0, 4)))
    + _prepare(2, _merge(_quarters("dfqk", range(4, 9)) + _quarters("z", range(0, 1)), _scans(range(4))))
    + [("zs", 0)]
    + _attention(_merge(_scans(range(4, 8)), _quarters("z", range(1, 8))) + [("zs", 1)] + _gating())
    + [("os", 6), ("or", 3), ("os", 7), ("og", 6), ("ol", 6), ("or", 4), ("w2", 0), ("w2", 1), ("og", 7), ("ol", 7)]
)
Z_EARLY = 1
PCOL = [P * i * (i + 1) // 2 for i in range(NB)]
PALL = P * NB * (NB + 1) // 2


def build(nc, x_t, wstream, params, consts, sgw_t, sgb, out_t):
    with ExitStack() as ctx:
        here = [16512]

        def place(name, shape, dt, at=None):
            size = 4 * int(np.prod(shape[1:]))
            if at is None:
                at = here[0]
                here[0] += (size + 31) // 32 * 32
            return nc.alloc_sbuf_tensor_at(name, shape, dt, offset=at)

        def sem(name):
            return ctx.enter_context(nc.semaphore(name))

        X_AT = here[0]
        X = place("X", [P, KC, T], F32)
        GH = place("GH", [P, KC, T], F32R)
        GL = place("GL", [P, KC, T], F32R)
        RAW = place("RAW", [P, RING, 1024], F32)
        HI = place("HI", [P, RING, 1024], F32R)
        LO = place("LO", [P, RING, 1024], F32R)
        CON = place("CON", [P, NCON], F32)
        PAR = place("PAR", [P, NPAR], F32)
        RB = place("RB", [P, T], F32)
        SM = place("SM", [P, 320], F32)
        arena = here[0]
        KB = 1024

        MT = place("MT", [P, 8, T], F32, arena)
        KT1 = place("KT1", [P, 4, T], F32, arena + 16 * KB)
        VB = place("VB", [P, NB, 512], F32, arena + 24 * KB)
        P1 = place("P1", [P, 2, PALL], F32, arena + 32 * KB)
        PT1 = place("PT1", [P, NB, T], F32, arena + 42 * KB)
        NCB = place("NCB", [P, 2, T], F32, arena + 50 * KB)
        NCD = place("NCD", [P, 2, T], F32, arena + 54 * KB)
        FR = place("FR", [P, 3, T], F32, arena + 58 * KB)
        SGW = place("SGW", [P, 8, P], F32, arena + 64 * KB)
        SGB = place("SGB", [P, 4, P], F32, arena + 68 * KB)
        VA = place("VA", [P, NB, 512], F32, arena + 70 * KB)
        SQV = place("SQV", [P, NB, 512], F32, arena + 78 * KB)
        MH = place("MH", [P, KC, T], F32R, arena + 64 * KB)
        ML = place("ML", [P, KC, T], F32R, arena + 80 * KB)
        AH = place("AH", [P, NFF, T], F32R, arena)
        AL = place("AL", [P, NFF, T], F32R, arena + 44 * KB)
        AB = place("AB", [P, 2, T + 2], F32, arena + 88 * KB)
        YC = place("YC", [P, 2, T], F32, arena + 88 * KB + 4128)
        SQ = place("SQ", [P, 2, T], F32, arena + 96 * KB + 96)
        ACC = SQ[:, 1, :]
        assert arena + 100 * KB + 96 <= 229368, arena
        SQB, ACCB = YC[:, 0, :], YC[:, 1, :]
        KT = place("KT", [P, 4, T], F32, arena)
        QT = place("QT", [P, 4, T], F32, arena + 8 * KB)
        VT = place("VT", [P, 4, T], F32, arena + 16 * KB)
        EG = place("EG", [P, 4, T], F32, arena + 24 * KB)
        AQK = place("AQK", [P, NB, 4, P], F32, arena + 32 * KB)
        KDEC = place("KDEC", [P, NB, 4, P], F32, arena + 40 * KB)
        TR = arena + 48 * KB
        NT = place("NT", [P, 2, 4, P], F32, TR)
        XI = place("XI", [P, 2, 4, P], F32, TR + 4 * KB)
        XT = place("XT", [P, 2, 4, P], F32, TR + 8 * KB)
        YM = place("YM", [P, 2, 4, P], F32, TR + 12 * KB)
        KBE = place("KBE", [P, 2, 4, P], F32, TR + 16 * KB)
        VBT = place("VBT", [P, 2, 4, P], F32, TR + 20 * KB)
        CB = place("CB", [P, 2, T + 4], F32, TR)
        R1 = place("R1", [P, T], F32, TR + 5 * KB)
        R2 = place("R2", [P, T], F32, TR + 7 * KB)
        R3 = place("R3", [P, T], F32, TR + 9 * KB)
        BR = place("BR", [P, T], F32, TR + 11 * KB)
        SQ2 = place("SQ2", [P, 2, T], F32, TR + 13 * KB)
        P0 = place("P0", [P, NB, T], F32, TR)
        PB = place("PB", [P, 2, T], F32, TR + 8 * KB)
        PT2 = place("PT2", [P, NB, T], F32, TR + 12 * KB)
        SQO = place("SQO", [P, 2, T], F32, TR + 20 * KB)
        DQ = place("DQ", [P, 4, T], F32, arena + 72 * KB)
        DK = place("DK", [P, 4, T], F32, arena + 80 * KB)
        DV = place("DV", [P, NB, 512], F32, arena + 88 * KB)
        RS = place("RS", [P, T], F32, arena + 96 * KB)
        ST = place("ST", [P, 4, P], F32, arena + 98 * KB)
        ZT = place("ZT", [P, 8, T], F32, X_AT)
        QNW = place("QNW", [P, T], F32, X_AT + 12 * KB)
        SQD = place("SQD", [P, T], F32, X_AT + 14 * KB)

        PS = [ctx.enter_context(nc.psum_tensor(f"bank{b}", [P, 512], F32)) for b in range(8)]

        EPSC = SM[:, 0:4]
        RCOL = SM[:, 4:8]
        MX = SM[:, 8:24].rearrange("p (a b) -> p a b", a=2)
        SU = SM[:, 24:40].rearrange("p (a b) -> p a b", a=2)
        RC = SM[:, 40:56].rearrange("p (a b) -> p a b", a=2)
        LP, LE, NEGLAM = SM[:, 56:58], SM[:, 58:60], SM[:, 60:61]
        EA = SM[:, 61:62]
        S1 = SM[:, 62:64]
        LNS, LNV = SM[:, 64:96], SM[:, 96:128]
        COLS = SM[:, 128:192].rearrange("p (b q h) -> p b q h", b=NB, q=4)
        MXA = SM[:, 192:200]
        R1C, SS2C = SM[:, 272:276], SM[:, 276:280]
        GG = SM[:, 280:288]
        L2C = SM[:, 200:232].rearrange("p (t b) -> p t b", b=NB)
        OC = SM[:, 232:264].rearrange("p (t b) -> p t b", b=NB)
        QNC = SM[:, 264:272].rearrange("p (b h) -> p b h", h=2)

        IDENT, ONES, HALF = (CON[:, c:c + P] for c in (K_ID, K_ONE, K_HALF))
        CAUSAL = CON[:, K_CAUSAL:K_CAUSAL + 512]
        GNEG = CON[:, K_GNEG:K_GNEG + P]

        def level_mask(l):
            return CON[:, K_LV + P * l:K_LV + P * (l + 1)]

        def par(c, n=1, p0=0, p1=P):
            return PAR[p0:p1, c:c + n]

        def heads(ap):
            return ap.rearrange("p (h c) -> p h c", h=4)

        x_landed = [sem(f"x_landed{k}") for k in range(KC)]
        par_landed, con_landed, masks_landed = sem("par_landed"), sem("con_landed"), sem("masks_landed")
        sg_landed = sem("sg_landed")
        w_landed = [sem("w_landed0"), sem("w_landed1")]
        hi_made, unit_split, unit_done = sem("hi_made"), sem("unit_split"), sem("unit_done")
        stored, x_spilled = sem("stored"), sem("x_spilled")
        x_back = [sem(f"x_back{k}") for k in range(KC)]
        sq_made, sq_added, ss_made = sem("sq_made"), sem("sq_added"), sem("ss_made")
        sqb_made, sqb_added, gg_made = sem("sqb_made"), sem("sqb_added"), sem("gg_made")
        r1_root, r1_made, r1_mm, ms_made = sem("r1_root"), sem("r1_made"), sem("r1_mm"), sem("ms_made")
        mh_made, ml_made = sem("mh_made"), sem("ml_made")
        rms_made, rcol_made, rb_mm, rb_ready = sem("rms_made"), sem("rcol_made"), sem("rb_mm"), sem("rb_ready")
        gh_made, gl_made, x_updated = sem("gh_made"), sem("gl_made"), sem("x_updated")
        gemm_freed = sem("gemm_freed")
        v_chain, a_chain = sem("v_chain"), sem("a_chain")
        eps_made = sem("eps_made")
        vb_freed, va_freed = sem("vb_freed"), sem("va_freed")
        ln_centered, ln_squared, ln_summed, ln_root, vn_ready = (
            sem(n) for n in ("ln_centered", "ln_squared", "ln_summed", "ln_root", "vn_ready"))
        sgw_masked = sem("sgw_masked")
        f_made, f_log, negc_ready = sem("f_made"), sem("f_log"), sem("negc_ready")
        gelu_made = sem("gelu_made")
        ncb_mm, ncb_made = sem("ncb_mm"), sem("ncb_made")
        s_made, max_made, exp_made, p_ready = (sem(n) for n in ("s_made", "max_made", "exp_made", "p_ready"))
        pt_mm, pt_freed, pv_made, attended = (sem(n) for n in ("pt_mm", "pt_freed", "pv_made", "attended"))
        gate_mm, gated = sem("gate_mm"), sem("gated")
        conv_started, conv_made = sem("conv_started"), sem("conv_made")
        silu_ff, ff_made, ah_made, al_made = (sem(n) for n in ("silu_ff", "ff_made", "ah_made", "al_made"))
        down_done = sem("down_done")
        lam_prod, lam_mm, lam_exp, lam_made = (sem(n) for n in ("lam_prod", "lam_mm", "lam_exp", "lam_made"))
        ba_v, ba_a, rows_ready = sem("ba_v"), sem("ba_a"), sem("rows_ready")
        cb_zero = sem("cb_zero")
        cv_a, cv_v, cv_s = sem("cv_a"), sem("cv_v"), sem("cv_s")
        cols_mm, cols_made, gcb_mm, gcb_made = (sem(n) for n in ("cols_mm", "cols_made", "gcb_mm", "gcb_made"))
        dfv_freed = sem("dfv_freed")
        l2_sq, l2_mm, l2_rt, l2_rc, l2_bc, l2_made = (
            sem(n) for n in ("l2_sq", "l2_mm", "l2_rt", "l2_rc", "l2_bc", "l2_made"))
        qn_sq, qn_mm, qn_rt, qn_rc, qn_wide, qn_bc, qn_made = (
            sem(n) for n in ("qn_sq", "qn_mm", "qn_rt", "qn_rc", "qn_wide", "qn_bc", "qn_made"))
        tk_mm, tv_mm, g_mm, aq_mm = (sem(n) for n in ("tk_mm", "tv_mm", "g_mm", "aq_mm"))
        d_made, d_exp, eg_made, kd_made, vbt_made, nt_made, qe_made = (
            sem(n) for n in ("d_made", "d_exp", "eg_made", "kd_made", "vbt_made", "nt_made", "qe_made"))
        y_mm, ym_made, z_mm, xi_made, xt_mm, xt_made = (
            sem(n) for n in ("y_mm", "ym_made", "z_mm", "xi_made", "xt_mm", "xt_made"))
        u_mm, w_mm, uw_made = sem("u_mm"), sem("w_mm"), sem("uw_made")
        st_made, ws_mm, vn_made, ot_mm, kv_mm, od_made = (
            sem(n) for n in ("st_made", "ws_mm", "vn_made", "ot_mm", "kv_mm", "od_made"))
        ds_mm, dmax, dexp, dw_made = (sem(n) for n in ("ds_mm", "dmax", "dexp", "dw_made"))
        dpt_mm, dpt_freed, dpv_mm, dpv_freed = (sem(n) for n in ("dpt_mm", "dpt_freed", "dpv_mm", "dpv_freed"))
        silu_z = sem("silu_z")
        o_sq, o_mm, o_rt, o_rc, o_bc, o_made = (sem(n) for n in ("o_sq", "o_mm", "o_rt", "o_rc", "o_bc", "o_made"))

        def bank_of(g):
            return PS[g % 2]

        block = ctx.enter_context(nc.Block())

        @block.sync
        def _(sp):
            def load(pair, slot):
                sp.dma_start(RAW[:, 2 * slot:2 * slot + 2, :],
                             wstream[pair].rearrange("p (a n) -> p a n", a=2)).then_inc(w_landed[slot], 16)

            def load_x(k):
                sp.dma_start(X[:, k, :], x_t[P * k:P * (k + 1), :]).then_inc(x_landed[k], 16)

            load_x(0)
            load(0, 0)
            for k in range(1, 4):
                load_x(k)
            load(1, 1)
            for k in range(4, KC):
                load_x(k)
            with sp.Fori(1, UNITS // 4) as i:
                for s in range(2):
                    sp.wait_ge(unit_split, 4 * i + (2 * s - 2))
                    sp.dma_start(RAW[:, 2 * s:2 * s + 2, :],
                                 wstream[bass.ds(2 * i + s, 1)].rearrange("o p (a n) -> p (o a) n", a=2))\
                      .then_inc(w_landed[s], 16)
            for m in range(KC):
                sp.wait_ge(gemm_freed, G_WO2 + m + 1)
                sp.dma_start(out_t[P * m:P * (m + 1), :], X[:, m, :]).then_inc(stored, 16)
            sp.wait_ge(stored, 16 * KC)

        @block.gpsimd
        def _(pool):
            def split(slot, done, unit):
                pool.wait_ge(w_landed[slot // 2], done)
                pool.tensor_tensor(HI[:, slot, :].rearrange("p (a n) -> p a n", n=P),
                                   RAW[:, slot, :].rearrange("p (a n) -> p a n", n=P),
                                   ONES.unsqueeze(1).to_broadcast([P, KC, P]), ALU.mult).then_inc(hi_made, 1)
                pool.wait_ge(hi_made, unit + 1)
                pool.tensor_tensor(LO[:, slot, :], RAW[:, slot, :], HI[:, slot, :].bitcast(F32),
                                   ALU.subtract).then_inc(unit_split, 1)

            pool.wait_ge(con_landed, 16)
            for s in range(RING):
                split(s, 16, s)
            with pool.Fori(1, UNITS // 4) as i:
                for s in range(RING):
                    pool.wait_ge(unit_done, 4 * i + (s - RING + 1))
                    split(s, 16 * i + 16, 4 * i + s)

        @block.tensor
        def _(pe):
            def three(out, w, x, k, first, last, flip=False):
                (wh, wl), (xh, xl) = w, x
                for n, (a, b) in enumerate(((wh, xh), (wh, xl), (wl, xh))):
                    if flip:
                        a, b = b, a
                    mm = pe.matmul(out, a, b, start=(first and n == 0), stop=(last and n == 2))
                return mm

            def ring(u, blk, n=P):
                s = u % RING
                return HI[:, s, n * blk:n * (blk + 1)], LO[:, s, n * blk:n * (blk + 1)]

            def product(u, g, made, m0, high=GH, low=GL, ks=range(KC)):
                pe.wait_ge(unit_split, u + 1)
                if g >= 2:
                    pe.wait_ge(gemm_freed, g - 1)
                for k in ks:
                    pe.wait_ge(made, m0 + k + 1)
                    mm = three(bank_of(g)[:, :], ring(u, k), (high[:, k, :], low[:, k, :]), k, k == 0, k == KC - 1)
                if k == KC - 1:
                    mm.then_inc(unit_done, 1)

            def product_tokens(u0, banks, m0, kks=range(KC)):
                for k in kks:
                    u = u0 + k // 2
                    pe.wait_ge(unit_split, u + 1)
                    pe.wait_ge(gl_made, m0 + k + 1)
                    for b in range(NB):
                        mm = three(PS[banks[b]][:, :], ring(u, k % 2, 512),
                                   (GH[:, k, P * b:P * (b + 1)], GL[:, k, P * b:P * (b + 1)]),
                                   k, k == 0, k == KC - 1, flip=True)
                    if k % 2 == 1:
                        mm.then_inc(unit_done, 1)

            def token_sums(out, src, groups=ONES[:, 0:1]):
                n = groups.shape[1]
                for b in range(NB):
                    mm = pe.matmul(out[:, n * b:n * (b + 1)], src[:, P * b:P * (b + 1)], groups, start=True, stop=True)
                return mm

            def over_rows(out, column):
                for b in range(NB):
                    mm = pe.matmul(out[:, P * b:P * (b + 1)], column(b), IDENT, start=True, stop=True)
                return mm

            def sum_squares(n):
                pe.wait_ge(sq_added, KC * (n + 1))
                token_sums(PS[7], ACC).then_inc(ss_made, 1)

            def spread_rms(n):
                pe.wait_ge(rcol_made, n + 1)
                over_rows(PS[7], lambda b: RCOL[:, b:b + 1].to_broadcast([P, P])).then_inc(rb_mm, 1)

            pe.wait_ge(con_landed, 16)

            product_tokens(U_VB, (2, 3, 4, 5), 0)
            sum_squares(0)
            pe.wait_ge(rms_made, 1)
            spread_rms(0)
            pe.wait_ge(rb_ready, 1)
            product_tokens(U_VA, (6, 7, 0, 1), 0)
            pe.wait_ge(va_freed, 4)
            product(U_F, G_F, gl_made, 0)

            def scores(h):
                pe.wait_ge(negc_ready, 1)
                if h >= 1:
                    pe.wait_ge(ncb_made, h)
                pe.matmul(PS[7][:, :], IDENT[0:8, h:h + 1].to_broadcast([8, P]), FR[0:8, 2, :],
                          start=True, stop=True).then_inc(ncb_mm, 1)
                pe.wait_ge(gemm_freed, G_QK + 2 * (h // 2) + 2)
                pe.wait_ge(vb_freed, 4)
                r = 64 * (h % 2)
                for i in range(NB):
                    s = NB * h + i
                    if s >= 2:
                        pe.wait_ge(exp_made, s - 1)
                    pe.matmul(PS[2 + s % 2][:, 0:P * (i + 1)], MT[r:r + 64, 4 + h // 2, P * i:P * (i + 1)],
                              KT1[r:r + 64, h // 2, 0:P * (i + 1)], start=True, stop=True).then_inc(s_made, 1)

            def turn(h):
                for i in range(NB):
                    n = NB * h + i
                    pe.wait_ge(p_ready, n + 1)
                    if n >= 2:
                        pe.wait_ge(pt_freed, n - 1)
                    for j in range(i + 1):
                        mm = pe.transpose(PS[4 + n % 2][:, P * j:P * (j + 1)],
                                          P1[:, h % 2, PCOL[i] + P * j:PCOL[i] + P * (j + 1)], IDENT)
                    mm.then_inc(pt_mm, 1)

            def attend(h):
                pe.wait_ge(pt_freed, NB * (h + 1))
                if h % 2 == 0 and h >= 2:
                    pe.wait_ge(attended, h // 2)
                r = 64 * (h % 2)
                for j in range(NB):
                    mm = pe.matmul(PS[6][r:r + 64, P * j:T], VB[:, j, 64 * h:64 * (h + 1)], PT1[:, j, P * j:T],
                                   start=(j == 0), stop=(j == NB - 1))
                mm.then_inc(pv_made, 1)

            def gate(p):
                pe.wait_ge(vn_ready, 1)
                pe.wait_ge(sgw_masked, 1)
                pe.wait_ge(gemm_freed, G_WO)
                if p >= 2:
                    pe.wait_ge(gated, p - 1)
                for b in range(NB):
                    for e in range(2):
                        hh = 2 * p + e
                        mm = pe.matmul(PS[p % 2][64 * e:64 * e + 64, P * b:P * (b + 1)],
                                       VA[:, b, 64 * hh:64 * (hh + 1)], SGW[:, hh, :], start=True, stop=True)
                mm.then_inc(gate_mm, 1)

            for what, n in MIX1_ORDER:
                if what == "qk":
                    product(U_QK + n, G_QK + n, gl_made, 0)
                elif what == "u":
                    product(U_UA + n, G_UA + n, gl_made, 0)
                elif what == "A":
                    scores(n)
                elif what == "B":
                    turn(n)
                elif what == "C":
                    attend(n)
                elif what == "gate":
                    gate(n)
                elif what == "wo":
                    pe.wait_ge(gated, 4)
                    product(U_WO + n, G_WO + n, ml_made, 0, MH, ML, range(KC - 1))
            for m in range(KC):
                product(U_WO + m, G_WO + m, ml_made, 0, MH, ML, range(KC - 1 if m < 2 else 0, KC))

            product(U_UP, G_UP, gl_made, KC)
            sum_squares(1)
            product(U_UP + 1, G_UP + 1, gl_made, KC)
            spread_rms(1)
            for q in (2, 3):
                product(U_UP + q, G_UP + q, gl_made, KC)
            with pe.Fori(1, NFF // 2) as i:
                for q in range(4):
                    u, g = U_UP + q, G_UP + q
                    pe.wait_ge(unit_split, 4 * i + (u + 1))
                    pe.wait_ge(gemm_freed, 4 * i + (g - 1))
                    for k in range(KC):
                        mm = three(bank_of(g)[:, :], ring(u, k), (GH[:, k, :], GL[:, k, :]), k, k == 0, k == KC - 1)
                    mm.then_inc(unit_done, 1)
            for m in range(KC):
                pe.wait_ge(gemm_freed, G_DN + m - 1)
                for c in range(NFF):
                    n = NFF * m + c
                    u = U_DN + n // 8
                    if n % 8 == 0:
                        pe.wait_ge(unit_split, u + 1)
                    if m == 0:
                        pe.wait_ge(al_made, c + 1)
                    mm = three(bank_of(G_DN + m)[:, :], ring(u, n % 8), (AH[:, c, :], AL[:, c, :]), c, c == 0, c == NFF - 1)
                    if n % 8 == 7:
                        mm.then_inc(unit_done, 1)
                    elif c == NFF - 1:
                        mm.then_inc(down_done, 1)


            def lam():
                pe.wait_ge(lam_prod, 1)
                pe.matmul(PS[2][:, 0:2], ONES[0:64, :], LP[0:64, :], start=True, stop=True).then_inc(lam_mm, 1)

            def rows_to_columns():
                pe.wait_ge(rows_ready, 1)
                for b in range(NB):
                    mm = pe.transpose(PS[4][:, P * b:P * (b + 1)], RS[:, P * b:P * (b + 1)], IDENT)
                mm.then_inc(cols_mm, 1)
                pe.wait_ge(x_updated, KC)
                pe.wait_ge(rb_ready, 3)
                for h in range(4):
                    pe.matmul(PS[(2, 3, 6, 7)[h]][:, :], IDENT[0:4, h:h + 1].to_broadcast([4, P]), RS[0:4, :],
                              start=True, stop=True).then_inc(gcb_mm, 1)

            def head_sums(t):
                pe.wait_ge(l2_sq, t + 1)
                if t == 4:
                    pe.wait_ge(l2_rt, 1)
                token_sums(PS[5][:, NB * t:NB * (t + 1)], SQ2[:, t % 2, :]).then_inc(l2_mm, 1)

            def spread_norm(t):
                pe.wait_ge(l2_rc, t // 4 + 1)
                if t >= 2:
                    pe.wait_ge(l2_made, t - 1)
                else:
                    pe.wait_ge(gcb_made, 4)
                over_rows(PS[2 + t % 2], lambda b: L2C[:, t, b:b + 1].to_broadcast([P, P])).then_inc(l2_bc, 1)

            def qk_sums(n):
                pe.wait_ge(qn_sq, n + 1)
                token_sums(bank_of(G_DFQK + n), SQD, HALF[:, 0:P:HD]).then_inc(qn_mm, 1)

            def spread_qk(n):
                pe.wait_ge(qn_wide, n + 1)
                over_rows(bank_of(G_DFQK + n), lambda b: QNW[:, P * b:P * (b + 1)]).then_inc(qn_bc, 1)

            def blk(b):
                return slice(P * b, P * (b + 1))

            def banks_for(b):
                return (PS[2 + 2 * (b % 2)], PS[3 + 2 * (b % 2)])

            def block_products(b):
                A, B = banks_for(b)
                if b < 2:
                    pe.wait_ge(l2_made, 8)
                    pe.wait_ge(cols_made, 1)
                else:
                    pe.wait_ge(uw_made, 2 * (b - 1))
                for h in range(4):
                    mm = pe.matmul(A[:, blk(h)], KT[:, h, blk(b)], KT[:, h, blk(b)], start=True, stop=True)
                mm.then_inc(g_mm, 1)
                for h in range(4):
                    mm = pe.matmul(B[:, blk(h)], KT[:, h, blk(b)], QT[:, h, blk(b)], start=True, stop=True)
                mm.then_inc(aq_mm, 1)

            def token_major(b):
                A, B = banks_for(b)
                pe.wait_ge(cv_s, 12)
                pe.wait_ge(nt_made, b + 1)
                for h in range(4):
                    mm = pe.transpose(A[:, blk(h)], KT[:, h, blk(b)], IDENT)
                mm.then_inc(tk_mm, 1)
                for h in range(4):
                    mm = pe.transpose(B[:, blk(h)], VT[:, h, blk(b)], IDENT)
                mm.then_inc(tv_mm, 1)

            def inverse_y(b, l):
                A = banks_for(b)[0]
                s = b % 2
                if l == 0:
                    pe.wait_ge(kd_made, b + 1)
                else:
                    pe.wait_ge(xi_made, step(b, l - 1) + 1)
                for h in range(4):
                    rhs = IDENT if l == 0 else XI[:, s, h, :]
                    mm = pe.matmul(A[:, blk(h)], NT[:, s, h, :], rhs, start=True, stop=True)
                mm.then_inc(y_mm, 1)

            def inverse_z(b, l):
                s = b % 2
                pe.wait_ge(ym_made, step(b, l) + 1)
                pe.wait_ge(xt_made, step(b, l - 1) + 1)
                for h in range(4):
                    mm = pe.matmul(banks_for(b)[1][:, blk(h)], XT[:, s, h, :], YM[:, s, h, :], start=True, stop=True)
                mm.then_inc(z_mm, 1)

            def inverse_x(b, l):
                pe.wait_ge(xi_made, step(b, l) + 1)
                if l == 0:
                    pe.wait_ge(vbt_made, b + 1)
                for h in range(4):
                    mm = pe.transpose(banks_for(b)[1][:, blk(h)], XI[:, b % 2, h, :], IDENT)
                mm.then_inc(xt_mm, 1)

            def solve(b):
                A, B = banks_for(b)
                s = b % 2
                pe.wait_ge(xt_made, step(b, LEVELS - 1) + 1)
                pe.wait_ge(vbt_made, b + 1)
                for h in range(4):
                    mm = pe.matmul(A[:, blk(h)], XT[:, s, h, :], VBT[:, s, h, :], start=True, stop=True)
                mm.then_inc(u_mm, 1)
                for h in range(4):
                    mm = pe.matmul(B[:, blk(h)], KBE[:, s, h, :], XT[:, s, h, :], start=True, stop=True)
                mm.then_inc(w_mm, 1)

            def scan_state(i):
                b, r = i // 2, 64 * (i % 2)
                pe.wait_ge(st_made, i + 1)
                pe.wait_ge(uw_made, 2 * (b + 1))
                if i >= 1:
                    pe.wait_ge(od_made, i)
                else:
                    pe.wait_ge(dfv_freed, 2)
                for h in range(4):
                    mm = pe.matmul(PS[6][r:r + 64, blk(h)], KT[:, h, P * b + r:P * b + r + 64], ST[:, h, :],
                                   start=True, stop=True)
                mm.then_inc(ws_mm, 1)

            def scan_output(i):
                b, r = i // 2, 64 * (i % 2)
                pe.wait_ge(vn_made, i + 1)
                pe.wait_ge(qe_made, b + 1)
                for h in range(4):
                    o = PS[6][:, 64 * h:64 * h + 64]
                    pe.matmul(o, ST[:, h, :], QT[:, h, CH * i:CH * (i + 1)], start=True, stop=False)
                    mm = pe.matmul(o, VT[:, h, blk(b)], AQK[:, b, h, r:r + 64], start=False, stop=True)
                mm.then_inc(ot_mm, 1)
                for h in range(4):
                    mm = pe.matmul(PS[7][:, blk(h)], KDEC[r:r + 64, b, h, :], VT[r:r + 64, h, blk(b)],
                                   start=True, stop=True)
                mm.then_inc(kv_mm, 1)

            def df_scores(n):
                h, i = n // NB, n % NB
                pe.wait_ge(qn_made, 8)
                pe.wait_ge(uw_made, 8)
                for c in range(2):
                    if n:
                        pe.wait_ge(dexp, 2 * n + c - 1)
                    pe.matmul(PS[2 + c][:, 0:P * (i + 1)], DQ[64 * c:64 * c + 64, h, blk(i)],
                              DK[64 * c:64 * c + 64, h, 0:P * (i + 1)], start=True, stop=True)\
                      .then_inc(ds_mm, 1)

            def df_turn(n):
                pe.wait_ge(dw_made, n + 1)
                if n >= 1:
                    pe.wait_ge(dpt_freed, n)
                for j in range(n % NB + 1):
                    mm = pe.transpose(PS[4][:, blk(j)], P0[:, n % NB, blk(j)], IDENT)
                mm.then_inc(dpt_mm, 1)

            def df_attend(h):
                pe.wait_ge(dpt_freed, NB * (h + 1))
                if h >= 1:
                    pe.wait_ge(dpv_freed, h)
                for j in range(NB):
                    mm = pe.matmul(PS[5][:, P * j:T], DV[:, j, blk(h)], PT2[:, j, P * j:T],
                                   start=(j == 0), stop=(j == NB - 1))
                mm.then_inc(dpv_mm, 1)

            def out_sums(t):
                pe.wait_ge(o_sq, t + 1)
                if t == 0:
                    pe.wait_ge(st_made, 9)
                elif t >= 4:
                    pe.wait_ge(o_rt, t - 3)
                token_sums(PS[7][:, NB * t:NB * (t + 1)], SQO[:, t % 2, :]).then_inc(o_mm, 1)

            def spread_out(t):
                pe.wait_ge(o_rc, max(t - 2, 1))
                if t:
                    pe.wait_ge(o_made, t)
                over_rows(PS[6], lambda b: OC[:, t, b:b + 1].to_broadcast([P, P])).then_inc(o_bc, 1)

            for what, n in MIX2_ORDER:
                if what == "lam":
                    lam()
                elif what == "ba":
                    product(U_BA, G_BA, gl_made, 2 * KC)
                    sum_squares(2)
                    pe.wait_ge(sqb_added, KC)
                    token_sums(PS[7][:, NB:2 * NB], ACCB).then_inc(ss_made, 1)
                elif what == "kqv":
                    product(U_KQV + n, G_KQV + n, gl_made, 2 * KC)
                    if n == 0:
                        spread_rms(2)
                        pe.wait_ge(r1_made, 1)
                        over_rows(PS[6], lambda b: R1C[:, b:b + 1].to_broadcast([P, P])).then_inc(r1_mm, 1)
                elif what == "cols":
                    rows_to_columns()
                elif what == "dfv":
                    if n == 0:
                        pe.wait_ge(gemm_freed, G_DFQK)
                        pe.wait_ge(gcb_made, 4)
                    product_tokens(U_DFV, (6, 7, 0, 1), 2 * KC, (n,))
                elif what == "l2s":
                    head_sums(n)
                elif what == "l2b":
                    spread_norm(n)
                elif what == "dfqk":
                    n, part = n
                    if n < 8:
                        if n < 2:
                            pe.wait_ge(dfv_freed, 4)
                        else:
                            pe.wait_ge(qn_made, n - 1)
                        product(U_DFQK + n, G_DFQK + n, gl_made, 2 * KC, ks=range(2 * part, 2 * part + 2))
                    if n >= 1 and part == 1:
                        qk_sums(n - 1)
                    if n >= 1 and part == 3:
                        spread_qk(n - 1)
                elif what == "T1":
                    block_products(n)
                elif what == "T2":
                    token_major(n)
                elif what == "Y":
                    inverse_y(*n)
                elif what == "Z":
                    inverse_z(*n)
                elif what == "X":
                    inverse_x(*n)
                elif what == "W":
                    solve(n)
                elif what == "sa":
                    scan_state(n)
                elif what == "sb":
                    scan_output(n)
                elif what == "A":
                    df_scores(n)
                elif what == "B":
                    df_turn(n)
                elif what == "C":
                    df_attend(n)
                elif what == "z":
                    n, part = n
                    if n == 0:
                        pe.wait_ge(qn_made, 8)
                    product(U_Z + n, G_Z + n, gl_made, 2 * KC, ks=range(2 * part, 2 * part + 2))
                elif what == "os":
                    out_sums(n)
                elif what == "og":
                    spread_out(n)
                elif what == "w2":
                    product(U_WO2 + n, G_WO2 + n, gl_made, 3 * KC, ks=range(KC - 1))
            for m in range(KC):
                product(U_WO2 + m, G_WO2 + m, gl_made, 3 * KC, ks=range(KC - 1 if m < 2 else 0, KC))

        @block.scalar
        def _(act):
            act.dma_start(PAR[:, :], params).then_inc(par_landed, 16)
            act.dma_start(CON[:, 0:K_CAUSAL], consts[:, 0:K_CAUSAL]).then_inc(con_landed, 16)
            act.wait_ge(par_landed, 16)
            act.wait_ge(eps_made, 4)

            def square_tile(n, k):
                if KC * n + k >= 1:
                    act.wait_ge(sq_added, KC * n + k)
                act.activation(SQ[:, 0, :], X[:, k, :], ACT.Square).then_inc(sq_made, 1)

            def root(n):
                act.wait_ge(ss_made, n + 1)
                act.activation(RCOL, PS[7][:, 0:NB], ACT.Sqrt, scale=1.0 / D, bias=EPSC[:, 0:1])\
                   .then_inc(rms_made, 1)
                act.wait_ge(rb_mm, n + 1)
                act.activation(RB[:, :], PS[7][:, :], ACT.Copy).then_inc(rb_ready, 1)

            def high(src, k, gain=None):
                act.activation(GH[:, k, :], src, ACT.Copy, scale=1.0 if gain is None else gain)\
                   .then_inc(gh_made, 1)

            for k in range(KC):
                act.wait_ge(x_landed[k], 16)
                high(X[:, k, :], k, par(C_GMIX + k))
                square_tile(0, k)
            act.dma_start(CON[:, K_CAUSAL:NCON], consts[:, K_CAUSAL:NCON]).then_inc(masks_landed, 16)
            act.dma_start(SGW[:, :, :], sgw_t).then_inc(sg_landed, 16)
            for e in range(2):
                act.dma_start(SGB[64 * e:64 * e + 64, :, :],
                              sgb[:, e, :].unsqueeze(0).to_broadcast([64, 4, P])).then_inc(sg_landed, 16)
            root(0)
            act.wait_ge(rcol_made, 1)
            act.wait_ge(unit_done, U_VB + 4)
            for b in range(NB):
                act.activation(VB[:, b, :], PS[2 + b][:, :], ACT.Copy, scale=RCOL[:, b:b + 1]).then_inc(vb_freed, 1)
            act.wait_ge(unit_done, U_VA + 4)
            for b, bank in enumerate((6, 7, 0, 1)):
                act.activation(VA[:, b, :], PS[bank][:, :], ACT.Gelu, scale=RCOL[:, b:b + 1]).then_inc(va_freed, 1)
            act.wait_ge(ln_centered, 1)
            act.activation(SQV[:, :, :], VA[:, :, :], ACT.Square).then_inc(ln_squared, 1)
            act.wait_ge(ln_summed, 1)
            act.activation(LNV, LNV, ACT.Sqrt, scale=1.0 / HD, bias=EPSC[:, 0:1]).then_inc(ln_root, 1)
            act.wait_ge(f_made, 1)
            act.activation(FR[0:8, 1, :], FR[0:8, 0, :], ACT.Abs).then_inc(f_log, 1)
            act.wait_ge(f_log, 1)
            act.activation(FR[0:8, 1, :], FR[0:8, 1, :], ACT.Exp, scale=-1.0).then_inc(f_log, 1)
            act.wait_ge(f_log, 2)
            act.activation(FR[0:8, 1, :], FR[0:8, 1, :], ACT.Ln, bias=EPSC[0:8, 3:4]).then_inc(f_log, 1)

            for what, h in MIX1_ORDER:
                if what == "A":
                    act.wait_ge(ncb_mm, h + 1)
                    if h >= 2:
                        act.wait_ge(max_made, NB * (h - 1))
                    act.activation(NCB[:, h % 2, :], PS[7][:, :], ACT.Copy).then_inc(ncb_made, 1)
                    for i in range(NB):
                        s = NB * h + i
                        w = P * (i + 1)
                        act.wait_ge(max_made, s + 1)
                        if h >= 2:
                            act.wait_ge(pt_mm, NB * (h - 2) + i + 1)
                        act.activation(P1[:, h % 2, PCOL[i]:PCOL[i] + w], PS[2 + s % 2][:, 0:w], ACT.Exp,
                                       scale=-1.0, bias=MX[:, h % 2, i:i + 1], accum_out=SU[:, h % 2, i:i + 1])\
                           .then_inc(exp_made, 1)
                elif what == "B":
                    if h >= 1:
                        act.wait_ge(pv_made, h)
                    for i in range(NB):
                        n = NB * h + i
                        act.wait_ge(pt_mm, n + 1)
                        act.activation(PT1[:, 0:i + 1, P * i:P * (i + 1)],
                                       PS[4 + n % 2][:, 0:P * (i + 1)].rearrange("p (j c) -> p j c", c=P),
                                       ACT.Copy).then_inc(pt_freed, 1)
                elif what == "gelu":
                    for p in range(4):
                        act.wait_ge(gemm_freed, G_UA + p + 1)
                        act.activation(MT[:, p, :], MT[:, p, :], ACT.Gelu).then_inc(gelu_made, 1)
                elif what == "split":
                    if h < 4:
                        act.wait_ge(gated, 4)
                    else:
                        act.wait_ge(attended, h - 3)
                    act.activation(MH[:, h, :], MT[:, h, :], ACT.Copy).then_inc(mh_made, 1)
            for m in range(KC):
                act.wait_ge(gemm_freed, G_WO + m + 1)
                high(X[:, m, :], m, par(C_GFFN + m))
                square_tile(1, m)

            root(1)

            def feed_forward(t):
                for gv in range(2):
                    act.wait_ge(gemm_freed, 2 * t + (G_UP + gv + 1))
                    act.activation(YC[:, gv, :], AB[:, gv, 2:T + 2], ACT.Identity,
                                   scale=PAR[:, bass.ds(6 * t + (C_FCW + 3 * gv + 2), 1)],
                                   bias=PAR[:, bass.ds(2 * t + (C_FCB + gv), 1)]).then_inc(conv_started, 1)
                act.wait_ge(conv_made, 2 * t + 1)
                act.activation(YC[:, 0, :], YC[:, 0, :], ACT.Silu).then_inc(silu_ff, 1)
                act.wait_ge(ff_made, t + 1)
                act.activation(AH[:, bass.ds(t, 1), :], YC[:, 0:1, :], ACT.Copy).then_inc(ah_made, 1)

            feed_forward(0)
            with act.Fori(1, NFF) as t:
                act.wait_ge(al_made, t)
                feed_forward(t)
            act.wait_ge(gg_made, 1)
            act.wait_ge(al_made, NFF)
            for m in range(KC):
                act.wait_ge(gemm_freed, G_DN + m + 1)
                high(X[:, m, :], m, GG[:, m:m + 1])
                square_tile(2, m)
                if m:
                    act.wait_ge(sqb_added, m)
                act.activation(SQB, X[:, m, :], ACT.Square, scale=par(C_GFIN + m)).then_inc(sqb_made, 1)
            act.wait_ge(ss_made, 4)
            act.activation(R1C, PS[7][:, 0:NB], ACT.Sqrt, scale=1.0 / D, bias=EPSC[:, 0:1]).then_inc(r1_root, 1)
            act.wait_ge(ms_made, 1)
            act.activation(RCOL, SS2C, ACT.Sqrt, scale=1.0 / D, bias=EPSC[:, 0:1]).then_inc(rms_made, 1)
            act.wait_ge(rb_mm, 3)
            act.activation(RB[:, :], PS[7][:, :], ACT.Copy).then_inc(rb_ready, 1)

            def rows(stage):
                if stage == 0:
                    act.activation(EA[0:4, :], par(C_ALOG, 1, 0, 4), ACT.Exp).then_inc(ba_a, 1)
                    act.wait_ge(ba_v, 1)
                    act.activation(R2[0:4, :], R1[0:4, :], ACT.Abs).then_inc(ba_a, 1)
                    act.wait_ge(ba_a, 2)
                    act.activation(R2[0:4, :], R2[0:4, :], ACT.Exp, scale=-1.0).then_inc(ba_a, 1)
                    act.wait_ge(ba_a, 3)
                    act.activation(R2[0:4, :], R2[0:4, :], ACT.Ln, bias=EPSC[0:4, 3:4]).then_inc(ba_a, 1)
                    act.activation(R3[32:36, :], BR[32:36, :], ACT.Exp, scale=-1.0).then_inc(ba_a, 1)
                elif stage == 1:
                    act.wait_ge(ba_v, 3)
                    act.activation(R3[32:36, :], RS[0:4, :], ACT.Exp).then_inc(ba_a, 1)
                    act.activation(RS[96:100, :], R1[0:4, :], ACT.Exp).then_inc(ba_a, 1)

            def tile_of(t):
                return (KT, QT, VT)[t // 4][:, t % 4, :]

            for what, n in MIX2_ORDER:
                if what == "lam":
                    act.wait_ge(lam_mm, 1)
                    act.activation(LE, PS[2][:, 0:2], ACT.Exp).then_inc(lam_exp, 1)
                elif what == "rows":
                    rows(n)
                elif what == "kqv":
                    act.wait_ge(gemm_freed, G_KQV + n + 1)
                    act.activation(tile_of(n), CB[:, n % 2, 3:T + 3], ACT.Copy,
                                   scale=par(C_DCW + 4 * n + 3)).then_inc(cv_a, 1)
                    act.wait_ge(cv_v, n + 1)
                    act.activation(tile_of(n), tile_of(n), ACT.Silu).then_inc(cv_s, 1)
                    if n < 8:
                        act.wait_ge(cv_s, n + 1)
                        if n >= 2:
                            act.wait_ge(l2_mm, n - 1)
                        act.activation(SQ2[:, n % 2, :], tile_of(n), ACT.Square).then_inc(l2_sq, 1)
                elif what == "cols":
                    for h in range(4):
                        act.wait_ge(gcb_mm, h + 1)
                        act.activation(EG[:, h, :], PS[(2, 3, 6, 7)[h]][:, :], ACT.Copy).then_inc(gcb_made, 1)
                elif what == "x2":
                    for k in (2 * n, 2 * n + 1):
                        act.wait_ge(x_updated, k + 1)
                        act.dma_start(out_t[P * k:P * (k + 1), :], X[:, k, :]).then_inc(x_spilled, 16)
                elif what == "dfv" and n == KC - 1:
                    act.wait_ge(rcol_made, 3)
                    act.wait_ge(unit_done, U_DFV + 4)
                    for b, bank in enumerate((6, 7, 0, 1)):
                        act.activation(DV[:, b, :], PS[bank][:, :], ACT.Copy, scale=RCOL[:, b:b + 1])\
                           .then_inc(dfv_freed, 1)
                elif what == "l2r":
                    act.wait_ge(l2_mm, 4 * n + 4)
                    act.activation(L2C[:, 4 * n:4 * n + 4, :],
                                   PS[5][:, 16 * n:16 * n + 16].rearrange("p (t b) -> p t b", b=NB), ACT.Sqrt,
                                   scale=1.0 if n == 0 else 128.0,
                                   bias=EPSC[:, 0:1] if n == 0 else EPSC[:, 1:2]).then_inc(l2_rt, 1)
                elif what == "dfqk":
                    m, part = n[0] - 1, n[1]
                    if m < 0:
                        continue
                    if part == 0:
                        tile = (DQ if m % 2 == 0 else DK)[:, m // 2, :]
                        act.wait_ge(gemm_freed, G_DFQK + m + 1)
                        if m >= 1:
                            act.wait_ge(qn_mm, m)
                        else:
                            act.wait_ge(x_spilled, 16 * KC)
                        act.activation(SQD[:, :], tile, ACT.Square).then_inc(qn_sq, 1)
                    elif part == 2:
                        act.wait_ge(qn_mm, m + 1)
                        if m >= 1:
                            act.wait_ge(qn_wide, m)
                        act.activation(QNC, bank_of(G_DFQK + m)[:, 0:8].rearrange("p (b h) -> p b h", h=2), ACT.Sqrt,
                                       scale=1.0 if m % 2 == 0 else 1.0 / HD,
                                       bias=EPSC[:, 2:3] if m % 2 == 0 else EPSC[:, 0:1]).then_inc(qn_rt, 1)
                    elif part == 3:
                        act.wait_ge(qn_rc, m + 1)
                        if m >= 1:
                            act.wait_ge(qn_bc, m)
                        act.activation(QNW[:, :].rearrange("p (b h c) -> p b h c", h=2, c=HD),
                                       QNC.unsqueeze(3).to_broadcast([P, NB, 2, HD]), ACT.Copy).then_inc(qn_wide, 1)
                elif what == "T1":
                    act.wait_ge(d_made, n + 1)
                    act.activation(NT[:, n % 2, :, :], NT[:, n % 2, :, :], ACT.Exp).then_inc(d_exp, 1)
                    act.activation(EG[:, :, P * n:P * (n + 1)], EG[:, :, P * n:P * (n + 1)], ACT.Exp)\
                       .then_inc(eg_made, 1)
                elif what == "X":
                    b, l = n
                    act.wait_ge(xt_mm, step(b, l) + 1)
                    act.activation(XT[:, b % 2, :, :], heads(PS[3 + 2 * (b % 2)][:, :]), ACT.Copy)\
                       .then_inc(xt_made, 1)
                elif what == "W":
                    act.wait_ge(u_mm, n + 1)
                    act.activation(VT[:, :, P * n:P * (n + 1)], heads(PS[2 + 2 * (n % 2)][:, :]), ACT.Copy)\
                       .then_inc(uw_made, 1)
                    act.wait_ge(w_mm, n + 1)
                    act.activation(KT[:, :, P * n:P * (n + 1)], heads(PS[3 + 2 * (n % 2)][:, :]), ACT.Copy)\
                       .then_inc(uw_made, 1)
                elif what == "sb":
                    act.wait_ge(ot_mm, n + 1)
                    act.activation(QT[:, :, CH * n:CH * (n + 1)],
                                   PS[6][:, 0:4 * CH].rearrange("p (h c) -> p h c", h=4), ACT.Copy)\
                       .then_inc(od_made, 1)
                elif what == "A":
                    h, i = n // NB, n % NB
                    w = P * (i + 1)
                    if n >= 4:
                        act.wait_ge(dpt_mm, n - 3)
                    if n >= 2:
                        act.wait_ge(dw_made, n - 1)
                    for c in range(2):
                        act.wait_ge(dmax, 2 * n + c + 1)
                        act.activation(P0[:, i, 0:w] if c == 0 else PB[:, n % 2, 0:w], PS[2 + c][:, 0:w], ACT.Exp,
                                       scale=-1.0, bias=MX[:, h % 2, 2 * i + c:2 * i + c + 1],
                                       accum_out=SU[:, h % 2, 2 * i + c:2 * i + c + 1]).then_inc(dexp, 1)
                elif what == "B":
                    h, i = n // NB, n % NB
                    if i == 0 and h:
                        act.wait_ge(dpv_mm, h)
                    act.wait_ge(dpt_mm, n + 1)
                    act.activation(PT2[:, 0:i + 1, P * i:P * (i + 1)],
                                   PS[4][:, 0:P * (i + 1)].rearrange("p (j c) -> p j c", c=P),
                                   ACT.Copy).then_inc(dpt_freed, 1)
                elif what == "C":
                    act.wait_ge(dpv_mm, n + 1)
                    act.activation(DQ[:, n, :], PS[5][:, :], ACT.Copy).then_inc(dpv_freed, 1)
                elif what == "zs":
                    for t in (range(Z_EARLY), range(Z_EARLY, 8))[n]:
                        act.wait_ge(gemm_freed, G_Z + t + 1)
                        act.activation(ZT[:, t, :], ZT[:, t, :], ACT.Silu).then_inc(silu_z, 1)
                elif what == "os":
                    if n < 4:
                        act.wait_ge(od_made, 8)
                    else:
                        act.wait_ge(dpv_freed, n - 3)
                    if n >= 2:
                        act.wait_ge(o_mm, n - 1)
                    act.activation(SQO[:, n % 2, :], (QT, DQ)[n // 4][:, n % 4, :], ACT.Square).then_inc(o_sq, 1)
                elif what == "or":
                    tiles = slice(0, 4) if n == 0 else slice(n + 3, n + 4)
                    act.wait_ge(o_mm, tiles.stop)
                    act.activation(OC[:, tiles, :], PS[7][:, NB * tiles.start:NB * tiles.stop]
                                   .rearrange("p (t b) -> p t b", b=NB), ACT.Sqrt,
                                   scale=1.0 / P, bias=EPSC[:, 0:1]).then_inc(o_rt, 1)
                elif what == "og":
                    act.wait_ge(unit_done, U_WO2)
                    act.wait_ge(o_made, n + 1)
                    high((QT, DQ)[n // 4][:, n % 4, :], n)
                    act.dma_start(X[:, n, :], out_t[P * n:P * (n + 1), :]).then_inc(x_back[n], 16)

        @block.vector
        def _(dve):
            chain = [0]

            def then(ins):
                chain[0] += 1
                ins.then_inc(v_chain, 1)
                dve.wait_ge(v_chain, chain[0])

            for c, v in enumerate((EPS, 128 * EPS, 64 * EPS, 1.0)):
                dve.memset(EPSC[:, c:c + 1], v).then_inc(eps_made, 1)
            dve.wait_ge(par_landed, 16)
            dve.wait_ge(con_landed, 16)

            def low(src, k, n, gain=None):
                dve.wait_ge(gh_made, KC * n + k + 1)
                if gain is None:
                    dve.tensor_tensor(GL[:, k, :], src, GH[:, k, :].bitcast(F32), ALU.subtract).then_inc(gl_made, 1)
                else:
                    dve.scalar_tensor_tensor(GL[:, k, :], src, gain, GH[:, k, :].bitcast(F32),
                                             ALU.mult, ALU.subtract).then_inc(gl_made, 1)

            def add_square(n, k):
                dve.wait_ge(sq_made, KC * n + k + 1)
                if k == 0:
                    if n:
                        dve.wait_ge(ss_made, n)
                    dve.tensor_copy(ACC, SQ[:, 0, :]).then_inc(sq_added, 1)
                else:
                    dve.wait_ge(sq_added, KC * n + k)
                    dve.tensor_tensor(ACC, ACC, SQ[:, 0, :], ALU.add).then_inc(sq_added, 1)

            def invert_rms(n):
                dve.wait_ge(rms_made, n + 1)
                dve.reciprocal(RCOL, RCOL).then_inc(rcol_made, 1)
                dve.wait_ge(rb_ready, n + 1)

            def evacuate(g, unit, out, rows=P):
                dve.wait_ge(unit_done, unit + 1)
                dve.tensor_tensor(out, bank_of(g)[0:rows, :], RB[0:rows, :], ALU.mult).then_inc(gemm_freed, 1)
                dve.wait_ge(gemm_freed, g + 1)

            for k in range(KC):
                low(X[:, k, :], k, 0, par(C_GMIX + k))
                add_square(0, k)
            invert_rms(0)
            dve.wait_ge(masks_landed, 16)
            dve.wait_ge(sg_landed, 48)
            dve.memset(SGW[64:128, :, 0:64], 0.0).then_inc(sgw_masked, 1)

            groups = VA[:, :, :].rearrange("p b (h d) -> p (b h) d", d=HD)

            def over_group(col):
                return col.unsqueeze(2).to_broadcast([P, 32, HD])

            dve.wait_ge(va_freed, 4)
            then(dve.tensor_reduce(LNS, groups, AX_X, ALU.add))
            then(dve.tensor_scalar(LNS, LNS, 1.0 / HD, None, ALU.mult))
            dve.tensor_tensor(groups, groups, over_group(LNS), ALU.subtract).then_inc(ln_centered, 1)
            evacuate(G_F, U_F, FR[0:8, 0, :], 8)
            dve.tensor_scalar(FR[0:8, 0, :], FR[0:8, 0, :], par(C_FB, 1, 0, 8), None, ALU.add).then_inc(f_made, 1)
            dve.wait_ge(ln_squared, 1)
            dve.tensor_reduce(LNV, SQV[:, :, :].rearrange("p b (h d) -> p (b h) d", d=HD), AX_X, ALU.add)\
               .then_inc(ln_summed, 1)
            dve.wait_ge(f_log, 3)
            then(dve.tensor_scalar(FR[0:8, 0, :], FR[0:8, 0, :], -1.0, 0.0, ALU.mult, ALU.max))
            dve.tensor_tensor_scan(FR[0:8, 2, :], FR[0:8, 0, :], FR[0:8, 1, :], 0.0, ALU.add, ALU.add)\
               .then_inc(negc_ready, 1)
            dve.wait_ge(ln_root, 1)
            then(dve.reciprocal(LNV, LNV))
            dve.wait_ge(ln_centered, 1)
            dve.tensor_tensor(groups, groups, over_group(LNV), ALU.mult).then_inc(vn_ready, 1)

            def biased_max(h, i):
                s = NB * h + i
                S = PS[2 + s % 2]
                e = h % 2
                dve.wait_ge(s_made, s + 1)
                first = 3e38
                if i:
                    then(dve.tensor_tensor_reduce(S[:, 0:P * i], S[:, 0:P * i], NCB[:, e, 0:P * i], -1.0, 3e38,
                                                  ALU.add, ALU.min, MXA[:, 4 * e + i:4 * e + i + 1]))
                    first = MXA[:, 4 * e + i:4 * e + i + 1]
                dve.tensor_tensor_reduce(S[:, P * i:P * (i + 1)], S[:, P * i:P * (i + 1)],
                                         NCD[:, e, P * i:P * (i + 1)], -1.0, first,
                                         ALU.add, ALU.min, MX[:, e, i:i + 1]).then_inc(max_made, 1)

            def normalise(h, i):
                e = h % 2
                p = P1[:, e, PCOL[i]:PCOL[i] + P * (i + 1)]
                dve.wait_ge(exp_made, NB * h + i + 1)
                then(dve.reciprocal(RC[:, e, i:i + 1], SU[:, e, i:i + 1]))
                dve.tensor_scalar(p, p, RC[:, e, i:i + 1], None, ALU.mult).then_inc(p_ready, 1)

            for what, n in MIX1_ORDER:
                if what == "qk":
                    g = G_QK + n
                    p = n // 2
                    if n % 2 == 0:
                        dve.wait_ge(unit_done, U_QK + n + 1)
                        dve.scalar_tensor_tensor(MT[:, 4 + p, :], bank_of(g)[:, :], HD ** -0.5, RB[:, :],
                                                 ALU.mult, ALU.mult).then_inc(gemm_freed, 1)
                    else:
                        dve.wait_ge(unit_done, U_QK + n + 1)
                        dve.tensor_tensor(KT1[:, p, :], bank_of(g)[:, :], RB[:, :], ALU.mult)\
                           .then_inc(gemm_freed, 1)
                    dve.wait_ge(gemm_freed, g + 1)
                elif what == "u":
                    evacuate(G_UA + n, U_UA + n, MT[:, n, :])
                elif what == "A":
                    dve.wait_ge(ncb_made, n + 1)
                    then(dve.tensor_tensor(heads(NCD[:, n % 2, :]), heads(NCB[:, n % 2, :]),
                                           CAUSAL[:, 384:512].unsqueeze(1).to_broadcast([P, 4, P]), ALU.add))
                    biased_max(n, 0)
                    for i in range(1, NB):
                        biased_max(n, i)
                        normalise(n, i - 1)
                    normalise(n, NB - 1)
                elif what == "C" and n % 2 == 1:
                    dve.wait_ge(pv_made, n + 1)
                    dve.tensor_copy(MT[:, 4 + n // 2, :], PS[6][:, :]).then_inc(attended, 1)
                elif what == "gate":
                    dve.wait_ge(gate_mm, n + 1)
                    dve.wait_ge(gelu_made, n + 1)
                    then(dve.scalar_tensor_tensor(heads(SQV[:, n, :]), heads(PS[n % 2][:, :]), par(C_SGG + n),
                                                  SGB[:, n, :].unsqueeze(1).to_broadcast([P, 4, P]),
                                                  ALU.mult, ALU.add))
                    dve.tensor_tensor(MT[:, n, :], MT[:, n, :], SQV[:, n, :], ALU.mult).then_inc(gated, 1)
                elif what == "split":
                    dve.wait_ge(mh_made, n + 1)
                    dve.tensor_tensor(ML[:, n, :], MT[:, n, :], MH[:, n, :].bitcast(F32), ALU.subtract)\
                       .then_inc(ml_made, 1)
            for m in range(KC):
                dve.wait_ge(unit_done, U_WO + m + 1)
                dve.tensor_tensor(X[:, m, :], X[:, m, :], bank_of(G_WO + m)[:, :], ALU.add).then_inc(gemm_freed, 1)
                dve.wait_ge(gemm_freed, G_WO + m + 1)
                low(X[:, m, :], m, 1, par(C_GFFN + m))
                add_square(1, m)
            invert_rms(1)
            then(dve.memset(AB[:, :, 0:2], 0.0))
            c0 = chain[0]
            with dve.Fori(0, NFF) as t:
                for gv in range(2):
                    dve.wait_ge(unit_done, 2 * t + (U_UP + gv + 1))
                    dve.tensor_tensor(AB[:, gv, 2:T + 2], bank_of(G_UP + gv)[:, :], RB[:, :], ALU.mult)\
                       .then_inc(gemm_freed, 1)
                for gv in range(2):
                    dve.wait_ge(gemm_freed, 2 * t + (G_UP + gv + 1))
                    dve.wait_ge(conv_started, 2 * t + (gv + 1))
                    dve.scalar_tensor_tensor(YC[:, gv, :], AB[:, gv, 1:T + 1],
                                             PAR[:, bass.ds(6 * t + (C_FCW + 3 * gv + 1), 1)], YC[:, gv, :],
                                             ALU.mult, ALU.add).then_inc(v_chain, 1)
                    dve.wait_ge(v_chain, 2 * t + (c0 + gv + 1))
                    dve.scalar_tensor_tensor(YC[:, gv, :], AB[:, gv, 0:T],
                                             PAR[:, bass.ds(6 * t + (C_FCW + 3 * gv), 1)], YC[:, gv, :],
                                             ALU.mult, ALU.add).then_inc(conv_made, 1)
                dve.wait_ge(silu_ff, t + 1)
                dve.wait_ge(conv_made, 2 * t + 2)
                dve.tensor_tensor(YC[:, 0, :], YC[:, 0, :], YC[:, 1, :], ALU.mult).then_inc(ff_made, 1)
                dve.wait_ge(ff_made, t + 1)
                dve.wait_ge(ah_made, t + 1)
                dve.tensor_tensor(AL[:, bass.ds(t, 1), :], YC[:, 0:1, :], AH[:, bass.ds(t, 1), :].bitcast(F32),
                                  ALU.subtract).then_inc(al_made, 1)
            chain[0] += 2 * NFF
            dve.tensor_tensor(GG, par(C_GFIN, KC), par(C_GN2, KC), ALU.mult).then_inc(gg_made, 1)
            dve.wait_ge(gg_made, 1)

            for m in range(KC):
                if m in (3, 7):
                    dve.wait_ge(unit_done, U_DN + 11 * (m + 1) // 4)
                else:
                    dve.wait_ge(down_done, m + 1 - m // 4)
                dve.tensor_tensor(X[:, m, :], X[:, m, :], bank_of(G_DN + m)[:, :], ALU.add).then_inc(gemm_freed, 1)
                dve.wait_ge(gemm_freed, G_DN + m + 1)
                low(X[:, m, :], m, 2, GG[:, m:m + 1])
                add_square(2, m)
                dve.wait_ge(sqb_made, m + 1)
                if m == 0:
                    dve.tensor_copy(ACCB, SQB).then_inc(sqb_added, 1)
                else:
                    dve.wait_ge(sqb_added, m)
                    dve.tensor_tensor(ACCB, ACCB, SQB, ALU.add).then_inc(sqb_added, 1)
            dve.wait_ge(r1_root, 1)
            dve.reciprocal(R1C, R1C).then_inc(r1_made, 1)
            dve.wait_ge(r1_made, 1)
            then(dve.tensor_tensor(SS2C, PS[7][:, NB:2 * NB], R1C, ALU.mult))
            dve.tensor_tensor(SS2C, SS2C, R1C, ALU.mult).then_inc(ms_made, 1)
            dve.wait_ge(rms_made, 3)
            then(dve.reciprocal(RCOL, RCOL))
            dve.tensor_tensor(RCOL, RCOL, R1C, ALU.mult).then_inc(rcol_made, 1)
            dve.wait_ge(rb_ready, 3)

            def rows(stage):
                if stage == 0:
                    dve.tensor_scalar(R1[0:4, :], BR[0:4, :], par(C_DTB, 1, 0, 4), None, ALU.add).then_inc(ba_v, 1)
                    then(dve.memset(RS[:, :], 0.0))
                elif stage == 1:
                    dve.wait_ge(ba_a, 4)
                    dve.wait_ge(ba_v, 1)
                    then(dve.tensor_scalar(R1[0:4, :], R1[0:4, :], 0.0, None, ALU.max))
                    then(dve.tensor_tensor(R1[0:4, :], R1[0:4, :], R2[0:4, :], ALU.add))
                    then(dve.tensor_scalar(R1[0:4, :], R1[0:4, :], EA[0:4, :], -1.0, ALU.mult, ALU.mult))
                    for c in range(T // CH):
                        last = dve.tensor_tensor_scan(RS[0:4, CH * c:CH * (c + 1)], ONES[0:4, 0:CH],
                                                      R1[0:4, CH * c:CH * (c + 1)], 0.0, ALU.mult, ALU.add)
                    then(last)
                    dve.wait_ge(ba_a, 5)
                    then(dve.tensor_scalar(R3[32:36, :], R3[32:36, :], 1.0, None, ALU.add))
                    dve.reciprocal(RS[32:36, :], R3[32:36, :]).then_inc(ba_v, 1)
                    rows_by_chunk = RS[0:4, :].rearrange("p (c n) -> p c n", n=CH)
                    dve.tensor_tensor(R1[0:4, :].rearrange("p (c n) -> p c n", n=CH),
                                      rows_by_chunk[:, :, CH - 1:CH].to_broadcast([4, T // CH, CH]),
                                      rows_by_chunk, ALU.subtract).then_inc(ba_v, 1)
                else:
                    dve.wait_ge(ba_a, 7)
                    dve.wait_ge(ba_v, 3)
                    dve.tensor_tensor(RS[64:68, :], R3[32:36, :], RS[32:36, :], ALU.mult).then_inc(rows_ready, 1)

            def tile_of(t):
                return (KT, QT, VT)[t // 4][:, t % 4, :]

            def over_head(col):
                return col.unsqueeze(2).to_broadcast([P, 4, P])

            def block_decays(b):
                s = b % 2
                A, B = (heads(PS[n + 2 * s][:, :]) for n in (2, 3))
                cols = slice(P * b, P * (b + 1))
                dve.wait_ge(gcb_made, 4)
                dve.wait_ge(cols_made, 1)
                then(dve.tensor_tensor(NT[:, s, :, :], EG[:, :, cols], over_head(COLS[:, b, 0, :]), ALU.subtract))
                dve.tensor_tensor(NT[:, s, :, :], NT[:, s, :, :], GNEG.unsqueeze(1).to_broadcast([P, 4, P]),
                                  ALU.add).then_inc(d_made, 1)
                dve.wait_ge(d_exp, b + 1)
                dve.wait_ge(aq_mm, b + 1)
                dve.tensor_tensor(AQK[:, b, :, :], B, NT[:, s, :, :], ALU.mult)
                dve.tensor_tensor(NT[:, s, :, :], A, NT[:, s, :, :], ALU.mult).then_inc(nt_made, 1)

            def block_inputs(b):
                s = b % 2
                A, B = (heads(PS[n + 2 * s][:, :]) for n in (2, 3))
                cols = slice(P * b, P * (b + 1))
                dve.wait_ge(tk_mm, b + 1)
                dve.tensor_tensor(KBE[:, s, :, :], A, over_head(COLS[:, b, 2, :]), ALU.mult)
                dve.tensor_tensor(KDEC[:, b, :, :], A, over_head(COLS[:, b, 3, :]), ALU.mult).then_inc(kd_made, 1)
                dve.wait_ge(tv_mm, b + 1)
                dve.tensor_tensor(VBT[:, s, :, :], B, over_head(COLS[:, b, 1, :]), ALU.mult).then_inc(vbt_made, 1)
                dve.wait_ge(eg_made, b + 1)
                dve.tensor_tensor(QT[:, :, cols], QT[:, :, cols], EG[:, :, cols], ALU.mult).then_inc(qe_made, 1)

            def masked_y(b, l):
                A = PS[2 + 2 * (b % 2)]
                dve.wait_ge(y_mm, step(b, l) + 1)
                for h in range(4):
                    last = dve.scalar_tensor_tensor(YM[:, b % 2, h, :], A[:, P * h:P * (h + 1)],
                                                    COLS[:, b, 1, h:h + 1], level_mask(l), ALU.mult, ALU.mult)
                last.then_inc(ym_made, 1)
                if l == 0:
                    dve.wait_ge(ym_made, step(b, l) + 1)
                    dve.tensor_tensor(XI[:, b % 2, :, :], IDENT.unsqueeze(1).to_broadcast([P, 4, P]),
                                      YM[:, b % 2, :, :], ALU.subtract).then_inc(xi_made, 1)

            def next_inverse(b, l):
                dve.wait_ge(z_mm, (b // 2) * 2 * (LEVELS - 1) + 2 * (l - 1) + b % 2 + 1)
                dve.wait_ge(xi_made, step(b, l - 1) + 1)
                dve.tensor_tensor(XI[:, b % 2, :, :], XI[:, b % 2, :, :], heads(PS[3 + 2 * (b % 2)][:, :]),
                                  ALU.subtract).then_inc(xi_made, 1)

            def normalise_qk(m):
                tile = (DQ if m % 2 == 0 else DK)[:, m // 2, :]
                dve.wait_ge(qn_bc, m + 1)
                dve.scalar_tensor_tensor(tile, tile, par(C_QG if m % 2 == 0 else C_KG), bank_of(G_DFQK + m)[:, :],
                                         ALU.mult, ALU.mult).then_inc(qn_made, 1)

            def masked_max(n, c):
                h, i = n // NB, n % NB
                w = P * (i + 1)
                dve.wait_ge(ds_mm, 2 * n + c + 1)
                dve.tensor_tensor_reduce(PS[2 + c][:, 0:w], PS[2 + c][:, 0:w], CAUSAL[:, 512 - w:512], -1.0, 3e38,
                                         ALU.add, ALU.min, MX[:, h % 2, 2 * i + c:2 * i + c + 1]).then_inc(dmax, 1)

            def difference(n):
                h, i = n // NB, n % NB
                w = P * (i + 1)
                rc = RC[:, h % 2, 2 * i:2 * i + 2]
                dve.wait_ge(dexp, 2 * n + 2)
                then(dve.reciprocal(rc, SU[:, h % 2, 2 * i:2 * i + 2]))
                dve.tensor_scalar(P0[:, i, 0:w], P0[:, i, 0:w], rc[:, 0:1], None, ALU.mult)
                then(dve.tensor_scalar(S1[:, 0:1], rc[:, 1:2], NEGLAM, None, ALU.mult))
                dve.scalar_tensor_tensor(P0[:, i, 0:w], PB[:, n % 2, 0:w], S1[:, 0:1], P0[:, i, 0:w],
                                         ALU.mult, ALU.add).then_inc(dw_made, 1)

            for what, n in MIX2_ORDER:
                if what == "lam":
                    dve.tensor_tensor(LP[0:64, :], par(C_LAM, 2, 0, 64), par(C_LAM + 2, 2, 0, 64), ALU.mult)\
                       .then_inc(lam_prod, 1)
                    dve.wait_ge(lam_exp, 1)
                    dve.scalar_tensor_tensor(NEGLAM, LE[:, 1:2], -LAMBDA_INIT, LE[:, 0:1],
                                             ALU.add, ALU.subtract).then_inc(lam_made, 1)
                    dve.tensor_scalar(par(C_DFG), par(C_DFG), 1.0 - LAMBDA_INIT, None, ALU.mult)\
                       .then_inc(lam_made, 1)
                    dve.wait_ge(lam_made, 2)
                elif what == "ba":
                    evacuate(G_BA, U_BA, BR[0:36, :], 36)
                    then(dve.memset(CB[:, :, 0:3], 0.0))
                elif what == "rows":
                    rows(n)
                elif what == "kqv":
                    evacuate(G_KQV + n, U_KQV + n, CB[:, n % 2, 3:T + 3])
                    dve.wait_ge(cv_a, n + 1)
                    for j in (2, 1, 0):
                        tap = dve.scalar_tensor_tensor(tile_of(n), CB[:, n % 2, j:T + j], par(C_DCW + 4 * n + j),
                                                       tile_of(n), ALU.mult, ALU.add)
                        if j:
                            then(tap)
                    tap.then_inc(cv_v, 1)
                elif what == "x2":
                    dve.wait_ge(r1_mm, 1)
                    for k in (2 * n, 2 * n + 1):
                        dve.scalar_tensor_tensor(X[:, k, :], X[:, k, :], par(C_GFIN + k), PS[6][:, :],
                                                 ALU.mult, ALU.mult).then_inc(x_updated, 1)
                elif what == "cols":
                    dve.wait_ge(cols_mm, 1)
                    dve.memset(ST[:, :, :], 0.0).then_inc(st_made, 1)
                    dve.tensor_copy(COLS, PS[4][:, :].rearrange("p (b q r) -> p b q r", b=NB, q=4)[:, :, :, 0:4])\
                       .then_inc(cols_made, 1)
                elif what == "l2r":
                    dve.wait_ge(l2_rt, n + 1)
                    dve.reciprocal(L2C[:, 4 * n:4 * n + 4, :], L2C[:, 4 * n:4 * n + 4, :]).then_inc(l2_rc, 1)
                elif what == "l2b":
                    dve.wait_ge(l2_bc, n + 1)
                    dve.tensor_tensor(tile_of(n), tile_of(n), PS[2 + n % 2][:, :], ALU.mult).then_inc(l2_made, 1)
                elif what == "dfqk":
                    n, part = n
                    if n >= 1 and part == 2:
                        dve.wait_ge(qn_rt, n)
                        dve.reciprocal(QNC, QNC).then_inc(qn_rc, 1)
                    if n >= 1 and part == 3:
                        normalise_qk(n - 1)
                    if n < 8 and part == 3:
                        evacuate(G_DFQK + n, U_DFQK + n, (DQ if n % 2 == 0 else DK)[:, n // 2, :])
                elif what == "T1":
                    block_decays(n)
                elif what == "T2":
                    block_inputs(n)
                elif what == "Y":
                    masked_y(*n)
                elif what == "Z":
                    next_inverse(*n)
                elif what == "sa":
                    b, r = n // 2, 64 * (n % 2)
                    dve.wait_ge(uw_made, 2 * (b + 1))
                    dve.wait_ge(ws_mm, n + 1)
                    new = VT[r:r + 64, :, P * b:P * (b + 1)]
                    dve.tensor_tensor(new, new, heads(PS[6][r:r + 64, :]), ALU.subtract).then_inc(vn_made, 1)
                elif what == "sb":
                    dve.wait_ge(kv_mm, n + 1)
                    dve.wait_ge(st_made, n + 1)
                    dve.wait_ge(eg_made, n // 2 + 1)
                    for h in range(4):
                        last = dve.scalar_tensor_tensor(ST[:, h, :], ST[:, h, :],
                                                        EG[:, h, CH * (n + 1) - 1:CH * (n + 1)],
                                                        PS[7][:, P * h:P * (h + 1)], ALU.mult, ALU.add)
                    last.then_inc(st_made, 1)
                elif what == "A":
                    masked_max(n, 0)
                    masked_max(n, 1)
                elif what == "D":
                    difference(n)
                elif what == "z" and n[1] == 3:
                    n = n[0]
                    if n == 0:
                        dve.wait_ge(x_spilled, 16 * KC)
                        dve.wait_ge(qn_made, 8)
                    evacuate(G_Z + n, U_Z + n, ZT[:, n, :])
                elif what == "or":
                    tiles = slice(0, 4) if n == 0 else slice(n + 3, n + 4)
                    dve.wait_ge(o_rt, n + 1)
                    dve.reciprocal(OC[:, tiles, :], OC[:, tiles, :]).then_inc(o_rc, 1)
                elif what == "og":
                    o = (QT, DQ)[n // 4][:, n % 4, :]
                    dve.wait_ge(silu_z, n + 1)
                    dve.wait_ge(o_sq, n + 1)
                    then(dve.scalar_tensor_tensor(o, o, par(C_DNG if n < 4 else C_DFG), ZT[:, n, :],
                                                  ALU.mult, ALU.mult))
                    dve.wait_ge(o_bc, n + 1)
                    dve.tensor_tensor(o, o, PS[6][:, :], ALU.mult).then_inc(o_made, 1)
                elif what == "ol":
                    dve.wait_ge(o_made, n + 1)
                    low((QT, DQ)[n // 4][:, n % 4, :], n, 3)
            for m in range(KC):
                dve.wait_ge(x_back[m], 16)
                dve.wait_ge(unit_done, U_WO2 + m + 1)
                dve.tensor_tensor(X[:, m, :], X[:, m, :], bank_of(G_WO2 + m)[:, :], ALU.add).then_inc(gemm_freed, 1)


def _constants():
    con = np.zeros((P, NCON), np.float32)
    i = np.arange(P)
    con[:, K_ID:K_ID + P] = i[:, None] == i[None, :]
    con[:, K_ONE:K_ONE + P] = 1.0
    con[:, K_HALF:K_HALF + P] = i[:, None] // HD == i[None, :] // HD
    con[:, K_CAUSAL + 384:K_CAUSAL + 512] = np.where(i[None, :] <= i[:, None], 0.0, NEG)
    same = i[:, None] // CH == i[None, :] // CH
    con[:, K_GNEG:K_GNEG + P] = np.where(same & (i[:, None] <= i[None, :]), 0.0, NEG)
    for l in range(LEVELS):
        pair = i[:, None] >> (l + 1) == i[None, :] >> (l + 1)
        con[:, K_LV + P * l:K_LV + P * (l + 1)] = pair & ((i[:, None] >> l & 1) == 1) & ((i[None, :] >> l & 1) == 0)
    return con


def _tiles(w):
    k, n = w.shape
    return w.reshape(k // P, P, n // P, P).transpose(2, 1, 0, 3).reshape(n // P, P, 1024)


def _moving(w):
    return w.reshape(4, 2, P, 512).transpose(0, 2, 1, 3).reshape(4, P, 1024)


def _padded(parts):
    out = np.zeros((D, P), np.float32)
    for at, w in parts:
        out[:, at:at + w.shape[1]] = w
    return _tiles(out)


def _stream(i):
    w_in, w_in2 = i["w_in"][0], i["w_in_2"][0]
    u, va, q, k, vb = (w_in[:, 512 * n:512 * (n + 1)] for n in range(5))
    dq, dk, dv, dz = (w_in2[:, 512 * n:512 * (n + 1)] for n in range(4))
    fq, fk, fv, fz = (w_in2[:, 2056 + 512 * n:2056 + 512 * (n + 1)] for n in range(4))
    qk = np.stack([_tiles(q), _tiles(k)], 1).reshape(8, P, 1024)
    fqk = np.stack([_tiles(fq), _tiles(fk)], 1).reshape(8, P, 1024)
    up = i["w_up"][0]
    up = np.stack([_tiles(up[:, :FF]), _tiles(up[:, FF:])], 1).reshape(2 * NFF, P, 1024)
    down = i["w_down"][0].reshape(NFF, P, KC, P).transpose(2, 0, 1, 3)
    down = down.reshape(NFF, 8, P, P).transpose(0, 2, 1, 3).reshape(NFF, P, 1024)
    units = [_moving(vb), _moving(va), _padded([(0, w_in[:, 2560:2568])]), qk, _tiles(u), _tiles(i["w_out"][0]),
             up, down, _padded([(0, w_in2[:, 2052:2056]), (32, w_in2[:, 2048:2052])]),
             _tiles(dk), _tiles(dq), _tiles(dv), _moving(fv), fqk, _tiles(dz), _tiles(fz), _tiles(i["w_out_2"][0])]
    s = np.concatenate(units)
    assert s.shape[0] == UNITS
    return np.ascontiguousarray(s.reshape(UNITS // 2, 2, P, 1024).transpose(0, 2, 1, 3).reshape(UNITS // 2, P, 2048))


def _parameters(i):
    p = np.zeros((P, NPAR), np.float32)

    def columns(at, v):
        v = v.reshape(-1, P).T
        p[:, at:at + v.shape[1]] = v

    columns(C_GMIX, i["norm_mix_g"])
    columns(C_GFFN, i["norm_ffn_g"])
    columns(C_GFIN, i["norm_final_g"])
    columns(C_GN2, i["norm_gain_2"])
    columns(C_SGG, i["sg_ln_g"])
    taps = i["w_conv"][0].reshape(3, 2, NFF, P).transpose(3, 2, 1, 0)
    p[:, C_FCW:C_FCW + 6 * NFF] = taps.reshape(P, -1)
    p[:, C_FCB:C_FCB + 2 * NFF] = i["b_conv"][0].reshape(2, NFF, P).transpose(2, 1, 0).reshape(P, -1)
    taps = i["conv_w_2"][0].reshape(4, 3, 4, P)[:, [1, 0, 2]]
    p[:, C_DCW:C_DCW + 48] = taps.transpose(3, 1, 2, 0).reshape(P, -1)
    p[0:8, C_FB] = i["f_bias"][0]
    p[0:4, C_ALOG] = i["a_log_2"][0]
    p[0:4, C_DTB] = i["dt_bias_2"][0]
    p[:, C_DNG] = i["dn_out_gain_2"][0]
    for c, name in ((C_QG, "q_gain_2"), (C_KG, "k_gain_2")):
        p[0:64, c] = p[64:128, c] = i[name][0]
    p[:, C_DFG] = i["df_out_gain_2"][0]
    for n, name in enumerate(("lambda_q1_2", "lambda_q2_2", "lambda_k1_2", "lambda_k2_2")):
        p[0:64, C_LAM + n] = i[name][0]
    return p


def kernel(**inputs):
    import concourse.bacc as bacc
    from concourse.bass_utils import run_bass_kernel_spmd

    i = {name: np.asarray(v) for name, v in inputs.items()}
    arrays = {
        "x_t": np.ascontiguousarray(i["x"][0].T),
        "wstream": _stream(i),
        "params": _parameters(i),
        "consts": _constants(),
        "sgw_t": np.ascontiguousarray(i["sg_w"][0].transpose(2, 0, 1)),
        "sgb": np.ascontiguousarray(i["sg_b"][0].reshape(4, 2, P)),
    }
    nc = bacc.Bacc("TRN2", target_bir_lowering=False, num_devices=1)
    args = [nc.dram_tensor(name, a.shape, F32, kind="ExternalInput").ap() for name, a in arrays.items()]
    args.append(nc.dram_tensor("out_t", (D, T), F32, kind="ExternalOutput").ap())
    build(nc, *args)
    r = run_bass_kernel_spmd(nc, [arrays], core_ids=[0])
    return np.ascontiguousarray(r.results[0]["out_t"].T)[None]
```

```python
from contextlib import ExitStack

import numpy as np

import concourse.bass as bass
from concourse import mybir

F32 = mybir.dt.float32
F32R = mybir.dt.float32r
ALU = mybir.AluOpType
ACT = mybir.ActivationFunctionType
AX_X = mybir.AxisListType.X

P = 128
T = 512
D = 1024
KC = D // P
NB = T // P
HD = 64
CH = 64
FF = 2816
NFF = FF // P
EPS = 1e-6
NEG = -1e30
LEVELS = 6
LAMBDA_INIT = 0.2

U_VB = 0
U_VA = 4
U_F = 8
U_QK = 9
U_WO = 21
U_UP = 29
U_DN = U_UP + 2 * NFF
U_BA = U_DN + NFF
U_KQV = U_BA + 1
U_DFV = U_KQV + 12
U_DFQK = U_DFV + 4
U_Z = U_DFQK + 8
U_WO2 = U_Z + 8
UNITS = U_WO2 + 8
RING = 4

G_F = 0
G_QK = 1
G_WO = 13
G_UP = 21
G_DN = G_UP + 2 * NFF
G_BA = G_DN + KC
G_KQV = G_BA + 1
G_DFQK = G_KQV + 12
G_Z = G_DFQK + 8
G_WO2 = G_Z + 8

_at = 0


def _cols(n):
    global _at
    _at += n
    return _at - n


C_GMIX, C_GFFN, C_GFIN, C_GN2 = (_cols(KC) for _ in range(4))
C_SGG = _cols(4)
C_FCW = _cols(2 * NFF * 3)
C_FCB = _cols(2 * NFF)
C_DCW = _cols(12 * 4)
C_FB, C_ALOG, C_DTB, C_DNG, C_QG, C_KG, C_DFG = (_cols(1) for _ in range(7))
C_LAM = _cols(4)
NPAR = _at

K_ID, K_ONE, K_HALF, K_CAUSAL, K_GNEG, K_LV = 0, 128, 256, 384, 896, 1024
NCON = K_LV + 128 * LEVELS

def _prepare(b, fills):
    steps = [(what, x) for what in ("T1", "T2") for x in (b, b + 1)]
    steps += [(what, (x, l)) for l in range(LEVELS) for what in ("Y", "Z", "X") if l or what != "Z" for x in (b, b + 1)]
    steps += [("W", b), ("W", b + 1)]
    return _spread([[x] for x in steps], fills)


def _quarters(what, units):
    return [(what, (n, part)) for n in units for part in range(4)]


def _merge(a, b):
    return _spread([[x] for x in a], b) if len(a) >= len(b) else _spread([[x] for x in b], a)


def _scans(steps):
    return [(what, i) for i in steps for what in ("sa", "sb")]


def _attention(heads, score="A", weigh="D", turn="B", attend="C", ahead=None):
    slots = []
    for n in range(NB * heads + 3):
        slot = []
        if 1 <= n <= NB * heads:
            slot.append((weigh, n - 1))
        if n < NB * heads:
            slot.append((score, n))
        if ahead and n % NB == 2 and n // NB + 1 < heads:
            slot.append((ahead, n // NB + 1))
        values = [(attend, (n - 6) // NB)] if n >= 6 and (n - 6) % NB == 0 else []
        turned = [(turn, n - 2)] if 2 <= n < NB * heads + 2 else []
        slots.append(slot + (values + turned if ahead else turned + values))
    return slots


def _flat(slots):
    return [x for slot in slots for x in slot]


MIX1_UNITS = [("qk", 0), ("qk", 1), ("qk", 2), ("u", 0), ("qk", 3), ("u", 1), ("qk", 4), ("u", 2), ("qk", 5),
              ("qk", 6), ("qk", 7), ("u", 3)]


def _mix1():
    slots = _attention(8, weigh="N", ahead="K")

    def part(a, b, fills):
        return _spread([[x] for x in _flat(slots[a:b])], fills)

    def products(a, b):
        return [(what, (n, q)) for what, n in MIX1_UNITS[a:b] for q in range(4)]

    partial = [("wo", (m, ks)) for m in range(4) for ks in ((0, 4), (4, 7))]
    return (products(0, 2) + [("K", 0)] + products(2, 3)[:2] + part(0, 8, products(2, 6)[2:])
            + part(8, 16, _merge(products(6, 9), [("ln", (n, b)) for n in range(3) for b in range(NB)]))
            + part(16, 24, products(9, 11)) + part(24, 27, products(11, 12) + [("gelu", 0)])
            + part(27, 30, [("gate", p) for p in range(4)])
            + part(30, 33, [("split", k) for k in range(7)] + partial[:2])
            + part(33, 35, partial[2:5]) + [("split", 7), ("wo", (0, (7, 8)))] + partial[5:6]
            + [("wo", (1, (7, 8)))] + partial[6:7] + [("wo", (2, (7, 8)))] + partial[7:] + [("wo", (3, (7, 8)))])


def step(b, l):
    return (b // 2) * 2 * LEVELS + 2 * l + b % 2


def _spread(groups, fills):
    order, used = [], 0
    for n, group in enumerate(groups):
        order += group
        upto = len(fills) * (n + 1) // len(groups)
        order += fills[used:upto]
        used = upto
    return order


def _projections():
    order = [("ba", 0)]
    for t in range(12):
        if t in (6, 10):
            order.append(("l2r", t // 4 - 1))
        order.append(("kqv", t))
        if t == 5:
            order.append(("lam", 0))
        if t in (0, 2):
            order.append(("rows", t // 2))
        if t == 7:
            order.append(("cols3", 0))
        if 7 <= t <= 10:
            order.append(("x2", t - 7))
        if t == 6:
            order.append(("cols", 0))
        if 2 <= t <= 9:
            order.append(("l2s", t - 2))
        if t >= 8:
            order.append(("l2b", t - 8))
    groups = [[("l2b", 4)], [("l2b", 5), ("decay", 0)], [("l2b", 6), ("decay", 1)],
              [("l2b", 7), ("decay", 2), ("decay", 3)]]
    return order + _spread(groups, [("dfv", n) for n in range(4)])


MIX1_ORDER = _mix1()
MIX2_ORDER = (
    _projections()
    + _prepare(0, [("dfv", n) for n in range(4, 8)] + _quarters("dfqk", range(9))[:35])
    + _prepare(2, _quarters("dfqk", range(9))[35:] + _flat(_attention(4)))
    + _merge(_quarters("z", range(4)), _merge(_scans(range(5)), [("os", t) for t in range(4)] + [("or", 0)]))
    + [("zs", 0)]
    + _merge(_quarters("z", range(4, 7)),
             _merge(_scans(range(5, 8)), [(what, t) for t in range(4) for what in ("og", "oh", "ol")]))
    + _merge(_quarters("z", range(7, 8)), [("os", t) for t in range(4, 8)] + [("or", 1)])
    + [("zs", 1), ("w2", 0), ("og", 4), ("og", 5), ("oh", 4), ("w2", 1), ("ol", 4), ("oh", 5), ("og", 6), ("w2", 2),
       ("ol", 5), ("oh", 6), ("og", 7), ("w2", 3), ("ol", 6), ("oh", 7), ("ol", 7)]
)
PCOL = [P * i * (i + 1) // 2 for i in range(NB)]
PALL = P * NB * (NB + 1) // 2


def build(nc, x_t, wstream, params, consts, sgw_t, sgb, out_t):
    with ExitStack() as ctx:
        here = [16512]

        def place(name, shape, dt, at=None):
            size = 4 * int(np.prod(shape[1:]))
            if at is None:
                at = here[0]
                here[0] += (size + 31) // 32 * 32
            return nc.alloc_sbuf_tensor_at(name, shape, dt, offset=at)

        def sem(name):
            return ctx.enter_context(nc.semaphore(name))

        X_AT = here[0]
        X = place("X", [P, KC, T], F32)
        GH = place("GH", [P, KC, T], F32R)
        GL = place("GL", [P, KC, T], F32R)
        RAW = place("RAW", [P, RING, 1024], F32)
        HI = place("HI", [P, RING, 1024], F32R)
        LO = place("LO", [P, RING, 1024], F32R)
        CON = place("CON", [P, NCON], F32)
        PAR = place("PAR", [P, NPAR], F32)
        RB = place("RB", [P, T], F32)
        SM = place("SM", [P, 320], F32)
        IDR = place("IDR", [P, 8], F32R)
        arena = here[0]
        KB = 1024

        MT = place("MT", [P, 8, T], F32, arena)
        KT1 = place("KT1", [P, 4, T], F32, arena + 16 * KB)
        VB = place("VB", [P, NB, 512], F32, arena + 24 * KB)
        P1 = place("P1", [P, 2, PALL], F32, arena + 32 * KB)
        PT1 = place("PT1", [P, NB, T], F32, arena + 42 * KB)
        NCB = place("NCB", [P, 2, T], F32, arena + 50 * KB)
        NCD = place("NCD", [P, 2, T], F32, arena + 54 * KB)
        FR = place("FR", [P, 3, T], F32, arena + 58 * KB)
        FRP = place("FRP", [P, 2, T], F32R, arena + 58 * KB)
        SGW = place("SGW", [P, 8, P], F32, arena + 64 * KB)
        SGB = place("SGB", [P, 4, P], F32, arena + 68 * KB)
        VA = place("VA", [P, NB, 512], F32, arena + 70 * KB)
        SQV = place("SQV", [P, NB, 512], F32, arena + 78 * KB)
        MH = place("MH", [P, KC, T], F32R, arena + 64 * KB)
        ML = place("ML", [P, KC, T], F32R, arena + 80 * KB)
        AH = place("AH", [P, NFF, T], F32R, arena)
        AL = place("AL", [P, NFF, T], F32R, arena + 44 * KB)
        AB = place("AB", [P, 2, T + 2], F32, arena + 88 * KB)
        YC = place("YC", [P, 2, T], F32, arena + 88 * KB + 4128)
        SQ = place("SQ", [P, 2, T], F32, arena + 96 * KB + 96)
        ACC = SQ[:, 1, :]
        assert arena + 100 * KB + 96 <= 229368, arena
        SQB, ACCB = YC[:, 0, :], YC[:, 1, :]
        KT = place("KT", [P, 4, T], F32, arena)
        QT = place("QT", [P, 4, T], F32, arena + 8 * KB)
        VT = place("VT", [P, 4, T], F32, arena + 16 * KB)
        EG = place("EG", [P, 4, T], F32, arena + 24 * KB)
        AQK = place("AQK", [P, NB, 4, P], F32, arena + 32 * KB)
        KDEC = place("KDEC", [P, NB, 4, P], F32, arena + 40 * KB)
        TR = arena + 48 * KB
        RSP = place("RSP", [P, 2, T], F32R, TR + 17 * KB)
        NT = place("NT", [P, 2, 4, P], F32, TR)
        XI = place("XI", [P, 2, 4, P], F32, TR + 4 * KB)
        XT = place("XT", [P, 2, 4, P], F32, TR + 8 * KB)
        YM = place("YM", [P, 2, 4, P], F32, TR + 12 * KB)
        KBE = place("KBE", [P, 2, 4, P], F32, TR + 16 * KB)
        VBT = place("VBT", [P, 2, 4, P], F32, TR + 20 * KB)
        CB = place("CB", [P, 2, T + 4], F32, TR)
        R1 = place("R1", [P, T], F32, TR + 5 * KB)
        R2 = place("R2", [P, T], F32, TR + 7 * KB)
        BR = place("BR", [P, T], F32, TR + 11 * KB)
        SQ2 = place("SQ2", [P, 2, T], F32, TR + 13 * KB)
        ZT = place("ZT", [P, 8, T], F32, TR)
        SQO = place("SQO", [P, 2, T], F32, TR + 16 * KB)
        DQ = place("DQ", [P, 4, T], F32, arena + 72 * KB)
        DK = place("DK", [P, 4, T], F32, arena + 80 * KB)
        DV = place("DV", [P, NB, 512], F32, arena + 88 * KB)
        RS = place("RS", [P, T], F32, arena + 96 * KB)
        ST = place("ST", [P, 4, P], F32, arena + 98 * KB)
        QNR = place("QNR", [P, T], F32, X_AT)
        SQD = place("SQD", [P, T], F32, X_AT + 2 * KB)
        P0 = place("P0", [P, 3, T], F32, X_AT)
        PB = place("PB", [P, T], F32, X_AT + 6 * KB)
        PT2 = place("PT2", [P, NB, T], F32, X_AT + 8 * KB)
        FH = place("FH", [P, 4, T], F32R, X_AT)
        FL = place("FL", [P, 4, T], F32R, X_AT + 8 * KB)
        XR = place("XR", [P, KC, T], F32, TR)

        PS = [ctx.enter_context(nc.psum_tensor(f"bank{b}", [P, 512], F32)) for b in range(8)]

        EPSC = SM[:, 0:4]
        RCOL = SM[:, 4:8]
        MX = SM[:, 8:24].rearrange("p (a b) -> p a b", a=2)
        SU = SM[:, 24:40].rearrange("p (a b) -> p a b", a=2)
        RC = SM[:, 40:56].rearrange("p (a b) -> p a b", a=2)
        LP, LE, NEGLAM = SM[:, 56:58], SM[:, 58:60], SM[:, 60:61]
        EA = SM[:, 61:62]
        S1 = SM[:, 62:64]
        LNS, LNV = SM[:, 64:96], SM[:, 96:128]
        COLS = SM[:, 128:192].rearrange("p (b q h) -> p b q h", b=NB, q=4)
        MXA = SM[:, 192:200]
        R1C, SS2C = SM[:, 272:276], SM[:, 276:280]
        GG = SM[:, 280:288]
        L2C = SM[:, 200:232].rearrange("p (t b) -> p t b", b=NB)
        OC = SM[:, 232:264].rearrange("p (t b) -> p t b", b=NB)

        IDENT, ONES, HALF = (CON[:, c:c + P] for c in (K_ID, K_ONE, K_HALF))
        CAUSAL = CON[:, K_CAUSAL:K_CAUSAL + 512]
        GNEG = CON[:, K_GNEG:K_GNEG + P]

        def level_mask(l):
            return CON[:, K_LV + P * l:K_LV + P * (l + 1)]

        def par(c, n=1, p0=0, p1=P):
            return PAR[p0:p1, c:c + n]

        def heads(ap):
            return ap.rearrange("p (h c) -> p h c", h=4)

        x_landed = [sem(f"x_landed{k}") for k in range(KC)]
        par_landed, con_landed, masks_landed = sem("par_landed"), sem("con_landed"), sem("masks_landed")
        sg_landed = sem("sg_landed")
        first_landed = sem("first_landed")
        w_landed = [sem("w_landed0"), sem("w_landed1")]
        hi_made, unit_split, unit_done = sem("hi_made"), sem("unit_split"), sem("unit_done")
        stored, x_spilled = sem("stored"), sem("x_spilled")
        x_back = [sem(f"x_back{k}") for k in range(KC)]
        sq_made, sq_added, ss_made = sem("sq_made"), sem("sq_added"), sem("ss_made")
        sqb_made, sqb_added, gg_made = sem("sqb_made"), sem("sqb_added"), sem("gg_made")
        r1_root, r1_made, r1_mm, ms_made = sem("r1_root"), sem("r1_made"), sem("r1_mm"), sem("ms_made")
        mh_made, ml_made = sem("mh_made"), sem("ml_made")
        fh_made, fl_made = sem("fh_made"), sem("fl_made")
        rms_made, rcol_made, rb_mm, rb_ready = sem("rms_made"), sem("rcol_made"), sem("rb_mm"), sem("rb_ready")
        gh_made, gl_made, x_updated = sem("gh_made"), sem("gl_made"), sem("x_updated")
        gemm_freed = sem("gemm_freed")
        v_chain = sem("v_chain")
        eps_made = sem("eps_made")
        vb_freed, va_freed = sem("vb_freed"), sem("va_freed")
        ln_centered, ln_squared, ln_summed, ln_root, vn_ready = (
            sem(n) for n in ("ln_centered", "ln_squared", "ln_summed", "ln_root", "vn_ready"))
        sgw_masked = sem("sgw_masked")
        idr_made, negc_high, negc_split = sem("idr_made"), sem("negc_high"), sem("negc_split")
        g_high, g_split = sem("g_high"), sem("g_split")
        f_made, f_log, negc_ready = sem("f_made"), sem("f_log"), sem("negc_ready")
        gelu_made = sem("gelu_made")
        ncb_mm, ncb_made = sem("ncb_mm"), sem("ncb_made")
        s_made, max_made, exp_made, p_ready = (sem(n) for n in ("s_made", "max_made", "exp_made", "p_ready"))
        pt_mm, pt_freed, pv_made, attended = (sem(n) for n in ("pt_mm", "pt_freed", "pv_made", "attended"))
        gate_mm, gated = sem("gate_mm"), sem("gated")
        conv_started, conv_made = sem("conv_started"), sem("conv_made")
        silu_ff, ff_made, ah_made, al_made = (sem(n) for n in ("silu_ff", "ff_made", "ah_made", "al_made"))
        down_done = sem("down_done")
        lam_prod, lam_mm, lam_exp, lam_made = (sem(n) for n in ("lam_prod", "lam_mm", "lam_exp", "lam_made"))
        ba_v, ba_a = sem("ba_v"), sem("ba_a")
        cv_a, cv_v, cv_s = sem("cv_a"), sem("cv_v"), sem("cv_s")
        cols_mm, cols_made, gcb_mm, gcb_made = (sem(n) for n in ("cols_mm", "cols_made", "gcb_mm", "gcb_made"))
        dfv_freed = sem("dfv_freed")
        l2_sq, l2_mm, l2_rt, l2_rc, l2_bc, l2_made = (
            sem(n) for n in ("l2_sq", "l2_mm", "l2_rt", "l2_rc", "l2_bc", "l2_made"))
        qn_sq, qn_mm, qn_rt, qn_rc, qn_made = (sem(n) for n in ("qn_sq", "qn_mm", "qn_rt", "qn_rc", "qn_made"))
        tk_mm, tv_mm, g_mm, aq_mm = (sem(n) for n in ("tk_mm", "tv_mm", "g_mm", "aq_mm"))
        d_made, d_exp, eg_made, kd_made, vbt_made, nt_made, qe_made = (
            sem(n) for n in ("d_made", "d_exp", "eg_made", "kd_made", "vbt_made", "nt_made", "qe_made"))
        y_mm, ym_made, z_mm, xi_made, xt_mm, xt_made = (
            sem(n) for n in ("y_mm", "ym_made", "z_mm", "xi_made", "xt_mm", "xt_made"))
        u_mm, w_mm, uw_made = sem("u_mm"), sem("w_mm"), sem("uw_made")
        st_made, ws_mm, vn_made, ot_mm, kv_mm, od_made = (
            sem(n) for n in ("st_made", "ws_mm", "vn_made", "ot_mm", "kv_mm", "od_made"))
        ds_mm, dmax, dexp, dw_made = (sem(n) for n in ("ds_mm", "dmax", "dexp", "dw_made"))
        dpt_mm, dpt_freed, dpv_mm, dpv_freed = (sem(n) for n in ("dpt_mm", "dpt_freed", "dpv_mm", "dpv_freed"))
        silu_z = sem("silu_z")
        o_sq, o_mm, o_rt, o_rc, o_bc, o_made = (sem(n) for n in ("o_sq", "o_mm", "o_rt", "o_rc", "o_bc", "o_made"))

        def bank_of(g):
            return PS[g % 2]

        def wo_bank(m):
            return PS[(G_WO % 2, 1 - G_WO % 2, 2, 3)[m % 4]]

        def turn_of(what, n):
            return MIX1_UNITS.index((what, n))

        def out_bank(m):
            return PS[(G_WO2 % 2, 1 - G_WO2 % 2, 6, 7)[m % 4]]

        def out_tile(t):
            return (DQ, QT)[t // 4][:, t % 4, :]

        block = ctx.enter_context(nc.Block())

        @block.sync
        def _(sp):
            def load(pair, slot):
                sp.dma_start(RAW[:, 2 * slot:2 * slot + 2, :],
                             wstream[pair].rearrange("p (a n) -> p a n", a=2)).then_inc(w_landed[slot], 16)

            def load_x(k):
                sp.dma_start(X[:, k, :], x_t[P * k:P * (k + 1), :]).then_inc(x_landed[k], 16)

            load_x(0)
            for a in range(2):
                sp.dma_start(RAW[:, a, :], wstream[0, :, 1024 * a:1024 * (a + 1)])\
                  .then_inc((first_landed, w_landed[0])[a], 16)
                load_x(a + 1)
            load(1, 1)
            for k in range(3, KC):
                load_x(k)
            with sp.Fori(1, UNITS // 4) as i:
                for s in range(2):
                    sp.wait_ge(unit_split, 4 * i + (2 * s - 2))
                    sp.dma_start(RAW[:, 2 * s:2 * s + 2, :],
                                 wstream[bass.ds(2 * i + s, 1)].rearrange("o p (a n) -> p (o a) n", a=2))\
                      .then_inc(w_landed[s], 16)
            for m in range(KC):
                sp.wait_ge(gemm_freed, G_WO2 + m + 1)
                sp.dma_start(out_t[P * m:P * (m + 1), :], XR[:, m, :]).then_inc(stored, 16)
            sp.wait_ge(stored, 16 * KC)

        @block.gpsimd
        def _(pool):
            def split(slot, done, unit):
                pool.wait_ge(w_landed[slot // 2], done)
                pool.tensor_tensor(HI[:, slot, :].rearrange("p (a n) -> p a n", n=P),
                                   RAW[:, slot, :].rearrange("p (a n) -> p a n", n=P),
                                   ONES.unsqueeze(1).to_broadcast([P, KC, P]), ALU.mult).then_inc(hi_made, 1)
                pool.wait_ge(hi_made, unit + 1)
                pool.tensor_tensor(LO[:, slot, :], RAW[:, slot, :], HI[:, slot, :].bitcast(F32),
                                   ALU.subtract).then_inc(unit_split, 1)

            pool.wait_ge(con_landed, 16)
            pool.wait_ge(unit_split, 1)
            for s in range(1, RING):
                split(s, 16, s)
            with pool.Fori(1, UNITS // 4) as i:
                for s in range(RING):
                    pool.wait_ge(unit_done, 4 * i + (s - RING + 1))
                    split(s, 16 * i + 16, 4 * i + s)

        @block.tensor
        def _(pe):
            def three(out, w, x, k, first, last, flip=False):
                (wh, wl), (xh, xl) = w, x
                for n, (a, b) in enumerate(((wh, xh), (wh, xl), (wl, xh))):
                    if flip:
                        a, b = b, a
                    mm = pe.matmul(out, a, b, start=(first and n == 0), stop=(last and n == 2))
                return mm

            def ring(u, blk, n=P):
                s = u % RING
                return HI[:, s, n * blk:n * (blk + 1)], LO[:, s, n * blk:n * (blk + 1)]

            def product(u, g, made, m0, high=GH, low=GL, ks=range(KC), out=None):
                pe.wait_ge(unit_split, u + 1)
                if g >= 2 and out is None:
                    pe.wait_ge(gemm_freed, g - 1)
                if out is None:
                    out = bank_of(g)
                for k in ks:
                    pe.wait_ge(made, m0 + k + 1)
                    mm = three(out[:, :], ring(u, k), (high[:, k, :], low[:, k, :]), k, k == 0, k == KC - 1)
                if k == KC - 1:
                    mm.then_inc(unit_done, 1)

            def product_out(m, ks):
                if m < 2:
                    pe.wait_ge(gemm_freed, G_WO2 + m - 1)
                elif m < 4:
                    pe.wait_ge(vn_made, 8)
                    pe.wait_ge(st_made, 9)
                else:
                    pe.wait_ge(gemm_freed, G_WO2 + m - 3)
                if ks[0] == 0:
                    product(U_WO2 + m, G_WO2 + m, fl_made, 0, FH, FL, range(4), out_bank(m))
                if ks[-1] == KC - 1:
                    product(U_WO2 + m, G_WO2 + m, gl_made, 3 * KC - 4, GH, GL, range(4, KC), out_bank(m))

            def product_tokens(u0, banks, m0, kks=range(KC), last_bank=None):
                for k in kks:
                    u = u0 + k // 2
                    pe.wait_ge(unit_split, u + 1)
                    pe.wait_ge(gl_made, m0 + k + 1)
                    for b in range(NB):
                        if last_bank and k == 0 and b == NB - 1:
                            pe.wait_ge(*last_bank)
                        mm = three(PS[banks[b]][:, :], ring(u, k % 2, 512),
                                   (GH[:, k, P * b:P * (b + 1)], GL[:, k, P * b:P * (b + 1)]),
                                   k, k == 0, k == KC - 1, flip=True)
                    if k % 2 == 1:
                        mm.then_inc(unit_done, 1)

            def token_sums(out, src, groups=ONES[:, 0:1]):
                n = groups.shape[1]
                for b in range(NB):
                    mm = pe.matmul(out[:, n * b:n * (b + 1)], src[:, P * b:P * (b + 1)], groups, start=True, stop=True)
                return mm

            def over_rows(out, column):
                for b in range(NB):
                    mm = pe.matmul(out[:, P * b:P * (b + 1)], column(b), IDENT, start=True, stop=True)
                return mm

            def sum_squares(n):
                pe.wait_ge(sq_added, KC * (n + 1))
                token_sums(PS[7], ACC).then_inc(ss_made, 1)

            def spread_rms(n, bank=PS[7]):
                pe.wait_ge(rcol_made, n + 1)
                over_rows(bank, lambda b: RCOL[:, b:b + 1].to_broadcast([P, P])).then_inc(rb_mm, 1)

            pe.wait_ge(con_landed, 16)

            product_tokens(U_VB, (2, 3, 4, 5), 0)
            sum_squares(0)
            product_tokens(U_VA, (0, 1, 6, 7), 0, last_bank=(rms_made, 1))
            pe.wait_ge(vb_freed, 1)
            spread_rms(0, PS[2])
            pe.wait_ge(va_freed, 2)
            product(U_F, G_F, gl_made, 0)

            def product_mixed(m, ks):
                if m < 2:
                    pe.wait_ge(gated, 4)
                elif m < 4:
                    pe.wait_ge(exp_made, 32)
                else:
                    pe.wait_ge(gemm_freed, G_WO + m - 3)
                product(U_WO + m, G_WO + m, ml_made, 0, MH, ML, ks, wo_bank(m))

            def one_row(out, rows, h, parts):
                for n in range(2):
                    mm = pe.matmul(out[:, :], IDR[0:rows, h:h + 1].to_broadcast([rows, P]), parts[0:rows, n, :],
                                   start=(n == 0), stop=(n == 1))
                return mm

            def spread_decay(h):
                pe.wait_ge(negc_split, 1)
                if h >= 1:
                    pe.wait_ge(ncb_made, h)
                else:
                    pe.wait_ge(va_freed, 4)
                one_row(PS[7], 8, h, FRP).then_inc(ncb_mm, 1)

            def scores(n):
                h, i = n // NB, n % NB
                r = 64 * (h % 2)
                if i == 0:
                    pe.wait_ge(gemm_freed, G_QK + turn_of("qk", 2 * (h // 2) + 1) + 1)
                    pe.wait_ge(vb_freed, 4)
                if n >= 2:
                    pe.wait_ge(exp_made, n - 1)
                pe.matmul(PS[2 + n % 2][:, 0:P * (i + 1)], MT[r:r + 64, 4 + h // 2, P * i:P * (i + 1)],
                          KT1[r:r + 64, h // 2, 0:P * (i + 1)], start=True, stop=True).then_inc(s_made, 1)

            def turn(n):
                h, i = n // NB, n % NB
                pe.wait_ge(p_ready, n + 1)
                if n >= 2:
                    pe.wait_ge(pt_freed, n - 1)
                for j in range(i + 1):
                    mm = pe.transpose(PS[4 + n % 2][:, P * j:P * (j + 1)],
                                      P1[:, h % 2, PCOL[i] + P * j:PCOL[i] + P * (j + 1)], IDENT)
                mm.then_inc(pt_mm, 1)

            def attend(h):
                pe.wait_ge(pt_freed, NB * (h + 1))
                if h % 2 == 0 and h >= 2:
                    pe.wait_ge(attended, h // 2)
                r = 64 * (h % 2)
                for j in range(NB):
                    mm = pe.matmul(PS[6][r:r + 64, P * j:T], VB[:, j, 64 * h:64 * (h + 1)], PT1[:, j, P * j:T],
                                   start=(j == 0), stop=(j == NB - 1))
                mm.then_inc(pv_made, 1)

            def gate(p):
                pe.wait_ge(vn_ready, NB)
                pe.wait_ge(sgw_masked, 1)
                pe.wait_ge(gemm_freed, G_WO)
                if p >= 2:
                    pe.wait_ge(gated, p - 1)
                for b in range(NB):
                    for e in range(2):
                        hh = 2 * p + e
                        mm = pe.matmul(PS[p % 2][64 * e:64 * e + 64, P * b:P * (b + 1)],
                                       VA[:, b, 64 * hh:64 * (hh + 1)], SGW[:, hh, :], start=True, stop=True)
                mm.then_inc(gate_mm, 1)

            for what, n in MIX1_ORDER:
                if what in ("qk", "u"):
                    turn_n = turn_of(what, n[0])
                    product(U_QK + turn_n, G_QK + turn_n, gl_made, 0, ks=range(2 * n[1], 2 * n[1] + 2))
                elif what == "K":
                    spread_decay(n)
                elif what == "A":
                    scores(n)
                elif what == "B":
                    turn(n)
                elif what == "C":
                    attend(n)
                elif what == "gate":
                    gate(n)
                elif what == "wo":
                    product_mixed(n[0], range(*n[1]))
            for m in range(4, KC):
                product_mixed(m, range(KC))

            product(U_UP, G_UP, gl_made, KC, ks=range(KC - 1))
            product(U_UP + 1, G_UP + 1, gl_made, KC, ks=range(2))
            sum_squares(1)
            product(U_UP + 1, G_UP + 1, gl_made, KC, ks=range(2, KC - 1))
            spread_rms(1)
            product(U_UP, G_UP, gl_made, KC, ks=(KC - 1,))
            product(U_UP + 1, G_UP + 1, gl_made, KC, ks=(KC - 1,))
            for q in (2, 3):
                product(U_UP + q, G_UP + q, gl_made, KC)
            with pe.Fori(1, NFF // 2) as i:
                for q in range(4):
                    u, g = U_UP + q, G_UP + q
                    pe.wait_ge(unit_split, 4 * i + (u + 1))
                    pe.wait_ge(gemm_freed, 4 * i + (g - 1))
                    for k in range(KC):
                        mm = three(bank_of(g)[:, :], ring(u, k), (GH[:, k, :], GL[:, k, :]), k, k == 0, k == KC - 1)
                    mm.then_inc(unit_done, 1)
            for m in range(KC):
                pe.wait_ge(gemm_freed, G_DN + m - 1)
                for c in range(NFF):
                    n = NFF * m + c
                    u = U_DN + n // 8
                    if n % 8 == 0:
                        pe.wait_ge(unit_split, u + 1)
                    if m == 0:
                        pe.wait_ge(al_made, c + 1)
                    mm = three(bank_of(G_DN + m)[:, :], ring(u, n % 8), (AH[:, c, :], AL[:, c, :]), c,
                               c == 0, c == NFF - 1)
                    if n % 8 == 7:
                        mm.then_inc(unit_done, 1)
                    elif c == NFF - 1:
                        mm.then_inc(down_done, 1)


            def lam():
                pe.wait_ge(lam_prod, 1)
                pe.matmul(PS[2][:, 0:2], ONES[0:64, :], LP[0:64, :], start=True, stop=True).then_inc(lam_mm, 1)

            def spread_row(h):
                one_row(PS[(2, 3, 7, 2)[h]], 4, h, RSP).then_inc(gcb_mm, 1)

            def rows_to_columns():
                pe.wait_ge(ba_a, 7)
                for b in range(NB):
                    mm = pe.transpose(PS[4][:, P * b:P * (b + 1)], RS[:, P * b:P * (b + 1)], IDENT)
                mm.then_inc(cols_mm, 1)
                pe.wait_ge(rb_ready, 3)
                pe.wait_ge(lam_exp, 1)
                pe.wait_ge(g_split, 1)
                for h in range(3):
                    spread_row(h)

            def head_sums(t):
                pe.wait_ge(l2_sq, t + 1)
                if t == 4:
                    pe.wait_ge(l2_rt, 1)
                token_sums(PS[5][:, NB * t:NB * (t + 1)], SQ2[:, t % 2, :]).then_inc(l2_mm, 1)

            def spread_norm(t):
                pe.wait_ge(l2_rc, t // 4 + 1)
                if t >= 2:
                    pe.wait_ge(l2_made, t - 1)
                else:
                    pe.wait_ge(gcb_made, 4)
                over_rows(PS[2 + t % 2], lambda b: L2C[:, t, b:b + 1].to_broadcast([P, P])).then_inc(l2_bc, 1)

            def qk_sums(n):
                pe.wait_ge(qn_sq, n + 1)
                pe.matmul(bank_of(G_DFQK + n)[:, :], HALF, SQD[:, :], start=True, stop=True).then_inc(qn_mm, 1)

            def blk(b):
                return slice(P * b, P * (b + 1))

            def banks_for(b):
                return (PS[2 + 2 * (b % 2)], PS[3 + 2 * (b % 2)])

            def block_products(b):
                A, B = banks_for(b)
                if b < 2:
                    pe.wait_ge(l2_made, 8)
                    pe.wait_ge(cols_made, 1)
                else:
                    pe.wait_ge(uw_made, 2 * (b - 1))
                for h in range(4):
                    mm = pe.matmul(A[:, blk(h)], KT[:, h, blk(b)], KT[:, h, blk(b)], start=True, stop=True)
                mm.then_inc(g_mm, 1)
                for h in range(4):
                    mm = pe.matmul(B[:, blk(h)], KT[:, h, blk(b)], QT[:, h, blk(b)], start=True, stop=True)
                mm.then_inc(aq_mm, 1)

            def token_major(b):
                A, B = banks_for(b)
                pe.wait_ge(cv_s, 12)
                pe.wait_ge(nt_made, b + 1)
                for h in range(4):
                    mm = pe.transpose(A[:, blk(h)], KT[:, h, blk(b)], IDENT)
                mm.then_inc(tk_mm, 1)
                for h in range(4):
                    mm = pe.transpose(B[:, blk(h)], VT[:, h, blk(b)], IDENT)
                mm.then_inc(tv_mm, 1)

            def inverse_y(b, l):
                A = banks_for(b)[0]
                s = b % 2
                if l == 0:
                    pe.wait_ge(kd_made, b + 1)
                else:
                    pe.wait_ge(xi_made, step(b, l - 1) + 1)
                for h in range(4):
                    if l == 0:
                        mm = pe.transpose(A[:, blk(h)], NT[:, s, h, :], IDENT)
                    else:
                        mm = pe.matmul(A[:, blk(h)], NT[:, s, h, :], XI[:, s, h, :], start=True, stop=True)
                mm.then_inc(y_mm, 1)

            def inverse_z(b, l):
                s = b % 2
                pe.wait_ge(ym_made, step(b, l) + 1)
                pe.wait_ge(xt_made, step(b, l - 1) + 1)
                for h in range(4):
                    mm = pe.matmul(banks_for(b)[1][:, blk(h)], XT[:, s, h, :], YM[:, s, h, :], start=True, stop=True)
                mm.then_inc(z_mm, 1)

            def inverse_x(b, l):
                pe.wait_ge(xi_made, step(b, l) + 1)
                if l == 0:
                    pe.wait_ge(vbt_made, b + 1)
                for h in range(4):
                    mm = pe.transpose(banks_for(b)[1][:, blk(h)], XI[:, b % 2, h, :], IDENT)
                mm.then_inc(xt_mm, 1)

            def solve(b):
                A, B = banks_for(b)
                s = b % 2
                pe.wait_ge(xt_made, step(b, LEVELS - 1) + 1)
                pe.wait_ge(vbt_made, b + 1)
                for h in range(4):
                    mm = pe.matmul(A[:, blk(h)], XT[:, s, h, :], VBT[:, s, h, :], start=True, stop=True)
                mm.then_inc(u_mm, 1)
                for h in range(4):
                    mm = pe.matmul(B[:, blk(h)], KBE[:, s, h, :], XT[:, s, h, :], start=True, stop=True)
                mm.then_inc(w_mm, 1)

            def scan_state(i):
                b, r = i // 2, 64 * (i % 2)
                pe.wait_ge(st_made, i + 1)
                pe.wait_ge(uw_made, 2 * (b + 1))
                if i == 0:
                    pe.wait_ge(dpt_freed, 16)
                    pe.wait_ge(dpv_freed, 4)
                for h in range(4):
                    mm = pe.matmul(PS[6][r:r + 64, blk(h)], KT[:, h, P * b + r:P * b + r + 64], ST[:, h, :],
                                   start=True, stop=True)
                mm.then_inc(ws_mm, 1)

            def scan_output(i):
                b, r = i // 2, 64 * (i % 2)
                pe.wait_ge(vn_made, i + 1)
                pe.wait_ge(qe_made, b + 1)
                if i % 2 == 0 and i:
                    pe.wait_ge(od_made, b)
                elif i == 0:
                    pe.wait_ge(uw_made, 8)
                for h in range(4):
                    o = PS[2][:, P * h + r:P * h + r + 64]
                    mm = pe.matmul(o, ST[:, h, :], QT[:, h, CH * i:CH * (i + 1)], start=(r == 0 and h == 0), stop=False)
                    if r:
                        mm = pe.matmul(PS[2][:, blk(h)], VT[:, h, blk(b)], AQK[:, b, h, :], start=False, stop=(h == 3))
                mm.then_inc(ot_mm, 1)
                for h in range(4):
                    mm = pe.matmul(PS[7][:, blk(h)], KDEC[r:r + 64, b, h, :], VT[r:r + 64, h, blk(b)],
                                   start=True, stop=True)
                mm.then_inc(kv_mm, 1)

            def df_scores(n):
                h, i = n // NB, n % NB
                pe.wait_ge(qn_made, 8)
                for c in range(2):
                    if n:
                        pe.wait_ge(dexp, 2 * n + c - 1)
                    pe.matmul(PS[c][:, 0:P * (i + 1)], DQ[64 * c:64 * c + 64, h, blk(i)],
                              DK[64 * c:64 * c + 64, h, 0:P * (i + 1)], start=True, stop=True)\
                      .then_inc(ds_mm, 1)

            def df_turn(n):
                pe.wait_ge(dw_made, n + 1)
                if n >= 1:
                    pe.wait_ge(dpt_freed, n)
                else:
                    pe.wait_ge(dfv_freed, 4)
                for j in range(n % NB + 1):
                    mm = pe.transpose(PS[6][:, blk(j)], P0[:, n % 3, blk(j)], IDENT)
                mm.then_inc(dpt_mm, 1)

            def df_attend(h):
                pe.wait_ge(dpt_freed, NB * (h + 1))
                if h >= 1:
                    pe.wait_ge(dpv_freed, h)
                for j in range(NB):
                    mm = pe.matmul(PS[7][:, P * j:T], DV[:, j, blk(h)], PT2[:, j, P * j:T],
                                   start=(j == 0), stop=(j == NB - 1))
                mm.then_inc(dpv_mm, 1)

            def out_sums(t):
                pe.wait_ge(o_sq, t + 1)
                if t == 0:
                    pe.wait_ge(uw_made, 8)
                elif t >= 4:
                    pe.wait_ge(o_rt, 1)
                token_sums(PS[5][:, NB * t:NB * (t + 1)], SQO[:, t % 2, :]).then_inc(o_mm, 1)

            def spread_out(t):
                pe.wait_ge(o_rc, t // 4 + 1)
                if t >= 2:
                    pe.wait_ge(o_made, t - 1)
                over_rows(PS[3 + t % 2], lambda b: OC[:, t, b:b + 1].to_broadcast([P, P])).then_inc(o_bc, 1)

            for what, n in MIX2_ORDER:
                if what == "lam":
                    lam()
                elif what == "ba":
                    product(U_BA, G_BA, gl_made, 2 * KC, ks=range(KC - 1))
                    product(U_KQV, G_KQV, gl_made, 2 * KC, ks=range(2))
                    sum_squares(2)
                    pe.wait_ge(sqb_added, KC)
                    token_sums(PS[7][:, NB:2 * NB], ACCB).then_inc(ss_made, 1)
                    product(U_KQV, G_KQV, gl_made, 2 * KC, ks=range(2, KC - 1))
                    product(U_BA, G_BA, gl_made, 2 * KC, ks=(KC - 1,))
                    product(U_KQV, G_KQV, gl_made, 2 * KC, ks=(KC - 1,))
                elif what == "kqv":
                    if n:
                        product(U_KQV + n, G_KQV + n, gl_made, 2 * KC)
                    else:
                        spread_rms(2)
                        pe.wait_ge(r1_made, 1)
                        over_rows(PS[6], lambda b: R1C[:, b:b + 1].to_broadcast([P, P])).then_inc(r1_mm, 1)
                elif what == "cols":
                    rows_to_columns()
                elif what == "cols3":
                    pe.wait_ge(gcb_made, 1)
                    spread_row(3)
                elif what == "dfv":
                    if n == 0:
                        pe.wait_ge(gemm_freed, G_DFQK)
                        pe.wait_ge(gcb_made, 4)
                        pe.wait_ge(x_updated, KC)
                    product_tokens(U_DFV, (0, 1, 6, 7), 2 * KC, (n,))
                elif what == "l2s":
                    head_sums(n)
                elif what == "l2b":
                    spread_norm(n)
                elif what == "dfqk":
                    n, part = n
                    if n < 8:
                        if n < 2:
                            pe.wait_ge(dfv_freed, 2)
                        else:
                            pe.wait_ge(qn_rt, n - 1)
                        product(U_DFQK + n, G_DFQK + n, gl_made, 2 * KC, ks=range(2 * part, 2 * part + 2))
                    if n >= 1 and part == 1:
                        qk_sums(n - 1)
                elif what == "T1":
                    block_products(n)
                elif what == "T2":
                    token_major(n)
                elif what == "Y":
                    inverse_y(*n)
                elif what == "Z":
                    inverse_z(*n)
                elif what == "X":
                    inverse_x(*n)
                elif what == "W":
                    solve(n)
                elif what == "sa":
                    scan_state(n)
                elif what == "sb":
                    scan_output(n)
                elif what == "A":
                    df_scores(n)
                elif what == "B":
                    df_turn(n)
                elif what == "C":
                    df_attend(n)
                elif what == "z":
                    n, part = n
                    if n == 0:
                        pe.wait_ge(dexp, 32)
                    product(U_Z + n, G_Z + n, gl_made, 2 * KC, ks=range(2 * part, 2 * part + 2))
                elif what == "os":
                    out_sums(n)
                elif what == "og":
                    spread_out(n)
                elif what == "w2":
                    product_out(n, range(4))
            for m in range(KC):
                product_out(m, range(4 if m < 4 else 0, KC))

        @block.scalar
        def _(act):
            act.dma_start(PAR[:, :], params).then_inc(par_landed, 16)
            act.dma_start(CON[:, 0:K_CAUSAL], consts[:, 0:K_CAUSAL]).then_inc(con_landed, 16)
            act.wait_ge(par_landed, 16)
            act.wait_ge(eps_made, 4)

            def square_tile(n, k):
                if KC * n + k >= 1:
                    act.wait_ge(sq_added, KC * n + k)
                act.activation(SQ[:, 0, :], X[:, k, :], ACT.Square).then_inc(sq_made, 1)

            def root(n):
                act.wait_ge(ss_made, n + 1)
                act.activation(RCOL, PS[7][:, 0:NB], ACT.Sqrt, scale=1.0 / D, bias=EPSC[:, 0:1])\
                   .then_inc(rms_made, 1)

            def keep_rms(n, bank=PS[7]):
                act.wait_ge(rb_mm, n + 1)
                act.activation(RB[:, :], bank[:, :], ACT.Copy).then_inc(rb_ready, 1)

            def high(src, k, gain=None):
                act.activation(GH[:, k, :], src, ACT.Copy, scale=1.0 if gain is None else gain)\
                   .then_inc(gh_made, 1)

            for k in range(KC):
                if k == 1:
                    act.wait_ge(first_landed, 16)
                    act.activation(HI[:, 0, :], RAW[:, 0, :], ACT.Copy).then_inc(hi_made, 1)
                act.wait_ge(x_landed[k], 16)
                high(X[:, k, :], k, par(C_GMIX + k))
                square_tile(0, k)
            act.dma_start(CON[:, K_CAUSAL:NCON], consts[:, K_CAUSAL:NCON]).then_inc(masks_landed, 16)
            act.dma_start(SGW[:, :, :], sgw_t).then_inc(sg_landed, 16)
            for e in range(2):
                act.dma_start(SGB[64 * e:64 * e + 64, :, :],
                              sgb[:, e, :].unsqueeze(0).to_broadcast([64, 4, P])).then_inc(sg_landed, 16)
            root(0)
            act.wait_ge(rcol_made, 1)
            act.wait_ge(unit_done, U_VB + 4)
            for b in range(NB):
                act.activation(VB[:, b, :], PS[2 + b][:, :], ACT.Copy, scale=RCOL[:, b:b + 1]).then_inc(vb_freed, 1)
            act.wait_ge(unit_done, U_VA + 4)
            for b, bank in enumerate((0, 1, 6, 7)):
                act.activation(VA[:, b, :], PS[bank][:, :], ACT.Gelu, scale=RCOL[:, b:b + 1]).then_inc(va_freed, 1)
                if b == 1:
                    keep_rms(0, PS[2])
            act.wait_ge(f_made, 1)
            act.activation(FR[0:8, 1, :], FR[0:8, 0, :], ACT.Abs).then_inc(f_log, 1)
            act.wait_ge(f_log, 1)
            act.activation(FR[0:8, 1, :], FR[0:8, 1, :], ACT.Exp, scale=-1.0).then_inc(f_log, 1)
            act.wait_ge(f_log, 2)
            act.activation(FR[0:8, 1, :], FR[0:8, 1, :], ACT.Ln, bias=EPSC[0:8, 3:4]).then_inc(f_log, 1)

            act.activation(IDR[:, :], IDENT[:, 0:8], ACT.Copy).then_inc(idr_made, 1)
            act.wait_ge(negc_ready, 1)
            act.activation(FRP[0:8, 0, :], FR[0:8, 2, :], ACT.Copy).then_inc(negc_high, 1)

            for what, h in MIX1_ORDER:
                n = h
                if what == "ln" and n[0] == 0:
                    act.wait_ge(ln_centered, n[1] + 1)
                    act.activation(SQV[:, n[1], :], VA[:, n[1], :], ACT.Square).then_inc(ln_squared, 1)
                elif what == "ln" and n == (1, NB - 1):
                    act.wait_ge(ln_summed, NB)
                    act.activation(LNV, LNV, ACT.Sqrt, scale=1.0 / HD, bias=EPSC[:, 0:1]).then_inc(ln_root, 1)
                elif what == "K":
                    act.wait_ge(ncb_mm, h + 1)
                    if h >= 2:
                        act.wait_ge(max_made, NB * (h - 1))
                    act.activation(NCB[:, h % 2, :], PS[7][:, :], ACT.Copy).then_inc(ncb_made, 1)
                elif what == "A":
                    h, i = n // NB, n % NB
                    w = P * (i + 1)
                    act.wait_ge(max_made, n + 1)
                    if h >= 2:
                        act.wait_ge(pt_mm, NB * (h - 2) + i + 1)
                    act.activation(P1[:, h % 2, PCOL[i]:PCOL[i] + w], PS[2 + n % 2][:, 0:w], ACT.Exp,
                                   scale=-1.0, bias=MX[:, h % 2, i:i + 1], accum_out=SU[:, h % 2, i:i + 1])\
                       .then_inc(exp_made, 1)
                elif what == "B":
                    h, i = n // NB, n % NB
                    if i == 0 and h >= 1:
                        act.wait_ge(pv_made, h)
                    act.wait_ge(pt_mm, n + 1)
                    act.activation(PT1[:, 0:i + 1, P * i:P * (i + 1)],
                                   PS[4 + n % 2][:, 0:P * (i + 1)].rearrange("p (j c) -> p j c", c=P),
                                   ACT.Copy).then_inc(pt_freed, 1)
                elif what == "gelu":
                    for p in range(4):
                        act.wait_ge(gemm_freed, G_QK + turn_of("u", p) + 1)
                        act.activation(MT[:, p, :], MT[:, p, :], ACT.Gelu).then_inc(gelu_made, 1)
                elif what == "split":
                    if h < 4:
                        act.wait_ge(gated, 4)
                    else:
                        act.wait_ge(attended, h - 3)
                    act.activation(MH[:, h, :], MT[:, h, :], ACT.Copy).then_inc(mh_made, 1)
            for m in range(KC):
                act.wait_ge(gemm_freed, G_WO + m + 1)
                high(X[:, m, :], m, par(C_GFFN + m))
                square_tile(1, m)

            root(1)
            keep_rms(1)

            def feed_forward(t):
                for gv in range(2):
                    act.wait_ge(gemm_freed, 2 * t + (G_UP + gv + 1))
                    act.activation(YC[:, gv, :], AB[:, gv, 2:T + 2], ACT.Identity,
                                   scale=PAR[:, bass.ds(6 * t + (C_FCW + 3 * gv + 2), 1)],
                                   bias=PAR[:, bass.ds(2 * t + (C_FCB + gv), 1)]).then_inc(conv_started, 1)
                act.wait_ge(conv_made, 2 * t + 1)
                act.activation(YC[:, 0, :], YC[:, 0, :], ACT.Silu).then_inc(silu_ff, 1)
                act.wait_ge(ff_made, t + 1)
                act.activation(AH[:, bass.ds(t, 1), :], YC[:, 0:1, :], ACT.Copy).then_inc(ah_made, 1)

            feed_forward(0)
            with act.Fori(1, NFF) as t:
                act.wait_ge(al_made, t)
                feed_forward(t)
            act.wait_ge(gg_made, 1)
            act.wait_ge(al_made, NFF)
            for m in range(KC):
                act.wait_ge(gemm_freed, G_DN + m + 1)
                high(X[:, m, :], m, GG[:, m:m + 1])
                square_tile(2, m)
                if m:
                    act.wait_ge(sqb_added, m)
                act.activation(SQB, X[:, m, :], ACT.Square, scale=par(C_GFIN + m)).then_inc(sqb_made, 1)
            act.wait_ge(ss_made, 4)
            act.activation(R1C, PS[7][:, 0:NB], ACT.Sqrt, scale=1.0 / D, bias=EPSC[:, 0:1]).then_inc(r1_root, 1)
            act.wait_ge(ms_made, 1)
            act.activation(RCOL, SS2C, ACT.Sqrt, scale=1.0 / D, bias=EPSC[:, 0:1]).then_inc(rms_made, 1)
            act.wait_ge(rb_mm, 3)
            act.activation(RB[:, :], PS[7][:, :], ACT.Copy).then_inc(rb_ready, 1)

            def rows(stage):
                if stage == 0:
                    act.activation(EA[0:4, :], par(C_ALOG, 1, 0, 4), ACT.Exp).then_inc(ba_a, 1)
                    act.wait_ge(ba_v, 1)
                    act.activation(R2[0:4, :], R1[0:4, :], ACT.Abs).then_inc(ba_a, 1)
                    act.wait_ge(ba_a, 2)
                    act.activation(R2[0:4, :], R2[0:4, :], ACT.Exp, scale=-1.0).then_inc(ba_a, 1)
                    act.wait_ge(ba_a, 3)
                    act.activation(R2[0:4, :], R2[0:4, :], ACT.Ln, bias=EPSC[0:4, 3:4]).then_inc(ba_a, 1)
                else:
                    act.wait_ge(ba_v, 2)
                    act.activation(RS[32:36, :], BR[32:36, :], ACT.Exp, scale=-1.0).then_inc(ba_a, 1)
                    act.wait_ge(ba_v, 4)
                    act.activation(RS[64:68, :], RS[0:4, :], ACT.Exp).then_inc(ba_a, 1)
                    act.activation(RS[96:100, :], R1[0:4, :], ACT.Exp).then_inc(ba_a, 1)
                    act.activation(RSP[0:4, 0, :], RS[0:4, :], ACT.Copy).then_inc(g_high, 1)

            def tile_of(t):
                return (KT, QT, VT)[t // 4][:, t % 4, :]

            for what, n in MIX2_ORDER:
                if what == "lam":
                    act.wait_ge(lam_mm, 1)
                    act.activation(LE, PS[2][:, 0:2], ACT.Exp).then_inc(lam_exp, 1)
                elif what == "rows":
                    rows(n)
                elif what == "kqv":
                    act.wait_ge(gemm_freed, G_KQV + n + 1)
                    act.activation(tile_of(n), CB[:, n % 2, 3:T + 3], ACT.Copy,
                                   scale=par(C_DCW + 4 * n + 3)).then_inc(cv_a, 1)
                    act.wait_ge(cv_v, n + 1)
                    act.activation(tile_of(n), tile_of(n), ACT.Silu).then_inc(cv_s, 1)
                    if n < 8:
                        act.wait_ge(cv_s, n + 1)
                        if n >= 2:
                            act.wait_ge(l2_mm, n - 1)
                        act.activation(SQ2[:, n % 2, :], tile_of(n), ACT.Square).then_inc(l2_sq, 1)
                elif what in ("cols", "cols3"):
                    for h in range(3) if what == "cols" else (3,):
                        act.wait_ge(gcb_mm, h + 1)
                        act.activation(EG[:, h, :], PS[(2, 3, 7, 2)[h]][:, :], ACT.Copy).then_inc(gcb_made, 1)
                elif what == "x2":
                    for k in (2 * n, 2 * n + 1):
                        act.wait_ge(x_updated, k + 1)
                        act.dma_start(out_t[P * k:P * (k + 1), :], X[:, k, :]).then_inc(x_spilled, 16)
                elif what == "dfv" and n == KC - 1:
                    act.wait_ge(rcol_made, 3)
                    act.wait_ge(unit_done, U_DFV + 4)
                    for b, bank in enumerate((0, 1, 6, 7)):
                        act.activation(DV[:, b, :], PS[bank][:, :], ACT.Copy, scale=RCOL[:, b:b + 1])\
                           .then_inc(dfv_freed, 1)
                elif what == "l2r":
                    act.wait_ge(l2_mm, 4 * n + 4)
                    act.activation(L2C[:, 4 * n:4 * n + 4, :],
                                   PS[5][:, 16 * n:16 * n + 16].rearrange("p (t b) -> p t b", b=NB), ACT.Sqrt,
                                   scale=1.0 if n == 0 else 128.0,
                                   bias=EPSC[:, 0:1] if n == 0 else EPSC[:, 1:2]).then_inc(l2_rt, 1)
                elif what == "dfqk":
                    m, part = n[0] - 1, n[1]
                    if m < 0:
                        continue
                    if part == 0:
                        tile = (DQ if m % 2 == 0 else DK)[:, m // 2, :]
                        act.wait_ge(gemm_freed, G_DFQK + m + 1)
                        if m >= 1:
                            act.wait_ge(qn_mm, m)
                        else:
                            act.wait_ge(x_spilled, 16 * KC)
                        act.activation(SQD[:, :], tile, ACT.Square).then_inc(qn_sq, 1)
                    elif part == 2:
                        act.wait_ge(qn_mm, m + 1)
                        if m >= 1:
                            act.wait_ge(qn_made, m)
                        act.activation(QNR[:, :], bank_of(G_DFQK + m)[:, :], ACT.Sqrt,
                                       scale=1.0 if m % 2 == 0 else 1.0 / HD,
                                       bias=EPSC[:, 2:3] if m % 2 == 0 else EPSC[:, 0:1]).then_inc(qn_rt, 1)
                elif what == "decay":
                    act.wait_ge(d_made, n + 1)
                    act.activation(AQK[:, n, :, :], AQK[:, n, :, :], ACT.Exp).then_inc(d_exp, 1)
                    if n == NB - 1:
                        act.activation(EG[:, :, :], EG[:, :, :], ACT.Exp).then_inc(eg_made, 1)
                elif what == "X":
                    b, l = n
                    act.wait_ge(xt_mm, step(b, l) + 1)
                    act.activation(XT[:, b % 2, :, :], heads(PS[3 + 2 * (b % 2)][:, :]), ACT.Copy)\
                       .then_inc(xt_made, 1)
                elif what == "W":
                    act.wait_ge(u_mm, n + 1)
                    act.activation(VT[:, :, P * n:P * (n + 1)], heads(PS[2 + 2 * (n % 2)][:, :]), ACT.Copy)\
                       .then_inc(uw_made, 1)
                    act.wait_ge(w_mm, n + 1)
                    act.activation(KT[:, :, P * n:P * (n + 1)], heads(PS[3 + 2 * (n % 2)][:, :]), ACT.Copy)\
                       .then_inc(uw_made, 1)
                elif what == "sb" and n % 2 == 1:
                    act.wait_ge(ot_mm, n + 1)
                    act.activation(QT[:, :, CH * (n - 1):CH * (n + 1)], heads(PS[2][:, :]), ACT.Copy)\
                       .then_inc(od_made, 1)
                elif what == "A":
                    h, i = n // NB, n % NB
                    w = P * (i + 1)
                    for c in range(2):
                        act.wait_ge(dmax, 2 * n + c + 1)
                        if c == 0 and n >= 3:
                            act.wait_ge(dpt_mm, n - 2)
                        if c == 1 and n >= 1:
                            act.wait_ge(dw_made, n)
                        act.activation(P0[:, n % 3, 0:w] if c == 0 else PB[:, 0:w], PS[c][:, 0:w], ACT.Exp,
                                       scale=-1.0, bias=MX[:, h % 2, 2 * i + c:2 * i + c + 1],
                                       accum_out=SU[:, h % 2, 2 * i + c:2 * i + c + 1]).then_inc(dexp, 1)
                elif what == "B":
                    h, i = n // NB, n % NB
                    if i == 0 and h:
                        act.wait_ge(dpv_mm, h)
                    act.wait_ge(dpt_mm, n + 1)
                    act.activation(PT2[:, 0:i + 1, P * i:P * (i + 1)],
                                   PS[6][:, 0:P * (i + 1)].rearrange("p (j c) -> p j c", c=P),
                                   ACT.Copy).then_inc(dpt_freed, 1)
                elif what == "C":
                    act.wait_ge(dpv_mm, n + 1)
                    act.activation(DQ[:, n, :], PS[7][:, :], ACT.Copy).then_inc(dpv_freed, 1)
                elif what == "zs":
                    for t in range(4 * n, 4 * n + 4):
                        act.wait_ge(gemm_freed, G_Z + t + 1)
                        act.activation(ZT[:, t, :], ZT[:, t, :], ACT.Silu).then_inc(silu_z, 1)
                elif what == "os":
                    if n < 4:
                        act.wait_ge(dpv_freed, 4)
                        act.wait_ge(uw_made, 8)
                    else:
                        act.wait_ge(od_made, 4)
                    if n >= 2:
                        act.wait_ge(o_mm, n - 1)
                    act.activation(SQO[:, n % 2, :], out_tile(n), ACT.Square).then_inc(o_sq, 1)
                elif what == "or":
                    tiles = slice(4 * n, 4 * n + 4)
                    act.wait_ge(o_mm, tiles.stop)
                    act.activation(OC[:, tiles, :], PS[5][:, NB * tiles.start:NB * tiles.stop]
                                   .rearrange("p (t b) -> p t b", b=NB), ACT.Sqrt,
                                   scale=1.0 / P, bias=EPSC[:, 0:1]).then_inc(o_rt, 1)
                elif what == "oh":
                    act.wait_ge(o_made, n + 1)
                    if n < 4:
                        act.wait_ge(dpv_mm, 4)
                        act.wait_ge(dw_made, 16)
                        act.activation(FH[:, n, :], out_tile(n), ACT.Copy).then_inc(fh_made, 1)
                    else:
                        act.wait_ge(unit_done, U_WO2)
                        high(out_tile(n), n)
                    act.dma_start(XR[:, n, :], out_t[P * n:P * (n + 1), :]).then_inc(x_back[n], 16)

        @block.vector
        def _(dve):
            chain = [0]

            def then(ins):
                chain[0] += 1
                ins.then_inc(v_chain, 1)
                dve.wait_ge(v_chain, chain[0])

            for c, v in enumerate((EPS, 128 * EPS, 64 * EPS, 1.0)):
                dve.memset(EPSC[:, c:c + 1], v).then_inc(eps_made, 1)
            dve.wait_ge(par_landed, 16)
            dve.wait_ge(con_landed, 16)

            def low(src, k, n, gain=None):
                dve.wait_ge(gh_made, KC * n + k + 1)
                if gain is None:
                    dve.tensor_tensor(GL[:, k, :], src, GH[:, k, :].bitcast(F32), ALU.subtract).then_inc(gl_made, 1)
                else:
                    dve.scalar_tensor_tensor(GL[:, k, :], src, gain, GH[:, k, :].bitcast(F32),
                                             ALU.mult, ALU.subtract).then_inc(gl_made, 1)

            def add_square(n, k):
                dve.wait_ge(sq_made, KC * n + k + 1)
                if k == 0:
                    if n:
                        dve.wait_ge(ss_made, n)
                    dve.tensor_copy(ACC, SQ[:, 0, :]).then_inc(sq_added, 1)
                else:
                    dve.wait_ge(sq_added, KC * n + k)
                    dve.tensor_tensor(ACC, ACC, SQ[:, 0, :], ALU.add).then_inc(sq_added, 1)

            def invert_rms(n):
                dve.wait_ge(rms_made, n + 1)
                dve.reciprocal(RCOL, RCOL).then_inc(rcol_made, 1)
                dve.wait_ge(rb_ready, n + 1)

            def evacuate(g, unit, out, rows=P):
                dve.wait_ge(unit_done, unit + 1)
                dve.tensor_tensor(out, bank_of(g)[0:rows, :], RB[0:rows, :], ALU.mult).then_inc(gemm_freed, 1)
                dve.wait_ge(gemm_freed, g + 1)

            for k in range(KC):
                if k == 1:
                    dve.wait_ge(hi_made, 1)
                    dve.tensor_tensor(LO[:, 0, :], RAW[:, 0, :], HI[:, 0, :].bitcast(F32), ALU.subtract)\
                       .then_inc(unit_split, 1)
                low(X[:, k, :], k, 0, par(C_GMIX + k))
                add_square(0, k)
            dve.wait_ge(rms_made, 1)
            dve.reciprocal(RCOL, RCOL).then_inc(rcol_made, 1)
            dve.wait_ge(masks_landed, 16)
            dve.wait_ge(sg_landed, 48)
            dve.memset(SGW[64:128, :, 0:64], 0.0).then_inc(sgw_masked, 1)

            def over_group(col):
                return col.unsqueeze(2).to_broadcast([P, 8, HD])

            def layer_norm(stage, b):
                groups = VA[:, b, :].rearrange("p (h d) -> p h d", d=HD)
                mean, deviation = LNS[:, 8 * b:8 * b + 8], LNV[:, 8 * b:8 * b + 8]
                if stage == 0:
                    dve.wait_ge(va_freed, b + 1)
                    then(dve.tensor_reduce(mean, groups, AX_X, ALU.add))
                    then(dve.tensor_scalar(mean, mean, 1.0 / HD, None, ALU.mult))
                    dve.tensor_tensor(groups, groups, over_group(mean), ALU.subtract).then_inc(ln_centered, 1)
                elif stage == 1:
                    dve.wait_ge(ln_squared, b + 1)
                    dve.tensor_reduce(deviation, SQV[:, b, :].rearrange("p (h d) -> p h d", d=HD), AX_X, ALU.add)\
                       .then_inc(ln_summed, 1)
                else:
                    dve.wait_ge(ln_root, 1)
                    then(dve.reciprocal(deviation, deviation))
                    dve.wait_ge(ln_centered, b + 1)
                    dve.tensor_tensor(groups, groups, over_group(deviation), ALU.mult).then_inc(vn_ready, 1)

            dve.wait_ge(rb_ready, 1)
            evacuate(G_F, U_F, FR[0:8, 0, :], 8)
            dve.tensor_scalar(FR[0:8, 0, :], FR[0:8, 0, :], par(C_FB, 1, 0, 8), None, ALU.add).then_inc(f_made, 1)
            dve.wait_ge(f_log, 3)
            then(dve.tensor_scalar(FR[0:8, 0, :], FR[0:8, 0, :], -1.0, 0.0, ALU.mult, ALU.max))
            dve.tensor_tensor_scan(FR[0:8, 2, :], FR[0:8, 0, :], FR[0:8, 1, :], 0.0, ALU.add, ALU.add)\
               .then_inc(negc_ready, 1)
            dve.wait_ge(negc_ready, 1)
            dve.wait_ge(negc_high, 1)
            dve.wait_ge(idr_made, 1)
            dve.tensor_tensor(FRP[0:8, 1, :], FR[0:8, 2, :], FRP[0:8, 0, :].bitcast(F32), ALU.subtract)\
               .then_inc(negc_split, 1)

            def biased_max(h, i):
                s = NB * h + i
                S = PS[2 + s % 2]
                e = h % 2
                dve.wait_ge(s_made, s + 1)
                first = 3e38
                if i:
                    then(dve.tensor_tensor_reduce(S[:, 0:P * i], S[:, 0:P * i], NCB[:, e, 0:P * i], -1.0, 3e38,
                                                  ALU.add, ALU.min, MXA[:, 4 * e + i:4 * e + i + 1]))
                    first = MXA[:, 4 * e + i:4 * e + i + 1]
                dve.tensor_tensor_reduce(S[:, P * i:P * (i + 1)], S[:, P * i:P * (i + 1)],
                                         NCD[:, e, P * i:P * (i + 1)], -1.0, first,
                                         ALU.add, ALU.min, MX[:, e, i:i + 1]).then_inc(max_made, 1)

            def normalise(h, i):
                e = h % 2
                p = P1[:, e, PCOL[i]:PCOL[i] + P * (i + 1)]
                dve.wait_ge(exp_made, NB * h + i + 1)
                then(dve.reciprocal(RC[:, e, i:i + 1], SU[:, e, i:i + 1]))
                dve.tensor_scalar(p, p, RC[:, e, i:i + 1], None, ALU.mult).then_inc(p_ready, 1)

            for what, n in MIX1_ORDER:
                if what in ("qk", "u") and n[1] == 3:
                    n = n[0]
                    unit, g = U_QK + turn_of(what, n), G_QK + turn_of(what, n)
                    if what == "qk" and n % 2 == 0:
                        dve.wait_ge(unit_done, unit + 1)
                        dve.scalar_tensor_tensor(MT[:, 4 + n // 2, :], bank_of(g)[:, :], HD ** -0.5, RB[:, :],
                                                 ALU.mult, ALU.mult).then_inc(gemm_freed, 1)
                        dve.wait_ge(gemm_freed, g + 1)
                    else:
                        evacuate(g, unit, KT1[:, n // 2, :] if what == "qk" else MT[:, n, :])
                elif what == "K":
                    dve.wait_ge(ncb_made, n + 1)
                    then(dve.tensor_tensor(heads(NCD[:, n % 2, :]), heads(NCB[:, n % 2, :]),
                                           CAUSAL[:, 384:512].unsqueeze(1).to_broadcast([P, 4, P]), ALU.add))
                elif what == "A":
                    biased_max(n // NB, n % NB)
                elif what == "ln":
                    layer_norm(*n)
                elif what == "N":
                    normalise(n // NB, n % NB)
                elif what == "C" and n % 2 == 1:
                    dve.wait_ge(pv_made, n + 1)
                    dve.tensor_copy(MT[:, 4 + n // 2, :], PS[6][:, :]).then_inc(attended, 1)
                elif what == "gate":
                    dve.wait_ge(gate_mm, n + 1)
                    dve.wait_ge(gelu_made, n + 1)
                    then(dve.scalar_tensor_tensor(heads(SQV[:, n, :]), heads(PS[n % 2][:, :]), par(C_SGG + n),
                                                  SGB[:, n, :].unsqueeze(1).to_broadcast([P, 4, P]),
                                                  ALU.mult, ALU.add))
                    dve.tensor_tensor(MT[:, n, :], MT[:, n, :], SQV[:, n, :], ALU.mult).then_inc(gated, 1)
                elif what == "split":
                    dve.wait_ge(mh_made, n + 1)
                    dve.tensor_tensor(ML[:, n, :], MT[:, n, :], MH[:, n, :].bitcast(F32), ALU.subtract)\
                       .then_inc(ml_made, 1)
            for m in range(KC):
                dve.wait_ge(unit_done, U_WO + m + 1)
                dve.tensor_tensor(X[:, m, :], X[:, m, :], wo_bank(m)[:, :], ALU.add).then_inc(gemm_freed, 1)
                dve.wait_ge(gemm_freed, G_WO + m + 1)
                low(X[:, m, :], m, 1, par(C_GFFN + m))
                add_square(1, m)
            invert_rms(1)
            then(dve.memset(AB[:, :, 0:2], 0.0))
            c0 = chain[0]
            with dve.Fori(0, NFF) as t:
                for gv in range(2):
                    dve.wait_ge(unit_done, 2 * t + (U_UP + gv + 1))
                    dve.tensor_tensor(AB[:, gv, 2:T + 2], bank_of(G_UP + gv)[:, :], RB[:, :], ALU.mult)\
                       .then_inc(gemm_freed, 1)
                for gv in range(2):
                    dve.wait_ge(gemm_freed, 2 * t + (G_UP + gv + 1))
                    dve.wait_ge(conv_started, 2 * t + (gv + 1))
                    dve.scalar_tensor_tensor(YC[:, gv, :], AB[:, gv, 1:T + 1],
                                             PAR[:, bass.ds(6 * t + (C_FCW + 3 * gv + 1), 1)], YC[:, gv, :],
                                             ALU.mult, ALU.add).then_inc(v_chain, 1)
                    dve.wait_ge(v_chain, 2 * t + (c0 + gv + 1))
                    dve.scalar_tensor_tensor(YC[:, gv, :], AB[:, gv, 0:T],
                                             PAR[:, bass.ds(6 * t + (C_FCW + 3 * gv), 1)], YC[:, gv, :],
                                             ALU.mult, ALU.add).then_inc(conv_made, 1)
                dve.wait_ge(silu_ff, t + 1)
                dve.wait_ge(conv_made, 2 * t + 2)
                dve.tensor_tensor(YC[:, 0, :], YC[:, 0, :], YC[:, 1, :], ALU.mult).then_inc(ff_made, 1)
                dve.wait_ge(ff_made, t + 1)
                dve.wait_ge(ah_made, t + 1)
                dve.tensor_tensor(AL[:, bass.ds(t, 1), :], YC[:, 0:1, :], AH[:, bass.ds(t, 1), :].bitcast(F32),
                                  ALU.subtract).then_inc(al_made, 1)
            chain[0] += 2 * NFF
            dve.tensor_tensor(GG, par(C_GFIN, KC), par(C_GN2, KC), ALU.mult).then_inc(gg_made, 1)
            dve.wait_ge(gg_made, 1)

            for m in range(KC):
                if m in (3, 7):
                    dve.wait_ge(unit_done, U_DN + 11 * (m + 1) // 4)
                else:
                    dve.wait_ge(down_done, m + 1 - m // 4)
                dve.tensor_tensor(X[:, m, :], X[:, m, :], bank_of(G_DN + m)[:, :], ALU.add).then_inc(gemm_freed, 1)
                dve.wait_ge(gemm_freed, G_DN + m + 1)
                low(X[:, m, :], m, 2, GG[:, m:m + 1])
                add_square(2, m)
                dve.wait_ge(sqb_made, m + 1)
                if m == 0:
                    dve.tensor_copy(ACCB, SQB).then_inc(sqb_added, 1)
                else:
                    dve.wait_ge(sqb_added, m)
                    dve.tensor_tensor(ACCB, ACCB, SQB, ALU.add).then_inc(sqb_added, 1)
            dve.wait_ge(r1_root, 1)
            dve.reciprocal(R1C, R1C).then_inc(r1_made, 1)
            dve.wait_ge(r1_made, 1)
            then(dve.tensor_tensor(SS2C, PS[7][:, NB:2 * NB], R1C, ALU.mult))
            dve.tensor_tensor(SS2C, SS2C, R1C, ALU.mult).then_inc(ms_made, 1)
            dve.wait_ge(rms_made, 3)
            then(dve.reciprocal(RCOL, RCOL))
            dve.tensor_tensor(RCOL, RCOL, R1C, ALU.mult).then_inc(rcol_made, 1)
            dve.wait_ge(rb_ready, 3)

            def rows(stage):
                if stage == 0:
                    dve.tensor_scalar(R1[0:4, :], BR[0:4, :], par(C_DTB, 1, 0, 4), None, ALU.add).then_inc(ba_v, 1)
                    dve.memset(RS[:, :], 0.0).then_inc(ba_v, 1)
                else:
                    dve.wait_ge(ba_a, 4)
                    dve.wait_ge(ba_v, 2)
                    then(dve.tensor_scalar(R1[0:4, :], R1[0:4, :], 0.0, None, ALU.max))
                    then(dve.tensor_tensor(R1[0:4, :], R1[0:4, :], R2[0:4, :], ALU.add))
                    then(dve.tensor_scalar(R1[0:4, :], R1[0:4, :], EA[0:4, :], -1.0, ALU.mult, ALU.mult))
                    for c in range(T // CH):
                        last = dve.tensor_tensor_scan(RS[0:4, CH * c:CH * (c + 1)], ONES[0:4, 0:CH],
                                                      R1[0:4, CH * c:CH * (c + 1)], 0.0, ALU.mult, ALU.add)
                    last.then_inc(ba_v, 1)
                    dve.wait_ge(ba_v, 3)
                    rows_by_chunk = RS[0:4, :].rearrange("p (c n) -> p c n", n=CH)
                    dve.tensor_tensor(R1[0:4, :].rearrange("p (c n) -> p c n", n=CH),
                                      rows_by_chunk[:, :, CH - 1:CH].to_broadcast([4, T // CH, CH]),
                                      rows_by_chunk, ALU.subtract).then_inc(ba_v, 1)

            def tile_of(t):
                return (KT, QT, VT)[t // 4][:, t % 4, :]

            def over_head(col):
                return col.unsqueeze(2).to_broadcast([P, 4, P])

            def block_decays(b):
                dve.wait_ge(gcb_made, 4)
                dve.wait_ge(cols_made, 1)
                then(dve.tensor_tensor(AQK[:, b, :, :], EG[:, :, P * b:P * (b + 1)], over_head(COLS[:, b, 0, :]),
                                       ALU.subtract))
                dve.tensor_tensor(AQK[:, b, :, :], AQK[:, b, :, :], GNEG.unsqueeze(1).to_broadcast([P, 4, P]),
                                  ALU.add).then_inc(d_made, 1)

            def block_products(b):
                s = b % 2
                A, B = (heads(PS[n + 2 * s][:, :]) for n in (2, 3))
                dve.wait_ge(d_exp, b + 1)
                dve.wait_ge(aq_mm, b + 1)
                dve.tensor_tensor(NT[:, s, :, :], A, AQK[:, b, :, :], ALU.mult)
                dve.tensor_tensor(AQK[:, b, :, :], B, AQK[:, b, :, :], ALU.mult).then_inc(nt_made, 1)

            def block_inputs(b):
                s = b % 2
                A, B = (heads(PS[n + 2 * s][:, :]) for n in (2, 3))
                cols = slice(P * b, P * (b + 1))
                dve.wait_ge(tk_mm, b + 1)
                dve.tensor_tensor(KBE[:, s, :, :], A, over_head(COLS[:, b, 2, :]), ALU.mult)
                dve.tensor_tensor(KDEC[:, b, :, :], A, over_head(COLS[:, b, 3, :]), ALU.mult).then_inc(kd_made, 1)
                dve.wait_ge(tv_mm, b + 1)
                dve.tensor_tensor(VBT[:, s, :, :], B, over_head(COLS[:, b, 1, :]), ALU.mult).then_inc(vbt_made, 1)
                dve.wait_ge(eg_made, 1)
                dve.tensor_tensor(QT[:, :, cols], QT[:, :, cols], EG[:, :, cols], ALU.mult).then_inc(qe_made, 1)

            def masked_y(b, l):
                A = PS[2 + 2 * (b % 2)]
                dve.wait_ge(y_mm, step(b, l) + 1)
                for h in range(4):
                    last = dve.scalar_tensor_tensor(YM[:, b % 2, h, :], A[:, P * h:P * (h + 1)],
                                                    COLS[:, b, 1, h:h + 1], level_mask(l), ALU.mult, ALU.mult)
                last.then_inc(ym_made, 1)
                if l == 0:
                    dve.wait_ge(ym_made, step(b, l) + 1)
                    dve.tensor_tensor(XI[:, b % 2, :, :], IDENT.unsqueeze(1).to_broadcast([P, 4, P]),
                                      YM[:, b % 2, :, :], ALU.subtract).then_inc(xi_made, 1)

            def next_inverse(b, l):
                dve.wait_ge(z_mm, (b // 2) * 2 * (LEVELS - 1) + 2 * (l - 1) + b % 2 + 1)
                dve.wait_ge(xi_made, step(b, l - 1) + 1)
                dve.tensor_tensor(XI[:, b % 2, :, :], XI[:, b % 2, :, :], heads(PS[3 + 2 * (b % 2)][:, :]),
                                  ALU.subtract).then_inc(xi_made, 1)

            def normalise_qk(m):
                tile = (DQ if m % 2 == 0 else DK)[:, m // 2, :]
                dve.wait_ge(qn_rc, 2 * m + 2)
                dve.scalar_tensor_tensor(tile, tile, par(C_QG if m % 2 == 0 else C_KG), QNR[:, :],
                                         ALU.mult, ALU.mult).then_inc(qn_made, 1)

            def masked_max(n, c):
                h, i = n // NB, n % NB
                w = P * (i + 1)
                dve.wait_ge(ds_mm, 2 * n + c + 1)
                dve.tensor_tensor_reduce(PS[c][:, 0:w], PS[c][:, 0:w], CAUSAL[:, 512 - w:512], -1.0, 3e38,
                                         ALU.add, ALU.min, MX[:, h % 2, 2 * i + c:2 * i + c + 1]).then_inc(dmax, 1)

            def difference(n):
                h, i = n // NB, n % NB
                w = P * (i + 1)
                rc = RC[:, h % 2, 2 * i:2 * i + 2]
                dve.wait_ge(dexp, 2 * n + 2)
                then(dve.reciprocal(rc, SU[:, h % 2, 2 * i:2 * i + 2]))
                p = P0[:, n % 3, 0:w]
                dve.tensor_scalar(p, p, rc[:, 0:1], None, ALU.mult)
                then(dve.tensor_scalar(S1[:, 0:1], rc[:, 1:2], NEGLAM, None, ALU.mult))
                dve.scalar_tensor_tensor(p, PB[:, 0:w], S1[:, 0:1], p, ALU.mult, ALU.add).then_inc(dw_made, 1)

            for what, n in MIX2_ORDER:
                if what == "lam":
                    dve.wait_ge(g_high, 1)
                    dve.tensor_tensor(RSP[0:4, 1, :], RS[0:4, :], RSP[0:4, 0, :].bitcast(F32), ALU.subtract)\
                       .then_inc(g_split, 1)
                    dve.wait_ge(lam_exp, 1)
                    dve.scalar_tensor_tensor(NEGLAM, LE[:, 1:2], -LAMBDA_INIT, LE[:, 0:1],
                                             ALU.add, ALU.subtract).then_inc(lam_made, 1)
                    dve.tensor_scalar(par(C_DFG), par(C_DFG), 1.0 - LAMBDA_INIT, None, ALU.mult)\
                       .then_inc(lam_made, 1)
                    dve.wait_ge(lam_made, 2)
                elif what == "ba":
                    dve.tensor_tensor(LP[0:64, :], par(C_LAM, 2, 0, 64), par(C_LAM + 2, 2, 0, 64), ALU.mult)\
                       .then_inc(lam_prod, 1)
                    evacuate(G_BA, U_BA, BR[0:36, :], 36)
                    then(dve.memset(CB[:, :, 0:3], 0.0))
                elif what == "rows":
                    rows(n)
                elif what == "kqv":
                    evacuate(G_KQV + n, U_KQV + n, CB[:, n % 2, 3:T + 3])
                    dve.wait_ge(cv_a, n + 1)
                    for j in (2, 1, 0):
                        tap = dve.scalar_tensor_tensor(tile_of(n), CB[:, n % 2, j:T + j], par(C_DCW + 4 * n + j),
                                                       tile_of(n), ALU.mult, ALU.add)
                        if j:
                            then(tap)
                    tap.then_inc(cv_v, 1)
                elif what == "x2":
                    dve.wait_ge(r1_mm, 1)
                    for k in (2 * n, 2 * n + 1):
                        dve.scalar_tensor_tensor(X[:, k, :], X[:, k, :], par(C_GFIN + k), PS[6][:, :],
                                                 ALU.mult, ALU.mult).then_inc(x_updated, 1)
                elif what == "cols":
                    dve.wait_ge(cols_mm, 1)
                    dve.memset(ST[:, :, :], 0.0).then_inc(st_made, 1)
                    then(dve.tensor_copy(COLS, PS[4][:, :].rearrange("p (b q r) -> p b q r", b=NB, q=4)[:, :, :, 0:4]))
                    then(dve.tensor_scalar(COLS[:, :, 1, :], COLS[:, :, 1, :], 1.0, None, ALU.add))
                    then(dve.reciprocal(COLS[:, :, 1, :], COLS[:, :, 1, :]))
                    dve.tensor_tensor(COLS[:, :, 2, :], COLS[:, :, 2, :], COLS[:, :, 1, :], ALU.mult)\
                       .then_inc(cols_made, 1)
                elif what == "l2r":
                    dve.wait_ge(l2_rt, n + 1)
                    dve.reciprocal(L2C[:, 4 * n:4 * n + 4, :], L2C[:, 4 * n:4 * n + 4, :]).then_inc(l2_rc, 1)
                elif what == "l2b":
                    dve.wait_ge(l2_bc, n + 1)
                    dve.tensor_tensor(tile_of(n), tile_of(n), PS[2 + n % 2][:, :], ALU.mult).then_inc(l2_made, 1)
                elif what == "dfqk":
                    n, part = n
                    if n >= 1 and part >= 2:
                        half = slice(256 * (part - 2), 256 * (part - 1))
                        dve.wait_ge(qn_rt, n)
                        dve.reciprocal(QNR[:, half], QNR[:, half]).then_inc(qn_rc, 1)
                    if n >= 1 and part == 3:
                        normalise_qk(n - 1)
                    if n < 8 and part == 3:
                        evacuate(G_DFQK + n, U_DFQK + n, (DQ if n % 2 == 0 else DK)[:, n // 2, :])
                elif what == "decay":
                    block_decays(n)
                elif what == "T1":
                    block_products(n)
                elif what == "T2":
                    block_inputs(n)
                elif what == "Y":
                    masked_y(*n)
                elif what == "Z":
                    next_inverse(*n)
                elif what == "sa":
                    b, r = n // 2, 64 * (n % 2)
                    dve.wait_ge(uw_made, 2 * (b + 1))
                    dve.wait_ge(ws_mm, n + 1)
                    new = VT[r:r + 64, :, P * b:P * (b + 1)]
                    dve.tensor_tensor(new, new, heads(PS[6][r:r + 64, :]), ALU.subtract).then_inc(vn_made, 1)
                elif what == "sb":
                    dve.wait_ge(kv_mm, n + 1)
                    dve.wait_ge(st_made, n + 1)
                    dve.wait_ge(eg_made, 1)
                    for h in range(4):
                        last = dve.scalar_tensor_tensor(ST[:, h, :], ST[:, h, :],
                                                        EG[:, h, CH * (n + 1) - 1:CH * (n + 1)],
                                                        PS[7][:, P * h:P * (h + 1)], ALU.mult, ALU.add)
                    last.then_inc(st_made, 1)
                elif what == "A":
                    masked_max(n, 0)
                    masked_max(n, 1)
                elif what == "D":
                    difference(n)
                elif what == "z" and n[1] == 3:
                    n = n[0]
                    if n == 0:
                        dve.wait_ge(uw_made, 8)
                    evacuate(G_Z + n, U_Z + n, ZT[:, n, :])
                elif what == "or":
                    tiles = slice(4 * n, 4 * n + 4)
                    dve.wait_ge(o_rt, n + 1)
                    dve.reciprocal(OC[:, tiles, :], OC[:, tiles, :]).then_inc(o_rc, 1)
                elif what == "og":
                    o = out_tile(n)
                    dve.wait_ge(silu_z, n + 1)
                    dve.wait_ge(o_sq, n + 1)
                    then(dve.scalar_tensor_tensor(o, o, par(C_DFG if n < 4 else C_DNG), ZT[:, n, :],
                                                  ALU.mult, ALU.mult))
                    dve.wait_ge(o_bc, n + 1)
                    dve.tensor_tensor(o, o, PS[3 + n % 2][:, :], ALU.mult).then_inc(o_made, 1)
                elif what == "ol":
                    dve.wait_ge(o_made, n + 1)
                    if n < 4:
                        dve.wait_ge(fh_made, n + 1)
                        dve.tensor_tensor(FL[:, n, :], out_tile(n), FH[:, n, :].bitcast(F32), ALU.subtract)\
                           .then_inc(fl_made, 1)
                    else:
                        dve.wait_ge(gh_made, 3 * KC + n - 3)
                        dve.tensor_tensor(GL[:, n, :], out_tile(n), GH[:, n, :].bitcast(F32), ALU.subtract)\
                           .then_inc(gl_made, 1)
            for m in range(KC):
                dve.wait_ge(x_back[m], 16)
                dve.wait_ge(unit_done, U_WO2 + m + 1)
                dve.tensor_tensor(XR[:, m, :], XR[:, m, :], out_bank(m)[:, :], ALU.add).then_inc(gemm_freed, 1)


def _constants():
    con = np.zeros((P, NCON), np.float32)
    i = np.arange(P)
    con[:, K_ID:K_ID + P] = i[:, None] == i[None, :]
    con[:, K_ONE:K_ONE + P] = 1.0
    con[:, K_HALF:K_HALF + P] = i[:, None] // HD == i[None, :] // HD
    con[:, K_CAUSAL + 384:K_CAUSAL + 512] = np.where(i[None, :] <= i[:, None], 0.0, NEG)
    same = i[:, None] // CH == i[None, :] // CH
    con[:, K_GNEG:K_GNEG + P] = np.where(same & (i[:, None] <= i[None, :]), 0.0, NEG)
    for l in range(LEVELS):
        pair = i[:, None] >> (l + 1) == i[None, :] >> (l + 1)
        con[:, K_LV + P * l:K_LV + P * (l + 1)] = pair & ((i[:, None] >> l & 1) == 1) & ((i[None, :] >> l & 1) == 0)
    return con


def _tiles(w):
    k, n = w.shape
    return w.reshape(k // P, P, n // P, P).transpose(2, 1, 0, 3).reshape(n // P, P, 1024)


def _moving(w):
    return w.reshape(4, 2, P, 512).transpose(0, 2, 1, 3).reshape(4, P, 1024)


def _padded(parts):
    out = np.zeros((D, P), np.float32)
    for at, w in parts:
        out[:, at:at + w.shape[1]] = w
    return _tiles(out)


def _stream(i):
    w_in, w_in2 = i["w_in"][0], i["w_in_2"][0]
    u, va, q, k, vb = (w_in[:, 512 * n:512 * (n + 1)] for n in range(5))
    dq, dk, dv, dz = (w_in2[:, 512 * n:512 * (n + 1)] for n in range(4))
    fq, fk, fv, fz = (w_in2[:, 2056 + 512 * n:2056 + 512 * (n + 1)] for n in range(4))
    qk = np.stack([_tiles(q), _tiles(k)], 1).reshape(8, P, 1024)
    tiles = {"qk": qk, "u": _tiles(u)}
    fqk = np.stack([_tiles(fq), _tiles(fk)], 1).reshape(8, P, 1024)
    up = i["w_up"][0]
    up = np.stack([_tiles(up[:, :FF]), _tiles(up[:, FF:])], 1).reshape(2 * NFF, P, 1024)
    down = i["w_down"][0].reshape(NFF, P, KC, P).transpose(2, 0, 1, 3)
    down = down.reshape(NFF, 8, P, P).transpose(0, 2, 1, 3).reshape(NFF, P, 1024)
    units = [_moving(vb), _moving(va), _padded([(0, w_in[:, 2560:2568])]),
             np.stack([tiles[what][n] for what, n in MIX1_UNITS]), _tiles(i["w_out"][0]),
             up, down, _padded([(0, w_in2[:, 2052:2056]), (32, w_in2[:, 2048:2052])]),
             _tiles(dk), _tiles(dq), _tiles(dv), _moving(fv), fqk, _tiles(fz), _tiles(dz),
             _tiles(np.roll(i["w_out_2"][0], -512, 0))]
    s = np.concatenate(units)
    assert s.shape[0] == UNITS
    return np.ascontiguousarray(s.reshape(UNITS // 2, 2, P, 1024).transpose(0, 2, 1, 3).reshape(UNITS // 2, P, 2048))


def _parameters(i):
    p = np.zeros((P, NPAR), np.float32)

    def columns(at, v):
        v = v.reshape(-1, P).T
        p[:, at:at + v.shape[1]] = v

    columns(C_GMIX, i["norm_mix_g"])
    columns(C_GFFN, i["norm_ffn_g"])
    columns(C_GFIN, i["norm_final_g"])
    columns(C_GN2, i["norm_gain_2"])
    columns(C_SGG, i["sg_ln_g"])
    taps = i["w_conv"][0].reshape(3, 2, NFF, P).transpose(3, 2, 1, 0)
    p[:, C_FCW:C_FCW + 6 * NFF] = taps.reshape(P, -1)
    p[:, C_FCB:C_FCB + 2 * NFF] = i["b_conv"][0].reshape(2, NFF, P).transpose(2, 1, 0).reshape(P, -1)
    taps = i["conv_w_2"][0].reshape(4, 3, 4, P)[:, [1, 0, 2]]
    p[:, C_DCW:C_DCW + 48] = taps.transpose(3, 1, 2, 0).reshape(P, -1)
    p[0:8, C_FB] = i["f_bias"][0]
    p[0:4, C_ALOG] = i["a_log_2"][0]
    p[0:4, C_DTB] = i["dt_bias_2"][0]
    p[:, C_DNG] = i["dn_out_gain_2"][0]
    for c, name in ((C_QG, "q_gain_2"), (C_KG, "k_gain_2")):
        p[0:64, c] = p[64:128, c] = i[name][0]
    p[:, C_DFG] = i["df_out_gain_2"][0]
    for n, name in enumerate(("lambda_q1_2", "lambda_q2_2", "lambda_k1_2", "lambda_k2_2")):
        p[0:64, C_LAM + n] = i[name][0]
    return p


def kernel(**inputs):
    import concourse.bacc as bacc
    from concourse.bass_utils import run_bass_kernel_spmd

    i = {name: np.asarray(v) for name, v in inputs.items()}
    arrays = {
        "x_t": np.ascontiguousarray(i["x"][0].T),
        "wstream": _stream(i),
        "params": _parameters(i),
        "consts": _constants(),
        "sgw_t": np.ascontiguousarray(i["sg_w"][0].transpose(2, 0, 1)),
        "sgb": np.ascontiguousarray(i["sg_b"][0].reshape(4, 2, P)),
    }
    nc = bacc.Bacc("TRN2", target_bir_lowering=False, num_devices=1)
    args = [nc.dram_tensor(name, a.shape, F32, kind="ExternalInput").ap() for name, a in arrays.items()]
    args.append(nc.dram_tensor("out_t", (D, T), F32, kind="ExternalOutput").ap())
    build(nc, *args)
    r = run_bass_kernel_spmd(nc, [arrays], core_ids=[0])
    return np.ascontiguousarray(r.results[0]["out_t"].T)[None]
```
